# Optimizing a Trainium2 kernel written in Bass

```python
import math
import jax, jax.numpy as jnp
from jax import lax
import numpy as np

D_MODEL = 1024
BATCH = 1
SEQ = 1024
DEPTH = 1
DEC_BATCH = 8
DEC_SEQ = 8
PAST_LEN = 8192
PAGE_SIZE = 128

D_MIX = D_MODEL
RG_WIDTH = D_MIX // 2
RG_HEADS = 8
RG_HEAD_DIM = RG_WIDTH // RG_HEADS
CONV_WIDTH = 4
RG_C = 8.0
GLA_WIDTH = D_MIX - RG_WIDTH
GLA_HEADS = 4
GLA_DV = GLA_WIDTH // GLA_HEADS
GLA_DK = GLA_DV // 2
GLA_KEY_WIDTH = GLA_HEADS * GLA_DK
GLA_GATE_RANK = 16
GLA_GATE_NORMALIZER = 16.0
GLA_CHUNK = 32
D_FF = 2816
N_MEM = 256
XA_HEADS = 4
XA_HEAD_DIM = D_MODEL // XA_HEADS
EPS = 1e-6

OFF_RG_X = 0
OFF_RG_Y = OFF_RG_X + RG_WIDTH
OFF_Q = OFF_RG_Y + RG_WIDTH
OFF_K = OFF_Q + GLA_KEY_WIDTH
OFF_V = OFF_K + GLA_KEY_WIDTH
OFF_G = OFF_V + GLA_WIDTH
OFF_A = OFF_G + GLA_WIDTH
D_IN = OFF_A + GLA_GATE_RANK

kernel_name = "hymba_rglru_gla_macaron_memxattn_step"

def rmsnorm(x, g):
    xf = x.astype(jnp.float32)
    xf = xf * lax.rsqrt(jnp.mean(xf * xf, axis=-1, keepdims=True) + EPS)
    return xf.astype(x.dtype) * g

def swiglu_ffn(x, g, w_gate, w_up, w_down):
    h = rmsnorm(x, g)
    return (jax.nn.silu(h @ w_gate) * (h @ w_up)) @ w_down

def causal_dwconv(xb, buf, w, b):
    T = xb.shape[1]
    xp = jnp.concatenate([buf, xb], axis=1)
    y = b + xp[:, 0:T] * w[0]
    for j in range(1, CONV_WIDTH):
        y = y + xp[:, j:j + T] * w[j]
    return y, xp[:, -(CONV_WIDTH - 1):]

def rglru(xc, h0, w_a, b_a, w_x, b_x, lam):
    B, T, _ = xc.shape
    xh = xc.reshape(B, T, RG_HEADS, RG_HEAD_DIM)
    r = jax.nn.sigmoid(jnp.einsum('bthi,hij->bthj', xh, w_a) + b_a).reshape(B, T, RG_WIDTH)
    i = jax.nn.sigmoid(jnp.einsum('bthi,hij->bthj', xh, w_x) + b_x).reshape(B, T, RG_WIDTH)
    log_a = -RG_C * jax.nn.softplus(-lam.astype(jnp.float32)) * r.astype(jnp.float32)
    a = jnp.exp(log_a)
    mult = jnp.sqrt(-jnp.expm1(2.0 * log_a))
    u = mult * (i * xc).astype(jnp.float32)
    u = u.at[:, 0].add(a[:, 0] * h0.astype(jnp.float32))

    def combine(lhs, rhs):
        return (lhs[0] * rhs[0], rhs[0] * lhs[1] + rhs[1])

    _, hs = lax.associative_scan(combine, (a, u), axis=1)
    return hs, hs[:, -1]

def gla_chunked(q, k, v, log_a, S0):
    B, T, H, DK = q.shape
    DV = v.shape[-1]
    C = math.gcd(T, GLA_CHUNK)
    n = T // C

    def to_chunks(t):
        return t.reshape(B, n, C, H, t.shape[-1]).swapaxes(0, 1)

    mask = jnp.tril(jnp.ones((C, C), dtype=bool))

    def step(S, inp):
        qc, kc, vc, lac = inp
        b = jnp.cumsum(lac, axis=1)
        b_last = b[:, -1]
        qt = qc * jnp.exp(b)
        kt = kc * jnp.exp(-b)
        attn = jnp.where(mask, jnp.einsum('bihk,bjhk->bhij', qt, kt), 0.0)
        o = jnp.einsum('bihk,bhkv->bihv', qt, S) + jnp.einsum('bhij,bjhv->bihv', attn, vc)
        kd = kc * jnp.exp(b_last[:, None] - b)
        S = jnp.exp(b_last)[..., None] * S + jnp.einsum('bjhk,bjhv->bhkv', kd, vc)
        return S, o

    S, o = lax.scan(step, S0, (to_chunks(q), to_chunks(k), to_chunks(v), to_chunks(log_a)))
    return o.swapaxes(0, 1).reshape(B, T, H, DV), S

def memory_kv(mem, mem_norm, w_ck, w_cv):
    B = mem.shape[0]
    m = rmsnorm(mem, mem_norm)
    k = (m @ w_ck).reshape(B, N_MEM, XA_HEADS, XA_HEAD_DIM)
    v = (m @ w_cv).reshape(B, N_MEM, XA_HEADS, XA_HEAD_DIM)
    return k, v

def cross_attend(x, mem_k, mem_v, g, w_cq, w_co):
    B, T, _ = x.shape
    q = (rmsnorm(x, g) @ w_cq).reshape(B, T, XA_HEADS, XA_HEAD_DIM)
    s = jnp.einsum('bthd,bmhd->bhtm', q, mem_k).astype(jnp.float32) * (XA_HEAD_DIM ** -0.5)
    pr = jax.nn.softmax(s, axis=-1).astype(mem_v.dtype)
    o = jnp.einsum('bhtm,bmhd->bthd', pr, mem_v).reshape(B, T, D_MODEL)
    return o @ w_co

def token_mixer(h, conv_buf, rg_h0, gla_S0, p):
    B, T, _ = h.shape
    pin = h @ p['w_in']
    xb = pin[..., OFF_RG_X:OFF_RG_Y]
    yb = pin[..., OFF_RG_Y:OFF_Q]
    q = pin[..., OFF_Q:OFF_K].reshape(B, T, GLA_HEADS, GLA_DK)
    k = pin[..., OFF_K:OFF_V].reshape(B, T, GLA_HEADS, GLA_DK)
    v = pin[..., OFF_V:OFF_G].reshape(B, T, GLA_HEADS, GLA_DV)
    g = pin[..., OFF_G:OFF_A]
    a_low = pin[..., OFF_A:D_IN]
    xc, new_conv = causal_dwconv(xb, conv_buf, p['conv_w'], p['conv_b'])
    hs, rg_h = rglru(xc, rg_h0, p['rg_w_a'], p['rg_b_a'], p['rg_w_x'], p['rg_b_x'], p['rg_lambda'])
    rg_out = rmsnorm(hs.astype(h.dtype) * jax.nn.gelu(yb), p['rg_out_norm'])
    z = (a_low @ p['gla_w_a2'] + p['gla_b_a2']).astype(jnp.float32)
    log_a = (jax.nn.log_sigmoid(z) / GLA_GATE_NORMALIZER).reshape(B, T, GLA_HEADS, GLA_DK)
    o, S = gla_chunked(q.astype(jnp.float32) * (GLA_DK ** -0.5), k.astype(jnp.float32),
                       v.astype(jnp.float32), log_a, gla_S0.astype(jnp.float32))
    gla_out = rmsnorm(o.astype(h.dtype), p['gla_out_norm']).reshape(B, T, GLA_WIDTH) * jax.nn.silu(g)
    out = jnp.concatenate([rg_out, gla_out], axis=-1) @ p['w_out']
    return out, new_conv, rg_h.astype(h.dtype), S.astype(h.dtype)

def decoder_layer(x, mem_k, mem_v, conv_buf, rg_h0, gla_S0, p):
    x = x + 0.5 * swiglu_ffn(x, p['ffn1_norm'], p['ffn1_w_gate'], p['ffn1_w_up'], p['ffn1_w_down'])
    mix, new_conv, new_h, new_S = token_mixer(rmsnorm(x, p['mix_norm']), conv_buf, rg_h0, gla_S0, p)
    x = x + mix
    x = x + cross_attend(x, mem_k, mem_v, p['xattn_norm'], p['w_cq'], p['w_co'])
    x = x + 0.5 * swiglu_ffn(x, p['ffn2_norm'], p['ffn2_w_gate'], p['ffn2_w_up'], p['ffn2_w_down'])
    return x, new_conv, new_h, new_S

def setup_inputs(seed: int = 0) -> dict:
    key = jax.random.key(seed)
    ks = iter(jax.random.split(key, 48))
    f32 = jnp.float32

    def nrm(shape, scale):
        return jax.random.normal(next(ks), shape, f32) * scale

    def gain(n):
        return 1.0 + nrm((n,), 0.02)

    u = jax.random.uniform(next(ks), (RG_WIDTH,), f32, 0.9, 0.999)
    rg_lambda = jnp.log(u) - jnp.log1p(-u)
    return {
        "x_prompt": nrm((BATCH, SEQ, D_MODEL), 1.0),
        "x_sample": nrm((DEC_BATCH, DEC_SEQ, D_MODEL), 1.0),
        "cache_mem_k": nrm((DEC_BATCH, N_MEM, XA_HEADS, XA_HEAD_DIM), 1.0),
        "cache_mem_v": nrm((DEC_BATCH, N_MEM, XA_HEADS, XA_HEAD_DIM), 1.0),
        "state_conv": nrm((DEC_BATCH, CONV_WIDTH - 1, RG_WIDTH), 1.0),
        "state_rglru": nrm((DEC_BATCH, RG_WIDTH), 0.5),
        "state_gla": nrm((DEC_BATCH, GLA_HEADS, GLA_DK, GLA_DV), 0.5),
        "mem_prompt": nrm((BATCH, N_MEM, D_MODEL), 1.0),
        "ffn1_norm": gain(D_MODEL),
        "ffn1_w_gate": nrm((D_MODEL, D_FF), D_MODEL ** -0.5),
        "ffn1_w_up": nrm((D_MODEL, D_FF), D_MODEL ** -0.5),
        "ffn1_w_down": nrm((D_FF, D_MODEL), D_FF ** -0.5),
        "mix_norm": gain(D_MODEL),
        "w_in": nrm((D_MODEL, D_IN), D_MODEL ** -0.5),
        "conv_w": nrm((CONV_WIDTH, RG_WIDTH), CONV_WIDTH ** -0.5),
        "conv_b": nrm((RG_WIDTH,), 0.01),
        "rg_w_a": nrm((RG_HEADS, RG_HEAD_DIM, RG_HEAD_DIM), RG_HEAD_DIM ** -0.5),
        "rg_b_a": nrm((RG_HEADS, RG_HEAD_DIM), 0.01),
        "rg_w_x": nrm((RG_HEADS, RG_HEAD_DIM, RG_HEAD_DIM), RG_HEAD_DIM ** -0.5),
        "rg_b_x": nrm((RG_HEADS, RG_HEAD_DIM), 0.01),
        "rg_lambda": rg_lambda,
        "rg_out_norm": gain(RG_WIDTH),
        "gla_w_a2": nrm((GLA_GATE_RANK, GLA_KEY_WIDTH), GLA_GATE_RANK ** -0.5),
        "gla_b_a2": nrm((GLA_KEY_WIDTH,), 0.01),
        "gla_out_norm": gain(GLA_DV),
        "w_out": nrm((D_MIX, D_MODEL), D_MIX ** -0.5),
        "xattn_norm": gain(D_MODEL),
        "mem_norm": gain(D_MODEL),
        "w_cq": nrm((D_MODEL, D_MODEL), D_MODEL ** -0.5),
        "w_ck": nrm((D_MODEL, D_MODEL), D_MODEL ** -0.5),
        "w_cv": nrm((D_MODEL, D_MODEL), D_MODEL ** -0.5),
        "w_co": nrm((D_MODEL, D_MODEL), D_MODEL ** -0.5),
        "ffn2_norm": gain(D_MODEL),
        "ffn2_w_gate": nrm((D_MODEL, D_FF), D_MODEL ** -0.5),
        "ffn2_w_up": nrm((D_MODEL, D_FF), D_MODEL ** -0.5),
        "ffn2_w_down": nrm((D_FF, D_MODEL), D_FF ** -0.5),
        "final_norm": gain(D_MODEL),
    }

def reference(x_prompt, x_sample, cache_mem_k, cache_mem_v, state_conv, state_rglru, state_gla,
              mem_prompt, ffn1_norm, ffn1_w_gate, ffn1_w_up, ffn1_w_down, mix_norm, w_in,
              conv_w, conv_b, rg_w_a, rg_b_a, rg_w_x, rg_b_x, rg_lambda, rg_out_norm,
              gla_w_a2, gla_b_a2, gla_out_norm, w_out, xattn_norm, mem_norm, w_cq, w_ck, w_cv,
              w_co, ffn2_norm, ffn2_w_gate, ffn2_w_up, ffn2_w_down, final_norm):
    p = dict(ffn1_norm=ffn1_norm, ffn1_w_gate=ffn1_w_gate, ffn1_w_up=ffn1_w_up,
             ffn1_w_down=ffn1_w_down, mix_norm=mix_norm, w_in=w_in, conv_w=conv_w,
             conv_b=conv_b, rg_w_a=rg_w_a, rg_b_a=rg_b_a, rg_w_x=rg_w_x, rg_b_x=rg_b_x,
             rg_lambda=rg_lambda, rg_out_norm=rg_out_norm, gla_w_a2=gla_w_a2,
             gla_b_a2=gla_b_a2, gla_out_norm=gla_out_norm, w_out=w_out,
             xattn_norm=xattn_norm, w_cq=w_cq, w_co=w_co, ffn2_norm=ffn2_norm,
             ffn2_w_gate=ffn2_w_gate, ffn2_w_up=ffn2_w_up, ffn2_w_down=ffn2_w_down)
    dt = x_prompt.dtype
    Bp = x_prompt.shape[0]

    mem_k_p, mem_v_p = memory_kv(mem_prompt, mem_norm, w_ck, w_cv)
    xp = x_prompt
    conv_p = jnp.zeros((Bp, CONV_WIDTH - 1, RG_WIDTH), dt)
    h_p = jnp.zeros((Bp, RG_WIDTH), dt)
    S_p = jnp.zeros((Bp, GLA_HEADS, GLA_DK, GLA_DV), dt)
    for _ in range(DEPTH):
        xp, conv_p, h_p, S_p = decoder_layer(xp, mem_k_p, mem_v_p, conv_p, h_p, S_p, p)
    y_prompt = rmsnorm(xp, final_norm)

    xs = x_sample
    conv_s, h_s, S_s = state_conv, state_rglru, state_gla
    for _ in range(DEPTH):
        xs, conv_s, h_s, S_s = decoder_layer(xs, cache_mem_k, cache_mem_v, conv_s, h_s, S_s, p)
    y_sample = rmsnorm(xs, final_norm)

    return (y_prompt, y_sample, mem_k_p, mem_v_p, conv_p, h_p, S_p, conv_s, h_s, S_s)


_drawn_inputs = setup_inputs


def setup_inputs(seed=0):
    import zlib

    import numpy as np

    out = dict(_drawn_inputs(seed))
    spreads = {}
    factors = {'ffn1_norm': 4.962,
     'rg_b_a': 8.0,
     'rg_b_x': 8.0,
     'rg_out_norm': 5.089,
     'gla_b_a2': 8.0,
     'gla_out_norm': 8.0,
     'xattn_norm': 8.0,
     'mem_norm': 3.099,
     'ffn2_norm': 8.0,
     'final_norm': 2.683}
    for name, (base, spread) in spreads.items():
        noise = np.random.default_rng([zlib.crc32(name.encode()), seed]).standard_normal(out[name].shape)
        drawn = base * np.exp(spread * noise) if base else spread * noise
        out[name] = __import__('jax').numpy.asarray(drawn.astype(out[name].dtype))
    for name, factor in factors.items():
        out[name] = (out[name] * factor).astype(out[name].dtype)
    return out
```

```python
from contextlib import ExitStack

import concourse.bass as bass
from concourse import mybir

P = 128
D = 1024
KT = D // P
FF = 2816
FT = FF // P
SEQ, NSEQ, TS = 1024, 8, 8
SAMPLE = NSEQ * TS
TOK = SEQ + SAMPLE
MEM = 256
HEADS = 4
RANK = 16
CH = 32
EPS = 1e-6
OFFS = [0, 384, 768]
NS = [384, 384, 320]
NMAX = 384
NPROMPT = [384, 384, 256]
TT = NMAX // P

F32 = mybir.dt.float32
F32R = mybir.dt.float32r
ALU = mybir.AluOpType
ACT = mybir.ActivationFunctionType
AX = mybir.AxisListType

GAINS = {"ffn1": 0, "mix": 8, "mem": 16, "xan": 24, "ffn2": 32, "fin": 40}
V_RGO, V_GLO = 48, 52
V_CW, V_CB = 53, 69
V_BA, V_BX, V_LAM, V_BA2 = 73, 77, 81, 85
NV = 87
C_ONES, C_ID, C_ROW, C_M32, C_M8, C_SCAN, C_SCAN2 = 0, 128, 256, 264, 392, 456, 840
NC_A = 256
NCONST = 1160

ITS = FT // 2
FFN_TILES = 6 * ITS
STAGE_TILES = {"rg": (0, 8), "gla": (8, 12), "out": (20, 8), "memk": (28, 8), "memv": (36, 8), "cq": (44, 8), "co": (52, 8)}
STAGES = [("rg", 0), ("gla", 0), ("rg", 1), ("out", 0), ("gla", 1), ("rg", 2), ("out", 1), ("gla", 2),
          ("memk", 0), ("memv", 0), ("out", 2), ("cq", 0), ("co", 0), ("cq", 1), ("co", 1), ("cq", 2), ("co", 2)]
FIRST = {}
_t = 0
for _s in STAGES:
    FIRST[_s] = _t
    _t += STAGE_TILES[_s[0]][1]
MIX_TILES = _t
RING = 4


class Norm:

    def __init__(self, kind, n, groups, rows, N, outs):
        self.kind, self.n, self.groups, self.rows, self.N, self.outs = kind, n, groups, rows, N, outs
        self.T = (N + P - 1) // P


NORMS = {}


def _norm(kind, n):
    if kind == "rgo":
        a = Norm(kind, n, 1, 4, NS[n], 1)
    elif kind == "glo":
        a = Norm(kind, n, 4, 1, NS[n], 1)
    elif kind == "mem":
        a = Norm(kind, n, 1, 8, MEM, 2)
    elif kind == "fin":
        a = Norm(kind, n, 1, 8, NS[n], 1)
    else:
        a = Norm(kind, n, 1, 8, NS[n], 2)
    a.index = len(NORMS)
    before = list(NORMS.values())
    a.sq0 = sum(b.groups * b.rows for b in before)
    a.out0 = sum(b.outs for b in before)
    a.diag0 = sum(b.groups for b in before)
    NORMS[kind, n] = a


for _k in [("ffn1", 0), ("ffn1", 1), ("ffn1", 2), ("mix", 0), ("rgo", 0), ("mix", 1), ("glo", 0), ("rgo", 1), ("mix", 2),
           ("glo", 1), ("rgo", 2), ("mem", 0), ("glo", 2), ("xan", 0), ("xan", 1), ("xan", 2),
           ("ffn2", 0), ("ffn2", 1), ("ffn2", 2), ("fin", 0), ("fin", 1), ("fin", 2)]:
    _norm(*_k)

TURN = {}
_used, _filled = [0] * 4, [0] * 4


def _turn(*key, full=True):
    b = len(TURN) % 4
    TURN[key] = (b, _used[b], _filled[b])
    _used[b] += 1
    _filled[b] += full


def _norm_turns(kind, n):
    _turn("st", kind, n, full=False)
    for g in range(NORMS[kind, n].groups):
        _turn("rb", kind, n, g)


def _gla_a(n, t):
    _turn("kdt", n, t)
    _turn("at", n, t, 0)
    _turn("at", n, t, 1)
    if NPROMPT[n] > t * P:
        for c in range(P // CH):
            _turn("kv", n, t, c)


def _gla_b(n, t):
    _turn("o", n, t, 0)
    _turn("o", n, t, 1)
    if NPROMPT[n] <= t * P:
        for b in range(NSEQ):
            _turn("kvs", b)


for _n in range(3):
    _norm_turns("ffn1", _n)
_norm_turns("mix", 0)
for _n in range(3):
    for _j in range(8):
        _turn("gate", _n, _j)
    _turn("low", _n)
    _turn("z", _n, 0)
    _turn("z", _n, 1)
    _norm_turns("rgo", _n)
    _norm_turns(*(("mix", _n + 1) if _n < 2 else ("mem", 0)))
    for _tt in range(TT):
        _gla_a(_n, _tt)
        if _tt:
            _gla_b(_n, _tt - 1)
    _gla_b(_n, TT - 1)
    _norm_turns("glo", _n)


def _att_b(n, t):
    _turn("pt", n, t, 0)
    _turn("pt", n, t, 1)
    _turn("pv", n, t, 0)
    if NPROMPT[n] > t * P:
        _turn("pv", n, t, 1)


for _n in range(3):
    _norm_turns("xan", _n)
    for _tt in range(TT):
        _turn("sc", _n, _tt, 0)
        _turn("sc", _n, _tt, 1)
        if _tt:
            _att_b(_n, _tt - 1)
    _att_b(_n, TT - 1)
for _k in ("ffn2", "fin"):
    for _n in range(3):
        _norm_turns(_k, _n)


def program(nc, a, out):
    base = (nc.sbuf_base + 63) // 64 * 64
    end = nc.sbuf_usable_end
    ctx = ExitStack()
    with ctx:
        def at(name, shape, offset, dtype=F32):
            offset = (offset + 31) // 32 * 32
            size = 4
            for s in shape[1:]:
                size *= s
            assert offset + size <= end, (name, offset + size - end)
            return nc.alloc_sbuf_tensor_at(name, shape, dtype, offset=offset), offset + size

        x, o = at("x", [P, KT, TOK], base)
        sq, o_ = at("sq", [P, 4, NMAX], o)
        sil, o2 = at("sil", [P, 2, NMAX], o)
        hf, _ = at("hf", [P, 2, NMAX], o2)
        o = o_
        diag, o = at("diag", [P, 2, TT, P], o)
        cst, o = at("cst", [P, NC_A], o)
        vec, o = at("vec", [P, NV + 1], o)
        rgc, o = at("rgc", [P, 8, 4], o)
        st, o = at("st", [P, 3, 12], o)
        o = (o + 63) // 64 * 64
        w_hi_sb, o = at("w_hi_sb", [P, 6, 1024], o, F32R)
        ffn_lo = o
        w_lo_sb, o = at("w_lo_sb", [P, 6, 1024], o, F32R)
        raw, o = at("raw", [P, 6, 1024], o)
        a_hi, o = at("a_hi", [P, KT, TOK], o, F32R)
        a_lo, o = at("a_lo", [P, KT, TOK], o, F32R)
        h_hi, o = at("h_hi", [P, 2, TOK], o, F32R)
        h_lo, o = at("h_lo", [P, 2, TOK], o, F32R)
        ffn_end = o
        slot = 4096
        hole_hi = ffn_lo - 2 * slot
        hole_lo = ffn_lo + 4 * slot
        hole_raw = ffn_lo + 6 * slot + 4 * slot
        S, _ = at("S", [P, 8, 2, P], hole_hi)
        qm, q = at("qm", [P, 2, KT, SAMPLE], hole_hi)
        pt, _ = at("pt", [P, 2 * HEADS, P], q)
        cmix, q = at("cmix", [P, NCONST - NC_A], hole_lo)
        bd, q = at("bd", [P, 8, P], q)
        assert q <= hole_lo + 2 * slot, q - hole_lo - 2 * slot
        o = hole_raw
        xn_hi, o = at("xn_hi", [P, KT, NMAX], o, F32R)
        xn_lo, o2 = at("xn_lo", [P, KT, NMAX], o, F32R)
        s0, q = at("s0", [P, NSEQ, 2, P], o - 4 * KT * NMAX)
        kdm, q = at("kdm", [P, NSEQ, 2 * P], o)
        o = o2
        mo_hi, o2 = at("mo_hi", [P, KT, NMAX], o, F32R)
        I, _ = at("I", [P, 4, NMAX], o + 4 * 4 * NMAX)
        osb, _ = at("osb", [P, 4, NMAX], o + 4 * 4 * NMAX)
        o = o2
        mo_lo, o2 = at("mo_lo", [P, KT, NMAX], o, F32R)
        T_, _ = at("T_", [P, 4, NMAX], o + 4 * 4 * NMAX)
        Z, q = at("Z", [P, 2, NMAX], o + 4 * 4 * NMAX)
        E_, _ = at("E_", [P, 2, NMAX], q)
        qa, _ = at("qa", [P, KT, NMAX], o)
        o = o2
        region = o
        xbuf, o = at("xbuf", [P, 4, 3 + NMAX], o)
        xs, o = at("xs", [P, 4, NSEQ, 3 + TS], o)
        ybuf, o = at("ybuf", [P, 4, NMAX], o)
        kmem, o2 = at("kmem", [P, KT, MEM], region)
        memx, _ = at("memx", [P, KT, MEM], o2)
        vmem, o2 = at("vmem", [P, 2, D], o2)
        o = max(o, o2)
        union = o
        qk, o = at("qk", [P, 4, NMAX], o)
        gg, o = at("gg", [P, 4, NMAX], o)
        vt, o = at("vt", [P, TT, 4 * P], o)
        w_al_hi, o = at("w_al_hi", [P, KT, RANK], o, F32R)
        w_al_lo, o = at("w_al_lo", [P, KT, RANK], o, F32R)
        w_a2, o = at("w_a2", [RANK, 2 * P], o)
        hcar, o = at("hcar", [P, 4, 1], o)
        h0, o = at("h0", [P, 4, NSEQ], o)
        h0a, o = at("h0a", [P, 4, NSEQ], o)
        hlast, o = at("hlast", [P, 4, 1 + NSEQ], o)
        al, o = at("al", [RANK, NMAX], o)
        temps = o
        xc, o = at("xc", [P, 4, NMAX], o)
        R, o = at("R", [P, 4, NMAX], o)
        o2 = temps
        B, o2 = at("B", [P, 2, NMAX], o2)
        kd, o2 = at("kd", [P, 2, NMAX], o2)
        kdt, o2 = at("kdt", [P, TT, 2 * P], o2)
        AT, o2 = at("AT", [P, 2, 4, P], o2)
        o = union
        pr, o = at("pr", [P, 2, HEADS, MEM], o)
        kc, o = at("kc", [P, 3, 2 * D], o)
        mx, o = at("mx", [P, 2, 4, HEADS], o)

        ps = ctx.enter_context(nc.psum_tensor("ps", [P, 8, 512], F32))
        ones, ident = cst[:, C_ONES:C_ONES + P], cst[:, C_ID:C_ID + P]

        def mixc(c0, n):
            return cmix[:, c0 - NC_A:c0 - NC_A + n]

        def sem(name):
            return ctx.enter_context(nc.semaphore(name))

        raw_in = [sem(f"raw_in{k}") for k in range(6)]
        w_hi, w_lo = sem("w_hi"), sem("w_lo")
        x_in, const_in, mix_in, mem_in, state_in, s0_in = [sem(k) for k in ("x_in", "const_in", "mix_in", "mem_in", "state_in", "s0_in")]
        gu_done, silu_done, h_done, hhi_done, hid_done, down_done, x_added = [
            sem(k) for k in ("gu_done", "silu_done", "h_done", "hhi_done", "hid_done", "down_done", "x_added")]
        tile_done, evicted = sem("tile_done"), sem("evicted")
        squared, sq_used, root_done, diag_done, normed = [
            sem(k) for k in ("squared", "sq_used", "root_done", "diag_done", "normed")]
        bank_full = [sem(f"bank_full{b}") for b in range(4)]
        bank_free = [sem(f"bank_free{b}") for b in range(4)]
        dve_chain, act_chain = sem("dve_chain"), sem("act_chain")
        lam_done, wal_done = sem("lam_done"), sem("wal_done")
        conv_done, gates_done, u_ready, decay_done, mult_ready, root_mult, y_done, rg_out, rg_free = [
            sem(k) for k in ("conv_done", "gates_done", "u_ready", "decay_done", "mult_ready", "root_mult", "y_done", "rg_out", "rg_free")]
        soft_done, b_out, eneg_done, db_out, edb_done, qk_out, silug_done = [
            sem(k) for k in ("soft_done", "b_out", "eneg_done", "db_out", "edb_done", "qk_out", "silug_done")]
        kdm_done, max_done, pr_done, ohi_done, qm_done, ss_done, sv_done = [
            sem(k) for k in ("kdm_done", "max_done", "pr_done", "ohi_done", "qm_done", "ss_done", "sv_done")]
        kc_in = [sem(f"kc_in{k}") for k in range(3)]
        stored, y_stored = sem("stored"), sem("y_stored")

        block = ctx.enter_context(nc.Block())

        def bank(*key):
            return ps[:, 4 + TURN[key][0], :]

        def fill_wait(eng, *key):
            b, used, _ = TURN[key]
            if used:
                eng.wait_ge(bank_free[b], used)

        def full_wait(eng, *key):
            b, _, filled = TURN[key]
            eng.wait_ge(bank_full[b], filled + 1)

        def filled(ins, *key):
            ins.then_inc(bank_full[TURN[key][0]], 1)

        def release(ins, *key):
            ins.then_inc(bank_free[TURN[key][0]], 1)

        def read_wait(eng, *key):
            b, used, _ = TURN[key]
            eng.wait_ge(bank_free[b], used + 1)

        def tokens(n):
            return slice(OFFS[n], OFFS[n] + NS[n])

        def norm_source(kind, n, g, k):
            N = NORMS[kind, n].N
            if kind == "rgo":
                return I[:, k, 0:N]
            if kind == "glo":
                return osb[:, g, 0:N]
            if kind == "mem":
                return memx[:, k, :]
            return x[:, k, tokens(n)]

        GATE_UP_STEPS = 6 * ITS
        DOWNS = 3 * KT * ITS

        def wait_source(eng, kind, n):
            if kind == "ffn1":
                eng.wait_ge(x_in, 16 * 3)
            elif kind == "mix":
                eng.wait_ge(x_added, DOWNS - 3 * KT + KT * (n + 1))
            elif kind == "rgo":
                eng.wait_ge(rg_out, n + 1)
            elif kind == "glo":
                for t in range(TT):
                    for e in range(2):
                        read_wait(eng, "o", n, t, e)
            elif kind == "mem":
                eng.wait_ge(mem_in, 16)
            elif kind == "xan":
                eng.wait_ge(evicted, FIRST["out", n] + 8)
            elif kind == "ffn2":
                eng.wait_ge(evicted, FIRST["co", n] + 8)
            elif kind == "fin":
                eng.wait_ge(x_added, 2 * DOWNS - 3 * KT + KT * (n + 1))

        @block.sync
        def _(sp):
            for n in range(3):
                sp.dma_start(x[:, :, tokens(n)], a["x"].rearrange("(k p) t -> p k t", p=P)[:, :, tokens(n)]).then_inc(x_in, 16)
            sp.dma_start(cst[:, :], a["consts"][:, 0:NC_A]).then_inc(const_in, 16)
            sp.dma_start(vec[:, 0:NV], a["vectors"]).then_inc(const_in, 16)

            def ffn_loads(f, it, first):
                src = [a[f"ffn{f + 1}_{w}"] for w in ("gate", "up", "gate", "up", "down", "down")]
                for k in range(6):
                    if not first:
                        sp.wait_ge(w_lo, f * (FFN_TILES + MIX_TILES) + 6 * it + k - 5)
                    elif f:
                        sp.wait_ge(w_lo, FFN_TILES + MIX_TILES - RING + min(k, RING - 1) + 1)
                    half = (0, 0, 1, 1, 0, 1)[k]
                    sp.dma_start(raw[:, k, :], src[k][bass.ds(2 * it + half, 1), :, :].rearrange("a p n -> p (a n)"))\
                      .then_inc(raw_in[k], 16)

            def cache_loads():
                for i in range(3, 2 * NSEQ):
                    if i - 3 < NSEQ - 1:
                        sp.wait_ge(ss_done, i - 2)
                    elif i - 3 == NSEQ - 1:
                        full_wait(sp, "sc", 2, 2, 1)
                    else:
                        sp.wait_ge(sv_done, i - 2 - NSEQ)
                    src = a["cache_k"][i, :, :] if i < NSEQ else a["cache_v"][i - NSEQ, :, :]
                    sp.dma_start(kc[:, i % 3, :], src).then_inc(kc_in[i % 3], 16)

            ffn_loads(0, 0, True)
            with sp.Fori(1, ITS) as it:
                ffn_loads(0, it, False)
            for t in range(MIX_TILES):
                if t == 4:
                    sp.wait_ge(down_done, DOWNS)
                    sp.dma_start(cmix[:, :], a["consts"][:, NC_A:NCONST]).then_inc(mix_in, 16)
                    sp.dma_start(bd[:, :, :], a["gates"]).then_inc(mix_in, 16)
                    sp.dma_start(w_a2[:, :], a["w_a2"]).then_inc(mix_in, 16)
                    sp.dma_start(h0[:, :, :], a["h0"]).then_inc(mix_in, 16)
                    sp.dma_start(R[:, 0, 0:KT * RANK], a["w_alow"]).then_inc(mix_in, 16)
                    for j in range(4):
                        sp.dma_start(xs[:, j, :, 0:3], a["conv0"][:, j, :, :]).then_inc(state_in, 16)
                if t == FIRST["memk", 0] + 3:
                    sp.wait_ge(rg_out, 3)
                    sp.dma_start(memx[:, :, :], a["mem"].rearrange("(k p) t -> p k t", p=P)).then_inc(mem_in, 16)
                    sp.dma_start(out["conv_p"], xbuf[:, :, NPROMPT[2]:NPROMPT[2] + 3]).then_inc(stored, 16)
                    for j in range(4):
                        sp.dma_start(out["conv_s"][:, j, :, :], xs[:, j, :, TS:TS + 3]).then_inc(stored, 16)
                    sp.dma_start(out["h"], hlast[:, :, :]).then_inc(stored, 16)
                if t == FIRST["co", 2] + 6:
                    cache_loads()
                stage = max((s for s in STAGES if FIRST[s] <= t), key=lambda s: FIRST[s])
                row = STAGE_TILES[stage[0]][0] + t - FIRST[stage]
                sp.wait_ge(w_lo, FFN_TILES + t - RING + 1 if t >= RING else FFN_TILES - 6 + t + 1)
                sp.dma_start(raw[:, t % RING, :], a["mix_tiles"][row, :, :]).then_inc(raw_in[t % RING], 16)
                if t == FIRST["out", 2]:
                    sp.wait_ge(tile_done, FIRST["memv", 0] + 8)
                    sp.dma_start(s0[:, :, :, :], a["s0"]).then_inc(s0_in, 16)
                    sp.wait_ge(evicted, FIRST["memv", 0] + 8)
                    sp.dma_start(out["mem_k"], kmem[:, :, :]).then_inc(stored, 16)
                    sp.dma_start(out["mem_v"], vmem[:, :, :]).then_inc(stored, 16)
                if t == FIRST["cq", 0]:
                    for b in range(NSEQ):
                        read_wait(sp, "kvs", b)
                    read_wait(sp, "kv", 2, 1, 3)
                    sp.dma_start(out["s_s"], s0[:, :, :, :]).then_inc(stored, 16)
                    sp.dma_start(out["s_p"], S[:, (SEQ // CH) % 8, :, :]).then_inc(stored, 16)
                if t == FIRST["cq", 2]:
                    for i in range(3):
                        sp.dma_start(kc[:, i, :], a["cache_k"][i, :, :]).then_inc(kc_in[i], 16)
            sp.wait_ge(evicted, MIX_TILES)
            sp.wait_ge(stored, 16 * 10)
            ffn_loads(1, 0, True)
            with sp.Fori(1, ITS) as it:
                ffn_loads(1, it, False)
            for n in range(3):
                p = NORMS["fin", n]
                for h in range(2):
                    if h == 0:
                        sp.wait_ge(normed, p.out0 + 1)
                    else:
                        read_wait(sp, "rb", "fin", n, 0)
                    sp.dma_start(out["y"].rearrange("(k p) t -> p k t", p=P)[:, 4 * h:4 * h + 4, tokens(n)], sq[:, :, 0:p.N])\
                      .then_inc(y_stored, 16)
            sp.wait_ge(y_stored, 16 * 6)

        @block.gpsimd
        def _(pool):
            def low(slot_, count):
                pool.wait_ge(w_hi, count)
                nc.gpsimd.tensor_tensor(w_lo_sb[:, slot_, :], raw[:, slot_, :], w_hi_sb[:, slot_, :].bitcast(F32), ALU.subtract)\
                  .then_inc(w_lo, 1)

            with pool.Fori(0, ITS) as it:
                for k in range(6):
                    low(k, 6 * it + k + 1)
            with pool.Fori(0, MIX_TILES // RING) as i:
                for k in range(RING):
                    low(k, FFN_TILES + RING * i + k + 1)
            with pool.Fori(0, ITS) as it:
                for k in range(6):
                    low(k, FFN_TILES + MIX_TILES + 6 * it + k + 1)

        @block.scalar
        def _(act):
            chain = [0]

            def link(ins):
                chain[0] += 1
                ins.then_inc(act_chain, 1)
                act.wait_ge(act_chain, chain[0])

            def prep(slot_, uses):
                act.wait_ge(raw_in[slot_], 16 * uses)
                nc.scalar.activation(w_hi_sb[:, slot_, :], raw[:, slot_, :], ACT.Copy).then_inc(w_hi, 1)

            mix_uses = MIX_TILES // RING

            def ffn_prep(f, it, k):
                before = f * (ITS + (mix_uses if k < RING else 0))
                prep(k, before + it + 1)

            def mix_prep(t):
                if t < MIX_TILES:
                    if t >= RING:
                        act.wait_ge(tile_done, t - RING + 1)
                    prep(t % RING, ITS + t // RING + 1)

            def norm_squares(kind, n, lo=0, hi=99):
                p = NORMS[kind, n]
                for i in range(max(lo, 0), min(hi, p.groups * p.rows)):
                    g, k = i // p.rows, i % p.rows
                    if i == 0:
                        wait_source(act, kind, n)
                        if p.out0:
                            act.wait_ge(normed, p.out0)
                        if kind == "fin" and n:
                            act.wait_ge(y_stored, 32 * n)
                    if p.sq0 + i >= 4:
                        act.wait_ge(sq_used, p.sq0 + i - 3)
                    nc.scalar.activation(sq[:, (p.sq0 + i) % 4, 0:p.N], norm_source(kind, n, g, k), ACT.Square).then_inc(squared, 1)

            def norm_root(kind, n):
                p = NORMS[kind, n]
                read_wait(act, "st", kind, n)
                m = p.groups * p.T
                nc.scalar.activation(st[:, 1, 0:m], st[:, 0, 0:m], ACT.Sqrt).then_inc(root_done, 1)

            def norm(kind, n):
                norm_squares(kind, n)
                norm_root(kind, n)

            def ffn(f):
                def step(q0, s, first):
                    act.wait_ge(gu_done, f * GATE_UP_STEPS + q0 + s + 1)
                    if f or not first or s >= 2:
                        act.wait_ge(h_done, f * GATE_UP_STEPS + q0 + s - 1)
                    N = NS[s % 3]
                    nc.scalar.activation(sil[:, s % 2, 0:N], ps[:, 4 + 2 * (s % 2), 0:N], ACT.Silu).then_inc(silu_done, 1)

                def body(it, first, last):
                    q0 = 6 * it
                    step(q0, 0, first)
                    for k in (4, 5):
                        if not first:
                            act.wait_ge(down_done, f * DOWNS + 3 * KT * it)
                        ffn_prep(f, it, k)
                        step(q0, k - 3, first)
                    for k in (0, 1):
                        step(q0, 3 + k, first)
                        if not last:
                            act.wait_ge(gu_done, f * GATE_UP_STEPS + q0 + 3)
                            ffn_prep(f, it + 1, k)
                    step(q0, 5, first)
                    if not last:
                        for k in (2, 3):
                            act.wait_ge(gu_done, f * GATE_UP_STEPS + q0 + 6)
                            ffn_prep(f, it + 1, k)

                body(0, True, False)
                with act.Fori(1, ITS - 1) as it:
                    body(it, False, False)
                body(ITS - 1, False, True)

            act.wait_ge(const_in, 32)
            for k in range(4):
                ffn_prep(0, 0, k)
            lam = vec[:, V_LAM:V_LAM + 4]
            link(nc.scalar.activation(rgc[:, 0, :], lam, ACT.Abs))
            nc.scalar.activation(rgc[:, 1, :], rgc[:, 0, :], ACT.Exp, scale=-1.0).then_inc(lam_done, 1)
            act.wait_ge(lam_done, 2)
            nc.scalar.activation(rgc[:, 3, :], rgc[:, 2, :], ACT.Ln).then_inc(lam_done, 1)

            for n in range(3):
                norm("ffn1", n)
            ffn(0)

            for t in range(3):
                mix_prep(t)
            norm("mix", 0)
            for t in range(8):
                mix_prep(FIRST["rg", 0] + t + 3)
                if t == 4:
                    act.wait_ge(mix_in, 16 * 5)
                    nc.scalar.activation(w_al_hi[:, :, :], R[:, 0, 0:KT * RANK].rearrange("p (k r) -> p k r", k=KT), ACT.Copy)\
                      .then_inc(wal_done, 1)

            def rg_act(n, j):
                N = NS[n]
                if j in (4, 5):
                    if j == 4:
                        act.wait_ge(wal_done, 2)
                    for i in range(4):
                        full_wait(act, "gate", n, 4 * (j - 4) + i)
                        dst, bias = ((R, V_BA), (I, V_BX))[j - 4]
                        ins = nc.scalar.activation(dst[:, i, 0:N], bank("gate", n, 4 * (j - 4) + i)[:, 0:N], ACT.Sigmoid,
                                                   bias=vec[:, bias + i:bias + i + 1])
                        release(ins, "gate", n, 4 * (j - 4) + i)
                if j == 6:
                    act.wait_ge(lam_done, 4)
                    for i in range(8):
                        read_wait(act, "gate", n, i)
                    for i in range(4):
                        nc.scalar.activation(T_[:, i, 0:N], R[:, i, 0:N], ACT.Tanh, scale=rgc[:, 5, i:i + 1])
                if j == 7:
                    for i in range(4):
                        ins = nc.scalar.activation(R[:, i, 0:N], R[:, i, 0:N], ACT.Exp, scale=rgc[:, 6, i:i + 1])
                    ins.then_inc(decay_done, 1)
                if j == 9:
                    act.wait_ge(mult_ready, n + 1)
                    nc.scalar.activation(T_[:, :, 0:N], T_[:, :, 0:N], ACT.Sqrt).then_inc(root_mult, 1)
                if j == 10:
                    nc.scalar.activation(ybuf[:, :, 0:N], ybuf[:, :, 0:N], ACT.Gelu_apprx_tanh).then_inc(y_done, 1)

            def gla_act(n):
                N = NS[n]
                read_wait(act, "z", n, 0)
                read_wait(act, "z", n, 1)
                link(nc.scalar.activation(E_[:, :, 0:N], Z[:, :, 0:N], ACT.Abs))
                link(nc.scalar.activation(E_[:, :, 0:N], E_[:, :, 0:N], ACT.Exp, scale=-1.0))
                nc.scalar.activation(E_[:, :, 0:N], E_[:, :, 0:N], ACT.Ln, bias=1.0).then_inc(soft_done, 1)

            def gla_exp(n):
                N = NS[n]
                act.wait_ge(b_out, n + 1)
                nc.scalar.activation(E_[:, :, 0:N], B[:, :, 0:N], ACT.Exp, scale=-1.0 / 16).then_inc(eneg_done, 1)
                act.wait_ge(db_out, n + 1)
                nc.scalar.activation(Z[:, :, 0:N], Z[:, :, 0:N], ACT.Exp, scale=1.0 / 16)
                nc.scalar.activation(B[:, :, 0:N], B[:, :, 0:N], ACT.Exp, scale=1.0 / 16).then_inc(edb_done, 1)

            def gla_gate(n):
                N = NS[n]
                act.wait_ge(evicted, FIRST["gla", n] + 12)
                nc.scalar.activation(gg[:, :, 0:N], gg[:, :, 0:N], ACT.Silu).then_inc(silug_done, 1)

            def gla_keys(n, t):
                w = min(P, NS[n] - t * P)
                full_wait(act, "kdt", n, t)
                ins = nc.scalar.activation(kdt[0:w, t, :], bank("kdt", n, t)[0:w, 0:2 * P], ACT.Copy)
                release(ins, "kdt", n, t)

            def gla_outs(n, t):
                w = min(P, NS[n] - t * P)
                for e in range(2):
                    full_wait(act, "o", n, t, e)
                    act.wait_ge(normed, NORMS["rgo", n].out0 + 1)
                    ins = nc.scalar.activation(osb[:, e:4:2, t * P:t * P + w],
                                               bank("o", n, t, e)[:, 0:2 * P].rearrange("p (a i) -> p a i", a=2)[:, :, 0:w], ACT.Copy)
                    release(ins, "o", n, t, e)

            def gla(n):
                for t in range(TT):
                    gla_keys(n, t)
                    if t:
                        gla_outs(n, t - 1)
                gla_outs(n, TT - 1)

            for n in range(3):
                for j in range(12):
                    mix_prep(FIRST["gla", n] + j + 3)
                    rg_act(n, j)
                norm("rgo", n)
                gla_act(n)
                if n < 2:
                    norm("mix", n + 1)
                    later = [(FIRST["rg", n + 1] + j + 3) for j in range(8)]
                else:
                    norm("mem", 0)
                    later = [(FIRST["memk", 0] + j + 3) for j in range(16)]
                for j, t in enumerate(later):
                    mix_prep(t)
                    if j == 1:
                        gla_exp(n)
                    if j == 3:
                        gla_gate(n)
                gla(n)
                norm("glo", n)
                for j in range(8):
                    mix_prep(FIRST["out", n] + j + 3)

            def softmax(n, t):
                w = P if NPROMPT[n] > t * P else SAMPLE
                i = TT * n + t
                act.wait_ge(max_done, i + 1)
                if i >= 2:
                    full_wait(act, "pt", (i - 2) // TT, (i - 2) % TT, 1)
                for h in range(HEADS):
                    ins = nc.scalar.activation(pr[0:w, i % 2, h, :], bank("sc", n, t, h // 2)[0:w, (h % 2) * MEM:(h % 2 + 1) * MEM], ACT.Exp,
                                               bias=mx[0:w, i % 2, 1, h:h + 1], scale=1.0 / 16, accum_out=mx[0:w, i % 2, 2, h:h + 1])
                    if h % 2:
                        release(ins, "sc", n, t, h // 2)

            def out_hi(n, t):
                w = P if NPROMPT[n] > t * P else SAMPLE
                for q in range(2):
                    full_wait(act, "pt", n, t, q)
                    ins = nc.scalar.activation(pt[:, 4 * q:4 * q + 4, 0:w], bank("pt", n, t, q)[:, 0:4 * w].rearrange("p (a i) -> p a i", a=4), ACT.Copy)
                    release(ins, "pt", n, t, q)
                for q in range(2 if w == P else 1):
                    full_wait(act, "pv", n, t, q)
                    m = 4 if w == P else 8
                    nc.scalar.activation(mo_hi[:, 4 * q:4 * q + m, t * P:t * P + w],
                                         bank("pv", n, t, q)[:, 0:m * w].rearrange("p (a i) -> p a i", a=m), ACT.Copy).then_inc(ohi_done, 1)

            for n in range(3):
                norm("xan", n)
                for j in range(8):
                    mix_prep(FIRST["cq", n] + j + 3)
                for t in range(TT):
                    softmax(n, t)
                    if t:
                        out_hi(n, t - 1)
                out_hi(n, TT - 1)
                for j in range(8):
                    mix_prep(FIRST["co", n] + j + 3)

            for k in range(4):
                if k == 0:
                    act.wait_ge(tile_done, MIX_TILES)
                ffn_prep(1, 0, k)
            for n in range(3):
                norm("ffn2", n)
            ffn(1)
            for n in range(3):
                norm("fin", n)

        @block.vector
        def _(dve):
            chain = [0]

            def link(ins):
                chain[0] += 1
                ins.then_inc(dve_chain, 1)
                dve.wait_ge(dve_chain, chain[0])

            def norm_scale(kind, n):
                p = NORMS[kind, n]
                m = p.groups * p.T
                dve.wait_ge(sq_used, p.sq0 + p.groups * p.rows)
                width = P * p.rows
                ins = nc.vector.tensor_scalar(st[:, 0, 0:m], bank("st", kind, n)[:, 0:m], 1.0 / width, EPS, ALU.mult, ALU.add)
                release(ins, "st", kind, n)
                dve.wait_ge(root_done, p.index + 1)
                link(nc.vector.reciprocal(st[:, 2, 0:m], st[:, 1, 0:m]))

            def norm_diag(kind, n, g):
                p = NORMS[kind, n]
                d = p.diag0 + g
                if g >= 2:
                    full_wait(dve, "rb", kind, n, g - 2)
                nc.vector.tensor_tensor(diag[:, d % 2, 0:p.T, :], ident.rearrange("p (a i) -> p a i", a=1).to_broadcast([P, p.T, P]),
                                        st[:, 2, g * p.T:(g + 1) * p.T].rearrange("p (a i) -> p a i", i=1).to_broadcast([P, p.T, P]),
                                        ALU.mult).then_inc(diag_done, 1)

            def norm_rows(kind, n):
                p = NORMS[kind, n]
                N = p.N
                gain = {"rgo": V_RGO, "glo": V_GLO}.get(kind) or GAINS[kind]
                for half in range(p.groups * p.rows // 4):
                    for r in range(4):
                        row = 4 * half + r
                        g = row // p.rows
                        if row % p.rows == 0:
                            if g == 0:
                                norm_diag(kind, n, 0)
                            if g + 1 < p.groups:
                                norm_diag(kind, n, g + 1)
                            full_wait(dve, "rb", kind, n, g)
                        if kind == "fin" and half:
                            dve.wait_ge(y_stored, 16 * (2 * n + 1))
                        c = gain + (0 if kind == "glo" else row)
                        ins = nc.vector.scalar_tensor_tensor(out=sq[:, r, 0:N], in0=norm_source(kind, n, g, row % p.rows),
                                                             scalar=vec[:, c:c + 1], in1=bank("rb", kind, n, g)[:, 0:N],
                                                             op0=ALU.mult, op1=ALU.mult)
                        if row % p.rows == p.rows - 1:
                            release(ins, "rb", kind, n, g)
                            read_wait(dve, "rb", kind, n, g)
                        elif r == 3 and kind != "fin":
                            link(ins)
                        elif r == 3:
                            ins.then_inc(normed, 1)
                    if kind == "fin":
                        continue
                    src = sq[:, :, 0:N]
                    if kind == "glo":
                        dve.wait_ge(silug_done, n + 1)
                        link(nc.vector.tensor_tensor(src, src, gg[:, :, 0:N], ALU.mult))
                    rows = slice(4 * half, 4 * half + 4)
                    if kind == "rgo":
                        hi, lo = mo_hi[:, 0:4, 0:N], mo_lo[:, 0:4, 0:N]
                    elif kind == "glo":
                        hi, lo = mo_hi[:, 4:8, 0:N], mo_lo[:, 4:8, 0:N]
                    elif kind in ("ffn1", "ffn2"):
                        hi, lo = a_hi[:, rows, tokens(n)], a_lo[:, rows, tokens(n)]
                    else:
                        hi, lo = xn_hi[:, rows, 0:N], xn_lo[:, rows, 0:N]
                    link(nc.vector.tensor_copy(hi, src))
                    nc.vector.tensor_tensor(lo, src, hi.bitcast(F32), ALU.subtract).then_inc(normed, 1)
                    dve.wait_ge(normed, p.out0 + half + 1)

            def norm_wait_free(kind, n):
                if kind == "rgo" and n:
                    dve.wait_ge(tile_done, FIRST["out", n - 1] + 8)
                if kind == "mix" and n == 0:
                    dve.wait_ge(down_done, DOWNS)
                if kind == "mix" and n:
                    full_wait(dve, "low", n - 1)
                if kind == "mem":
                    full_wait(dve, "low", 2)
                if kind == "xan":
                    if n == 0:
                        dve.wait_ge(stored, 16 * 10)
                    else:
                        dve.wait_ge(tile_done, FIRST["cq", n - 1] + 8)

            def norm(kind, n):
                norm_scale(kind, n)
                norm_wait_free(kind, n)
                norm_rows(kind, n)

            def ffn(f):
                G, X, Q = f * GATE_UP_STEPS, f * DOWNS, 3 * KT

                def body(it, first):
                    q0 = 6 * it
                    for s in range(6):
                        ft, n = s // 3, s % 3
                        N = NS[n]
                        b = 4 + 2 * (s % 2)
                        dve.wait_ge(silu_done, G + q0 + s + 1)
                        if f or not first or s >= 2:
                            dve.wait_ge(hid_done, G + q0 + s - 1)
                        nc.vector.tensor_tensor(hf[:, s % 2, 0:N], sil[:, s % 2, 0:N], ps[:, b + 1, 0:N], ALU.mult).then_inc(h_done, 1)
                        if f or not first:
                            dve.wait_ge(down_done, X + Q * it - Q + KT * (n + 1))
                        dve.wait_ge(h_done, G + q0 + s + 1)
                        nc.vector.tensor_copy(h_hi[:, ft, tokens(n)], hf[:, s % 2, 0:N]).then_inc(hhi_done, 1)
                        dve.wait_ge(hhi_done, G + q0 + s + 1)
                        nc.vector.tensor_tensor(h_lo[:, ft, tokens(n)], hf[:, s % 2, 0:N], h_hi[:, ft, tokens(n)].bitcast(F32), ALU.subtract)\
                          .then_inc(hid_done, 1)
                    for n in range(3):
                        for m in range(KT):
                            d = X + Q * it + KT * n + m
                            dve.wait_ge(down_done, d + 1)
                            if f or not first:
                                dve.wait_ge(x_added, d - Q + 1)
                            nc.vector.scalar_tensor_tensor(out=x[:, m, tokens(n)], in0=ps[:, m % 4, 0:NS[n]], scalar=0.5,
                                                           in1=x[:, m, tokens(n)], op0=ALU.mult, op1=ALU.add).then_inc(x_added, 1)

                body(0, True)
                with dve.Fori(1, ITS) as it:
                    body(it, False)

            dve.wait_ge(lam_done, 1)
            nc.vector.tensor_scalar(rgc[:, 2, :], rgc[:, 1, :], 1.0, None, ALU.add).then_inc(lam_done, 1)
            dve.wait_ge(lam_done, 3)
            link(nc.vector.tensor_scalar(rgc[:, 4, :], rgc[:, 2, :], -1.0, None, ALU.add))
            link(nc.vector.tensor_scalar(rgc[:, 5, :], rgc[:, 4, :], 0.0, None, ALU.is_equal))
            link(nc.vector.tensor_tensor(rgc[:, 4, :], rgc[:, 4, :], rgc[:, 5, :], ALU.add))
            link(nc.vector.tensor_tensor(rgc[:, 3, :], rgc[:, 3, :], rgc[:, 5, :], ALU.add))
            link(nc.vector.reciprocal(rgc[:, 6, :], rgc[:, 4, :]))
            link(nc.vector.tensor_tensor(rgc[:, 3, :], rgc[:, 3, :], rgc[:, 6, :], ALU.mult))
            link(nc.vector.tensor_tensor(rgc[:, 3, :], rgc[:, 3, :], rgc[:, 1, :], ALU.mult))
            link(nc.vector.tensor_scalar(rgc[:, 4, :], vec[:, V_LAM:V_LAM + 4], -1.0, 0.0, ALU.mult, ALU.max))
            link(nc.vector.tensor_tensor(rgc[:, 3, :], rgc[:, 3, :], rgc[:, 4, :], ALU.add))
            link(nc.vector.tensor_scalar(rgc[:, 5, :], rgc[:, 3, :], 8.0, None, ALU.mult))
            nc.vector.tensor_scalar(rgc[:, 6, :], rgc[:, 3, :], -8.0, None, ALU.mult).then_inc(lam_done, 1)

            for n in range(3):
                norm("ffn1", n)
            ffn(0)

            def evict(kind, n, j):
                t = FIRST[kind, n] + j
                N = NS[n]
                dve.wait_ge(tile_done, t + 1)
                src = ps[:, t % RING, 0:N]
                if kind == "rg":
                    if j < 4:
                        np_ = NPROMPT[n]
                        if n == 2:
                            nc.vector.tensor_copy(xs[:, j, :, 3:3 + TS], ps[:, t % RING, np_:N].rearrange("p (b t) -> p b t", t=TS))
                        ins = nc.vector.tensor_copy(xbuf[:, j, 3:3 + np_], ps[:, t % RING, 0:np_])
                    else:
                        ins = nc.vector.tensor_copy(ybuf[:, j - 4, 0:N], src)
                elif kind == "gla":
                    dst = qk[:, j - 4, 0:N] if j < 8 else gg[:, j - 8, 0:N]
                    ins = nc.vector.tensor_copy(dst, src)
                elif kind == "memk":
                    ins = nc.vector.tensor_copy(kmem[:, j, :], ps[:, t % RING, 0:MEM])
                elif kind == "cq":
                    ins = nc.vector.tensor_copy(qa[:, j, 0:N], src)
                else:
                    ins = nc.vector.tensor_tensor(x[:, j, tokens(n)], x[:, j, tokens(n)], src, ALU.add)
                ins.then_inc(evicted, 1)

            def evict_values(n):
                t = FIRST["gla", n]
                dve.wait_ge(tile_done, t + 4)
                for i in range(TT):
                    w = min(P, NS[n] - i * P)
                    if w < P:
                        nc.vector.memset(vt[w:P, i, :], 0.0)
                    ins = nc.vector.tensor_copy(vt[0:w, i, :], ps[0:w, i, :])
                ins.then_inc(evicted, 4)

            def rg_conv(n):
                np_, N = NPROMPT[n], NS[n]
                dve.wait_ge(evicted, FIRST["rg", n] + 4)
                if n == 2:
                    dve.wait_ge(state_in, 16 * 4)
                for tap in range(4):
                    for j in range(4):
                        w = vec[:, V_CW + 4 * tap + j:V_CW + 4 * tap + j + 1]
                        parts = [(xc[:, j, 0:np_], xbuf[:, j, tap:tap + np_])]
                        if n == 2:
                            parts.append((xc[:, j, np_:N].rearrange("p (b t) -> p b t", t=TS), xs[:, j, :, tap:tap + TS]))
                        for dst, src in parts:
                            if tap == 0:
                                ins = nc.vector.tensor_scalar(dst, src, w, vec[:, V_CB + j:V_CB + j + 1], ALU.mult, ALU.add)
                            else:
                                ins = nc.vector.scalar_tensor_tensor(out=dst, in0=src, scalar=w, in1=dst, op0=ALU.mult, op1=ALU.add)
                    if tap < 3:
                        link(ins)
                ins.then_inc(conv_done, 1)
                if n < 2:
                    dve.wait_ge(conv_done, n + 1)
                    link(nc.vector.tensor_copy(xbuf[:, :, 0:3], xbuf[:, :, np_:np_ + 3]))

            def rg_vec(n, j):
                N, np_ = NS[n], NPROMPT[n]
                if j == 7:
                    dve.wait_ge(decay_done, n + 1)
                    link(nc.vector.tensor_tensor(I[:, :, 0:N], I[:, :, 0:N], xc[:, :, 0:N], ALU.mult))
                    link(nc.vector.tensor_tensor(xc[:, :, 0:N], R[:, :, 0:N], R[:, :, 0:N], ALU.mult))
                    nc.vector.scalar_tensor_tensor(out=T_[:, :, 0:N], in0=xc[:, :, 0:N], scalar=1.0, in1=T_[:, :, 0:N],
                                                   op0=ALU.add, op1=ALU.mult).then_inc(mult_ready, 1)
                if j == 9:
                    dve.wait_ge(root_mult, n + 1)
                    link(nc.vector.tensor_tensor(I[:, :, 0:N], I[:, :, 0:N], T_[:, :, 0:N], ALU.mult))
                    if n == 2:
                        starts_a = R[:, :, np_:N].rearrange("p j (b t) -> p j b t", t=TS)[:, :, :, 0]
                        starts_u = I[:, :, np_:N].rearrange("p j (b t) -> p j b t", t=TS)[:, :, :, 0]
                        link(nc.vector.tensor_tensor(h0a[:, :, :], starts_a, h0[:, :, :], ALU.mult))
                        link(nc.vector.tensor_tensor(starts_u, starts_u, h0a[:, :, :], ALU.add))
                        link(nc.vector.memset(starts_a, 0.0))
                    for i in range(4):
                        init = 0.0 if n == 0 else hcar[:, i, :]
                        ins = nc.vector.tensor_tensor_scan(xc[:, i, 0:N], R[:, i, 0:N], I[:, i, 0:N], init, ALU.mult, ALU.add)
                    link(ins)
                    if n < 2:
                        nc.vector.tensor_copy(hcar[:, :, :], xc[:, :, N - 1:N])
                    else:
                        nc.vector.tensor_copy(hlast[:, :, 0:1], xc[:, :, np_ - 1:np_])
                        nc.vector.tensor_copy(hlast[:, :, 1:], xc[:, :, np_ + TS - 1:N:TS])
                if j == 10:
                    dve.wait_ge(y_done, n + 1)
                    nc.vector.tensor_tensor(I[:, :, 0:N], xc[:, :, 0:N], ybuf[:, :, 0:N], ALU.mult).then_inc(rg_out, 1)

            def z_vec(n):
                N = NS[n]
                full_wait(dve, "low", n)
                ins = nc.vector.tensor_copy(al[:, 0:N], bank("low", n)[0:RANK, 0:N])
                release(ins, "low", n)
                for j in range(2):
                    full_wait(dve, "z", n, j)
                    ins = nc.vector.tensor_scalar(Z[:, j, 0:N], bank("z", n, j)[:, 0:N], vec[:, V_BA2 + j:V_BA2 + j + 1], None, ALU.add)
                    release(ins, "z", n, j)

            def blocks(ap, lo, hi, c):
                return ap[:, :, lo:hi].rearrange("p j (b t) -> p j b t", t=c)

            def gla_cumsum(n):
                N, np_ = NS[n], NPROMPT[n]
                dve.wait_ge(soft_done, n + 1)
                link(nc.vector.scalar_tensor_tensor(out=Z[:, :, 0:N], in0=Z[:, :, 0:N], scalar=0.0, in1=E_[:, :, 0:N],
                                                    op0=ALU.min, op1=ALU.subtract))
                mask = mixc(C_SCAN2, N) if n == 2 else mixc(C_SCAN, N)
                for j in range(2):
                    ins = nc.vector.tensor_tensor_scan(B[:, j, 0:N], mask, Z[:, j, 0:N], 0.0, ALU.mult, ALU.add)
                ins.then_inc(b_out, 1)
                dve.wait_ge(b_out, n + 1)
                for lo, hi, c in [(0, np_, CH)] + ([(np_, N, TS)] if n == 2 else []):
                    for j in range(2):
                        bb = B[:, j, lo:hi].rearrange("p (b t) -> p b t", t=c)
                        ins = nc.vector.tensor_tensor(Z[:, j, lo:hi].rearrange("p (b t) -> p b t", t=c),
                                                      bb[:, :, c - 1:c].to_broadcast([P, (hi - lo) // c, c]), bb, ALU.subtract)
                ins.then_inc(db_out, 1)

            def gla_scaled(n):
                N = NS[n]
                dve.wait_ge(edb_done, n + 1)
                dve.wait_ge(evicted, FIRST["gla", n] + 8)
                link(nc.vector.tensor_tensor(kd[:, :, 0:N], qk[:, 2:4, 0:N], Z[:, :, 0:N], ALU.mult))
                nc.vector.tensor_tensor(qk[:, 2:4, 0:N], qk[:, 2:4, 0:N], E_[:, :, 0:N], ALU.mult)
                nc.vector.scalar_tensor_tensor(out=qk[:, 0:2, 0:N], in0=qk[:, 0:2, 0:N], scalar=0.125, in1=B[:, :, 0:N],
                                               op0=ALU.mult, op1=ALU.mult).then_inc(qk_out, 1)

            def gla_scores(n, t):
                i = TT * n + t
                prompt = NPROMPT[n] > t * P
                w = P if prompt else SAMPLE
                mask = (mixc(C_M32, P) if prompt else mixc(C_M8, SAMPLE))[0:w, :].rearrange("p (a i) -> p a i", a=1).to_broadcast([w, 2, w])
                for e in range(2):
                    full_wait(dve, "at", n, t, e)
                    if i >= 2:
                        full_wait(dve, "o", (i - 2) // TT, (i - 2) % TT, e)
                    if w < P:
                        nc.vector.memset(AT[w:P, i % 2, 2 * e:2 * e + 2, 0:w], 0.0)
                    ins = nc.vector.tensor_tensor(AT[0:w, i % 2, 2 * e:2 * e + 2, 0:w],
                                                  bank("at", n, t, e)[0:w, 0:2 * w].rearrange("p (a i) -> p a i", a=2), mask, ALU.mult)
                    release(ins, "at", n, t, e)

            def gla_states(n, t):
                tile = TT * n + t
                for c in range(P // CH):
                    g = 4 * tile + c
                    full_wait(dve, "kv", n, t, c)
                    if g + 1 >= 8:
                        old = (g + 1 - 8) // 4
                        full_wait(dve, "o", old // TT, old % TT, 1)
                    for p in range(2):
                        for e in range(2):
                            rows = slice(64 * e, 64 * e + 64)
                            col = t * P + (c + 1) * CH - 1
                            ins = nc.vector.scalar_tensor_tensor(
                                out=S[rows, (g + 1) % 8, p, :], in0=S[rows, g % 8, p, :], scalar=B[rows, p, col:col + 1],
                                in1=bank("kv", n, t, c)[rows, (2 * p + e) * P:(2 * p + e + 1) * P], op0=ALU.mult, op1=ALU.add)
                    release(ins, "kv", n, t, c)
                    read_wait(dve, "kv", n, t, c)

            def gla_sample_keys():
                read_wait(dve, "kdt", 2, 2)
                dve.wait_ge(tile_done, FIRST["memv", 0] + 8)
                for b in range(NSEQ):
                    ins = nc.vector.tensor_scalar(kdm[0:SAMPLE, b, :], kdt[0:SAMPLE, 2, :], mixc(C_ROW, 8)[0:SAMPLE, b:b + 1], None, ALU.mult)
                ins.then_inc(kdm_done, 1)

            def gla_sample_states():
                for b in range(NSEQ):
                    full_wait(dve, "kvs", b)
                    for p in range(2):
                        for e in range(2):
                            rows = slice(64 * e, 64 * e + 64)
                            col = NPROMPT[2] + TS * b + TS - 1
                            ins = nc.vector.scalar_tensor_tensor(
                                out=s0[rows, b, p, :], in0=s0[rows, b, p, :], scalar=B[rows, p, col:col + 1],
                                in1=bank("kvs", b)[rows, (2 * p + e) * P:(2 * p + e + 1) * P], op0=ALU.mult, op1=ALU.add)
                    release(ins, "kvs", b)

            def gla(n):
                for t in range(TT):
                    gla_scores(n, t)
                    if NPROMPT[n] > t * P:
                        gla_states(n, t)
                if n == 2:
                    gla_sample_keys()
                    gla_sample_states()

            norm("mix", 0)
            dve.wait_ge(down_done, DOWNS)
            nc.vector.memset(S[:, 0, :, :], 0.0)
            link(nc.vector.memset(xbuf[:, :, 0:3], 0.0))
            for j in range(8):
                evict("rg", 0, j)
            dve.wait_ge(wal_done, 1)
            nc.vector.tensor_tensor(w_al_lo[:, :, :], R[:, 0, 0:KT * RANK].rearrange("p (k r) -> p k r", k=KT),
                                    w_al_hi[:, :, :].bitcast(F32), ALU.subtract).then_inc(wal_done, 1)
            for n in range(3):
                rg_conv(n)
                evict_values(n)
                for j in range(4, 12):
                    evict("gla", n, j)
                    rg_vec(n, j)
                z_vec(n)
                norm("rgo", n)
                if n < 2:
                    norm("mix", n + 1)
                    gla_cumsum(n)
                    for j in range(8):
                        evict("rg", n + 1, j)
                        if j == 4:
                            gla_scaled(n)
                else:
                    norm("mem", 0)
                    gla_cumsum(n)
                    for j in range(8):
                        if j == 0:
                            dve.wait_ge(stored, 16 * 6)
                        evict("memk", 0, j)
                        if j == 4:
                            gla_scaled(n)
                    for half in range(2):
                        t = FIRST["memv", 0] + 4 * half
                        dve.wait_ge(tile_done, t + 4)
                        for i in range(2):
                            ins = nc.vector.tensor_copy(vmem[:, i, 512 * half:512 * half + 512], ps[:, i, :])
                        ins.then_inc(evicted, 4)
                gla(n)
                norm("glo", n)
                for j in range(8):
                    evict("out", n, j)

            def row_max(n, t):
                w = P if NPROMPT[n] > t * P else SAMPLE
                i = TT * n + t
                for q in range(2):
                    full_wait(dve, "sc", n, t, q)
                    ins = nc.vector.tensor_reduce(mx[0:w, i % 2, 0, 2 * q:2 * q + 2],
                                                  bank("sc", n, t, q)[0:w, :].rearrange("p (a m) -> p a m", a=2), AX.X, ALU.max)
                link(ins)
                nc.vector.tensor_scalar(mx[0:w, i % 2, 1, :], mx[0:w, i % 2, 0, :], -1.0 / 16, None, ALU.mult).then_inc(max_done, 1)

            def normalise(n, t):
                w = P if NPROMPT[n] > t * P else SAMPLE
                i = TT * n + t
                for q in range(2):
                    read_wait(dve, "sc", n, t, q)
                link(nc.vector.reciprocal(mx[0:w, i % 2, 3, :], mx[0:w, i % 2, 2, :]))
                for h in range(HEADS):
                    ins = nc.vector.tensor_scalar(pr[0:w, i % 2, h, :], pr[0:w, i % 2, h, :], mx[0:w, i % 2, 3, h:h + 1], None, ALU.mult)
                ins.then_inc(pr_done, 1)

            def out_lo(n, t):
                w = P if NPROMPT[n] > t * P else SAMPLE
                m = 4 if w == P else 8
                for q in range(2 if w == P else 1):
                    dve.wait_ge(ohi_done, 2 * (TT * n + t) + q + 1)
                    ins = nc.vector.tensor_tensor(mo_lo[:, 4 * q:4 * q + m, t * P:t * P + w],
                                                  bank("pv", n, t, q)[:, 0:m * w].rearrange("p (a i) -> p a i", a=m),
                                                  mo_hi[:, 4 * q:4 * q + m, t * P:t * P + w].bitcast(F32), ALU.subtract)
                    release(ins, "pv", n, t, q)

            def sample_queries():
                dve.wait_ge(evicted, FIRST["cq", 2] + 8)
                link(nc.vector.memset(qm[:, :, :, :], 0.0))
                for b in range(NSEQ):
                    if b >= 2:
                        dve.wait_ge(ss_done, b - 1)
                        link(nc.vector.memset(qm[:, b % 2, :, TS * (b - 2):TS * (b - 1)], 0.0))
                    c = NPROMPT[2] + TS * b
                    nc.vector.tensor_copy(qm[:, b % 2, :, TS * b:TS * b + TS], qa[:, :, c:c + TS]).then_inc(qm_done, 1)

            for n in range(3):
                norm("xan", n)
                for j in range(8):
                    evict("cq", n, j)
                for t in range(TT):
                    if n == 2 and t == 2:
                        sample_queries()
                    row_max(n, t)
                    normalise(n, t)
                    if t:
                        out_lo(n, t - 1)
                out_lo(n, TT - 1)
                for j in range(8):
                    evict("co", n, j)

            for n in range(3):
                if n == 0:
                    dve.wait_ge(evicted, MIX_TILES)
                norm("ffn2", n)
            ffn(1)
            for n in range(3):
                norm("fin", n)

        @block.tensor
        def _(pe):
            def split_mm(dst, w_h, w_l, x_h, x_l, start, stop):
                nc.tensor.matmul(dst, w_h, x_h, start=start, stop=False)
                nc.tensor.matmul(dst, w_h, x_l, start=False, stop=False)
                return nc.tensor.matmul(dst, w_l, x_h, start=False, stop=stop)

            def norm(kind, n):
                p = NORMS[kind, n]
                fill_wait(pe, "st", kind, n)
                dst = bank("st", kind, n)
                for i in range(p.groups * p.rows):
                    g = i // p.rows
                    pe.wait_ge(squared, p.sq0 + i + 1)
                    for t in range(p.T):
                        c = min(t * P, p.N - P)
                        ins = nc.tensor.matmul(dst[:, g * p.T + t:g * p.T + t + 1], sq[:, (p.sq0 + i) % 4, c:c + P], ones[:, 0:1],
                                               start=(i == 0 and t == 0), stop=(i % p.rows == p.rows - 1), skip_group_check=True)
                    ins.then_inc(sq_used, 1)
                for g in range(p.groups):
                    fill_wait(pe, "rb", kind, n, g)
                    pe.wait_ge(diag_done, p.diag0 + g + 1)
                    d = diag[:, (p.diag0 + g) % 2, :, :].rearrange("p a i -> p (a i)")
                    whole = p.N // P * P
                    ins = nc.tensor.matmul(bank("rb", kind, n, g)[:, 0:whole], ones, d[:, 0:whole], start=True, stop=True)
                    if whole < p.N:
                        ins = nc.tensor.matmul(bank("rb", kind, n, g)[:, whole:p.N], ones, d[:, whole + P - (p.N - whole):whole + P], start=True, stop=True)
                    filled(ins, "rb", kind, n, g)

            def ffn(f):
                T0 = f * (FFN_TILES + MIX_TILES)
                G, X, Q = f * GATE_UP_STEPS, f * DOWNS, 3 * KT

                def body(it, first):
                    for s in range(6):
                        ft, n = s // 3, s % 3
                        if n == 0:
                            pe.wait_ge(w_lo, T0 + 6 * it + 2 * ft + 2)
                        if f or not first or s >= 2:
                            pe.wait_ge(h_done, G + 6 * it + s - 1)
                        for u in range(2):
                            w = 2 * ft + u
                            for k in range(KT):
                                c = slice(k * P, k * P + P)
                                ins = split_mm(ps[:, 4 + 2 * (s % 2) + u, 0:NS[n]], w_hi_sb[:, w, c], w_lo_sb[:, w, c],
                                               a_hi[:, k, tokens(n)], a_lo[:, k, tokens(n)], k == 0, k == KT - 1)
                        ins.then_inc(gu_done, 1)
                    pe.wait_ge(w_lo, T0 + 6 * it + 6)
                    for n in range(3):
                        pe.wait_ge(hid_done, G + 6 * it + 3 + n + 1)
                        for m in range(KT):
                            if f or not first or KT * n + m >= 4:
                                pe.wait_ge(x_added, X + Q * it + KT * n + m - 3)
                            c = slice(m * P, m * P + P)
                            for ft in range(2):
                                ins = split_mm(ps[:, m % 4, 0:NS[n]], w_hi_sb[:, 4 + ft, c], w_lo_sb[:, 4 + ft, c],
                                               h_hi[:, ft, tokens(n)], h_lo[:, ft, tokens(n)], ft == 0, ft == 1)
                            ins.then_inc(down_done, 1)

                body(0, True)
                with pe.Fori(1, ITS) as it:
                    body(it, False)

            def tiles(first, groups, hi, lo, N):
                def group(t):
                    for k4 in range(RING):
                        pe.wait_ge(w_lo, t + FFN_TILES + k4 + 1)
                        if not (first < 4 and isinstance(t, int) and t < 4):
                            pe.wait_ge(evicted, t + k4 - 3)
                        for k in range(KT):
                            c = slice(k * P, k * P + P)
                            ins = split_mm(ps[:, k4, 0:N], w_hi_sb[:, k4, c], w_lo_sb[:, k4, c], hi[:, k, 0:N], lo[:, k, 0:N],
                                           k == 0, k == KT - 1)
                        ins.then_inc(tile_done, 1)
                if first < 4:
                    for g in range(groups):
                        group(first + RING * g)
                else:
                    with pe.Fori(0, groups) as g:
                        group(first + RING * g)

            def token_tiles(first, hi, lo, N):
                pe.wait_ge(evicted, first)
                for k4 in range(4):
                    pe.wait_ge(w_lo, FFN_TILES + first + k4 + 1)
                    for kk in range(2):
                        k = 2 * k4 + kk
                        c = slice(kk * 512, kk * 512 + 512)
                        for i in range((N + P - 1) // P):
                            r = slice(i * P, min(N, i * P + P))
                            w = r.stop - r.start
                            nc.tensor.matmul(ps[0:w, i, :], hi[:, k, r], w_hi_sb[:, k4, c], start=(k == 0), stop=False)
                            nc.tensor.matmul(ps[0:w, i, :], lo[:, k, r], w_hi_sb[:, k4, c], start=False, stop=False)
                            ins = nc.tensor.matmul(ps[0:w, i, :], hi[:, k, r], w_lo_sb[:, k4, c], start=False, stop=(k == KT - 1))
                    ins.then_inc(tile_done, 1)

            def gates(n):
                N = NS[n]
                pe.wait_ge(conv_done, n + 1)
                for j in range(8):
                    fill_wait(pe, "gate", n, j)
                    filled(nc.tensor.matmul(bank("gate", n, j)[:, 0:N], bd[:, j, :], xc[:, j % 4, 0:N], start=True, stop=True), "gate", n, j)

            def decay_logits(n):
                N = NS[n]
                if n == 0:
                    pe.wait_ge(wal_done, 2)
                fill_wait(pe, "low", n)
                for k in range(KT):
                    ins = split_mm(bank("low", n)[0:RANK, 0:N], w_al_hi[:, k, :], w_al_lo[:, k, :], xn_hi[:, k, 0:N], xn_lo[:, k, 0:N],
                                   k == 0, k == KT - 1)
                filled(ins, "low", n)
                read_wait(pe, "low", n)
                for j in range(2):
                    fill_wait(pe, "z", n, j)
                    filled(nc.tensor.matmul(bank("z", n, j)[:, 0:N], w_a2[:, j * P:j * P + P], al[:, 0:N], start=True, stop=True), "z", n, j)

            def gla_a(n, t):
                prompt = NPROMPT[n] > t * P
                w = P if prompt else SAMPLE
                cols = slice(t * P, t * P + w)
                if t == 0:
                    pe.wait_ge(qk_out, n + 1)
                fill_wait(pe, "kdt", n, t)
                for p in range(2):
                    ins = nc.tensor.transpose(bank("kdt", n, t)[0:w, p * P:p * P + P], kd[:, p, cols], ident)
                filled(ins, "kdt", n, t)
                for e in range(2):
                    rows = slice(64 * e, 64 * e + 64)
                    fill_wait(pe, "at", n, t, e)
                    for p in range(2):
                        ins = nc.tensor.matmul(bank("at", n, t, e)[0:w, p * w:p * w + w], qk[rows, 2 + p, cols], qk[rows, p, cols],
                                               start=True, stop=True)
                    filled(ins, "at", n, t, e)
                if prompt:
                    read_wait(pe, "kdt", n, t)
                    for c in range(P // CH):
                        rows = slice(c * CH, c * CH + CH)
                        fill_wait(pe, "kv", n, t, c)
                        for p in range(2):
                            ins = nc.tensor.matmul(bank("kv", n, t, c)[:, 2 * p * P:2 * (p + 1) * P], kdt[rows, t, p * P:p * P + P],
                                                   vt[rows, t, 2 * p * P:2 * (p + 1) * P], start=True, stop=True)
                        filled(ins, "kv", n, t, c)

            def gla_b(n, t):
                prompt = NPROMPT[n] > t * P
                w = P if prompt else SAMPLE
                tile = TT * n + t
                for e in range(2):
                    rows = slice(64 * e, 64 * e + 64)
                    fill_wait(pe, "o", n, t, e)
                    read_wait(pe, "at", n, t, e)
                    if prompt:
                        read_wait(pe, "kv", n, t, 2)
                    else:
                        pe.wait_ge(s0_in, 16)
                    dst = bank("o", n, t, e)
                    for p in range(2):
                        h = 2 * p + e
                        nc.tensor.matmul(dst[:, p * P:p * P + w], vt[:, t, h * P:h * P + P], AT[:, tile % 2, 2 * e + p, 0:w],
                                         start=True, stop=False)
                        if prompt:
                            for c in range(P // CH):
                                s = slice(t * P + c * CH, t * P + (c + 1) * CH)
                                ins = nc.tensor.matmul(dst[:, p * P + c * CH:p * P + (c + 1) * CH], S[rows, (4 * tile + c) % 8, p, :],
                                                       qk[rows, p, s], start=False, stop=(c == P // CH - 1))
                        else:
                            for b in range(NSEQ):
                                s = slice(t * P + TS * b, t * P + TS * b + TS)
                                ins = nc.tensor.matmul(dst[:, p * P + TS * b:p * P + TS * b + TS], s0[rows, b, p, :],
                                                       qk[rows, p, s], start=False, stop=(b == NSEQ - 1))
                    filled(ins, "o", n, t, e)
                if not prompt:
                    pe.wait_ge(kdm_done, 1)
                    for b in range(NSEQ):
                        fill_wait(pe, "kvs", b)
                        for p in range(2):
                            ins = nc.tensor.matmul(bank("kvs", b)[:, 2 * p * P:2 * (p + 1) * P], kdm[0:SAMPLE, b, p * P:p * P + P],
                                                   vt[0:SAMPLE, 2, 2 * p * P:2 * (p + 1) * P], start=True, stop=True)
                        filled(ins, "kvs", b)

            pe.wait_ge(const_in, 32)
            for n in range(3):
                norm("ffn1", n)
            pe.wait_ge(normed, NORMS["ffn1", 2].out0 + 2)
            ffn(0)

            pe.wait_ge(h_done, GATE_UP_STEPS)
            norm("mix", 0)
            pe.wait_ge(normed, NORMS["mix", 0].out0 + 2)
            pe.wait_ge(x_added, DOWNS)
            tiles(FIRST["rg", 0], 2, xn_hi, xn_lo, NS[0])
            for n in range(3):
                token_tiles(FIRST["gla", n], xn_hi, xn_lo, NS[n])
                gates(n)
                tiles(FIRST["gla", n] + 4, 2, xn_hi, xn_lo, NS[n])
                decay_logits(n)
                norm("rgo", n)
                if n < 2:
                    norm("mix", n + 1)
                    pe.wait_ge(normed, NORMS["mix", n + 1].out0 + 2)
                    tiles(FIRST["rg", n + 1], 2, xn_hi, xn_lo, NS[n + 1])
                else:
                    norm("mem", 0)
                    pe.wait_ge(normed, NORMS["mem", 0].out0 + 2)
                    tiles(FIRST["memk", 0], 2, xn_hi, xn_lo, MEM)
                    for half in range(2):
                        token_tiles(FIRST["memv", 0] + 4 * half, xn_hi, xn_lo, MEM)
                for t in range(TT):
                    gla_a(n, t)
                    if t:
                        gla_b(n, t - 1)
                gla_b(n, TT - 1)
                norm("glo", n)
                pe.wait_ge(normed, NORMS["glo", n].out0 + 1)
                tiles(FIRST["out", n], 2, mo_hi, mo_lo, NS[n])

            def scores(n, t):
                i = TT * n + t
                if t == 0:
                    pe.wait_ge(evicted, FIRST["cq", n] + 8)
                for q in range(2):
                    fill_wait(pe, "sc", n, t, q)
                if NPROMPT[n] > t * P:
                    for q in range(2):
                        for hh in range(2):
                            for dc in range(2):
                                f = 2 * (2 * q + hh) + dc
                                ins = nc.tensor.matmul(bank("sc", n, t, q)[:, hh * MEM:(hh + 1) * MEM], qa[:, f, t * P:t * P + P], kmem[:, f, :],
                                                       start=(dc == 0), stop=(dc == 1))
                        filled(ins, "sc", n, t, q)
                    return
                for b in range(NSEQ):
                    pe.wait_ge(qm_done, b + 1)
                    pe.wait_ge(kc_in[b % 3], 16 * (b // 3 + 1))
                    for f in range(KT):
                        q, hh, dc = f // 4, f // 2 % 2, f % 2
                        ins = nc.tensor.matmul(bank("sc", n, t, q)[0:SAMPLE, hh * MEM:(hh + 1) * MEM], qm[:, b % 2, f, :],
                                               kc[:, b % 3, f * MEM:(f + 1) * MEM], start=(b == 0 and hh == 0 and dc == 0),
                                               stop=(b == NSEQ - 1 and dc == 1), skip_group_check=True)
                        if b == NSEQ - 1 and f == 3:
                            filled(ins, "sc", n, t, 0)
                    if b < NSEQ - 1:
                        ins.then_inc(ss_done, 1)
                    else:
                        filled(ins, "sc", n, t, 1)

            def attend(n, t):
                prompt = NPROMPT[n] > t * P
                w = P if prompt else SAMPLE
                i = TT * n + t
                pe.wait_ge(pr_done, i + 1)
                for q in range(2):
                    fill_wait(pe, "pt", n, t, q)
                    for r in range(4):
                        h, mc = 2 * q + r // 2, r % 2
                        ins = nc.tensor.transpose(bank("pt", n, t, q)[:, r * w:r * w + w], pr[0:w, i % 2, h, mc * P:mc * P + P], ident[0:w, 0:w])
                    filled(ins, "pt", n, t, q)
                for q in range(2):
                    read_wait(pe, "pt", n, t, q)
                if prompt:
                    for q in range(2):
                        fill_wait(pe, "pv", n, t, q)
                        for r in range(4):
                            h, dc = 2 * q + r // 2, r % 2
                            for mc in range(2):
                                c = h * 2 * P + dc * P
                                ins = nc.tensor.matmul(bank("pv", n, t, q)[:, r * P:r * P + P], vmem[:, mc, c:c + P], pt[:, 2 * h + mc, :],
                                                       start=(mc == 0), stop=(mc == 1))
                        filled(ins, "pv", n, t, q)
                    return
                fill_wait(pe, "pv", n, t, 0)
                for b in range(NSEQ):
                    kb = NSEQ + b
                    pe.wait_ge(kc_in[kb % 3], 16 * (kb // 3 + 1))
                    for f in range(KT):
                        for mc in range(2):
                            ins = nc.tensor.matmul(bank("pv", n, t, 0)[:, f * SAMPLE + TS * b:f * SAMPLE + TS * b + TS],
                                                   kc[:, kb % 3, mc * D + f * P:mc * D + f * P + P],
                                                   pt[:, 2 * (f // 2) + mc, TS * b:TS * b + TS],
                                                   start=(b == 0 and f == 0 and mc == 0), stop=(mc == 1), skip_group_check=True)
                    if b < NSEQ - 1:
                        ins.then_inc(sv_done, 1)
                filled(ins, "pv", n, t, 0)

            for n in range(3):
                norm("xan", n)
                pe.wait_ge(normed, NORMS["xan", n].out0 + 2)
                tiles(FIRST["cq", n], 2, xn_hi, xn_lo, NS[n])
                for t in range(TT):
                    scores(n, t)
                    if t:
                        attend(n, t - 1)
                attend(n, TT - 1)
                for t in range(TT):
                    for q in range(2 if NPROMPT[n] > t * P else 1):
                        read_wait(pe, "pv", n, t, q)
                tiles(FIRST["co", n], 2, mo_hi, mo_lo, NS[n])

            for n in range(3):
                norm("ffn2", n)
            pe.wait_ge(normed, NORMS["ffn2", 2].out0 + 2)
            ffn(1)
            pe.wait_ge(h_done, 2 * GATE_UP_STEPS)
            for n in range(3):
                norm("fin", n)


_OUTS = {"y": (D, TOK), "mem_k": (P, KT, MEM), "mem_v": (P, 2, D), "conv_p": (P, 4, 3), "h": (P, 4, 1 + NSEQ), "s_p": (P, 2, P),
         "conv_s": (P, 4, NSEQ, 3), "s_s": (P, NSEQ, 2, P)}


def kernel(**inputs):
    import numpy as np
    import concourse.bacc as bacc
    from concourse.bass_utils import run_bass_kernel_spmd

    i = {k: np.asarray(v) for k, v in inputs.items()}
    f32 = np.float32

    def tiles(w):
        return w.reshape(KT, P, -1, P).transpose(2, 1, 0, 3).reshape(-1, P, D)

    def wide(w):
        h = w.shape[1] // 512
        return w.reshape(4, 2, P, h, 512).transpose(3, 0, 2, 1, 4).reshape(4 * h, P, D)

    def cols(v):
        return v.reshape(-1, P).T

    w_in = i["w_in"]
    rg, q, k, v, g, low = np.split(w_in, [1024, 1280, 1536, 2048, 2560], axis=1)
    mix_tiles = np.concatenate([tiles(rg), wide(v), tiles(q), tiles(k), tiles(g), tiles(i["w_out"]), tiles(i["w_ck"]), wide(i["w_cv"]),
                                tiles(i["w_cq"]), tiles(i["w_co"])])
    vectors = np.concatenate([cols(i["ffn1_norm"]), cols(i["mix_norm"]), cols(i["mem_norm"]), cols(i["xattn_norm"]), cols(i["ffn2_norm"]),
                              cols(i["final_norm"]), cols(i["rg_out_norm"]), cols(i["gla_out_norm"]),
                              i["conv_w"].reshape(4, 4, P).transpose(2, 0, 1).reshape(P, 16), cols(i["conv_b"]),
                              cols(i["rg_b_a"].reshape(-1)), cols(i["rg_b_x"].reshape(-1)), cols(i["rg_lambda"]), cols(i["gla_b_a2"])], axis=1)

    gates = np.zeros((P, 8, P), f32)
    for j in range(4):
        for h in range(2):
            s = slice(64 * h, 64 * h + 64)
            gates[s, j, s] = i["rg_w_a"][2 * j + h]
            gates[s, 4 + j, s] = i["rg_w_x"][2 * j + h]

    consts = np.zeros((P, NCONST), f32)
    r, c = np.arange(P)[:, None], np.arange(P)[None, :]
    consts[:, C_ONES:C_ONES + P] = 1
    consts[:, C_ID:C_ID + P] = r == c
    consts[:, C_ROW:C_ROW + NSEQ] = r // TS == np.arange(NSEQ)
    consts[:, C_M32:C_M32 + P] = (r // CH == c // CH) & (r <= c)
    consts[:, C_M8:C_M8 + SAMPLE] = ((r // TS == c // TS) & (r <= c))[:, 0:SAMPLE]
    consts[:, C_SCAN:C_SCAN + NMAX] = np.arange(NMAX) % CH != 0
    t = np.arange(NS[2])
    consts[:, C_SCAN2:C_SCAN2 + NS[2]] = np.where(t < NPROMPT[2], t % CH != 0, t % TS != 0)

    def heads(s):
        return s.reshape(-1, 2, 2, 64, P).transpose(2, 3, 0, 1, 4).reshape(P, -1, 2, P)

    given = {
        "x": np.concatenate([i["x_prompt"].reshape(SEQ, D), i["x_sample"].reshape(SAMPLE, D)]).T,
        "consts": consts, "vectors": vectors, "gates": gates, "mix_tiles": mix_tiles,
        "w_alow": low.reshape(KT, P, RANK).transpose(1, 0, 2).reshape(P, KT * RANK), "w_a2": i["gla_w_a2"],
        "mem": i["mem_prompt"].reshape(MEM, D).T,
        "conv0": i["state_conv"].reshape(NSEQ, 3, 4, P).transpose(3, 2, 0, 1),
        "h0": i["state_rglru"].reshape(NSEQ, 4, P).transpose(2, 1, 0),
        "s0": heads(i["state_gla"]),
        "cache_k": i["cache_mem_k"].reshape(NSEQ, MEM, KT, P).transpose(0, 3, 2, 1).reshape(NSEQ, P, 2 * D),
        "cache_v": i["cache_mem_v"].reshape(NSEQ, 2, P, D).transpose(0, 2, 1, 3).reshape(NSEQ, P, 2 * D),
    }
    for f in (1, 2):
        given[f"ffn{f}_gate"] = tiles(i[f"ffn{f}_w_gate"])
        given[f"ffn{f}_up"] = tiles(i[f"ffn{f}_w_up"])
        given[f"ffn{f}_down"] = i[f"ffn{f}_w_down"].reshape(FT, P, D)

    nc = bacc.Bacc("TRN2", target_bir_lowering=False, num_devices=1)
    arrays, a, out = {}, {}, {}
    for name, v in given.items():
        arrays[f"in_{name}"] = np.ascontiguousarray(v)
        a[name] = nc.dram_tensor(f"in_{name}", v.shape, mybir.dt.from_np(v.dtype), kind="ExternalInput").ap()
    for name, shape in _OUTS.items():
        out[name] = nc.dram_tensor(f"out_{name}", shape, F32, kind="ExternalOutput").ap()
    program(nc, a, out)
    r = run_bass_kernel_spmd(nc, [arrays], core_ids=[0])
    o = {name: r.results[0][f"out_{name}"] for name in _OUTS}

    y = o["y"].T
    s_p, s_s = o["s_p"].reshape(P, 1, 2, P), o["s_s"]

    def unheads(s):
        return s.reshape(2, 64, -1, 2, P).transpose(2, 3, 0, 1, 4).reshape(-1, HEADS, 64, P)

    return (y[:SEQ].reshape(1, SEQ, D), y[SEQ:].reshape(NSEQ, TS, D),
            o["mem_k"].transpose(2, 1, 0).reshape(1, MEM, HEADS, MEM), o["mem_v"].transpose(1, 0, 2).reshape(1, MEM, HEADS, MEM),
            o["conv_p"].transpose(2, 1, 0).reshape(1, 3, 512), o["h"][:, :, 0].T.reshape(1, 512), unheads(s_p),
            o["conv_s"].transpose(2, 3, 1, 0).reshape(NSEQ, 3, 512), o["h"][:, :, 1:].transpose(2, 1, 0).reshape(NSEQ, 512), unheads(s_s))
```

```python
from contextlib import ExitStack

import concourse.bass as bass
from concourse import mybir

P = 128
D = 1024
KT = D // P
FF = 2816
FT = FF // P
SEQ, NSEQ, TS = 1024, 8, 8
SAMPLE = NSEQ * TS
TOK = SEQ + SAMPLE
MEM = 256
HEADS = 4
RANK = 16
CH = 32
EPS = 1e-6
OFFS = [0, 384, 768]
NS = [384, 384, 320]
NMAX = 384
NPROMPT = [384, 384, 256]
TT = NMAX // P

F32 = mybir.dt.float32
F32R = mybir.dt.float32r
ALU = mybir.AluOpType
ACT = mybir.ActivationFunctionType
AX = mybir.AxisListType

GAINS = {"ffn1": 0, "mix": 8, "mem": 16, "xan": 24, "ffn2": 32, "fin": 40}
V_RGO, V_GLO = 48, 52
V_CW, V_CB = 53, 69
V_BA, V_BX, V_LAM, V_BA2 = 73, 77, 81, 85
NV = 87
C_ONES, C_ID, C_ROW, C_M32, C_M8, C_SCAN, C_SCAN2 = 0, 128, 256, 264, 392, 456, 840
NC_A = 256
NCONST = 1160

ITS = FT // 2
FFN_TILES = 6 * ITS
STAGE_TILES = {"rg": (0, 8), "gla": (8, 12), "out": (20, 8), "memk": (28, 8), "memv": (36, 8), "cq": (44, 8), "co": (52, 8)}
STAGES = [("rg", 0), ("gla", 0), ("rg", 1), ("out", 0), ("gla", 1), ("rg", 2), ("out", 1), ("gla", 2),
          ("memk", 0), ("memv", 0), ("out", 2), ("cq", 0), ("co", 0), ("cq", 1), ("co", 1), ("cq", 2), ("co", 2)]
FIRST = {}
_t = 0
for _s in STAGES:
    FIRST[_s] = _t
    _t += STAGE_TILES[_s[0]][1]
MIX_TILES = _t
RING = 4


class Norm:

    def __init__(self, kind, n, groups, rows, N, outs):
        self.kind, self.n, self.groups, self.rows, self.N, self.outs = kind, n, groups, rows, N, outs
        self.T = (N + P - 1) // P


NORMS = {}


def _norm(kind, n):
    if kind == "rgo":
        a = Norm(kind, n, 1, 4, NS[n], 1)
    elif kind == "glo":
        a = Norm(kind, n, 4, 1, NS[n], 1)
    elif kind == "mem":
        a = Norm(kind, n, 1, 8, MEM, 2)
    elif kind == "fin":
        a = Norm(kind, n, 1, 8, NS[n], 1)
    else:
        a = Norm(kind, n, 1, 8, NS[n], 2)
    a.index = len(NORMS)
    before = list(NORMS.values())
    a.sq0 = sum(b.groups * b.rows for b in before)
    a.out0 = sum(b.outs for b in before)
    a.diag0 = sum(b.groups for b in before)
    NORMS[kind, n] = a


for _k in [("ffn1", 0), ("ffn1", 1), ("ffn1", 2), ("mix", 0), ("mix", 1), ("rgo", 0), ("glo", 0), ("mix", 2), ("rgo", 1),
           ("glo", 1), ("mem", 0), ("rgo", 2), ("glo", 2), ("xan", 0), ("xan", 1), ("xan", 2),
           ("ffn2", 0), ("ffn2", 1), ("ffn2", 2), ("fin", 0), ("fin", 1), ("fin", 2)]:
    _norm(*_k)

TURN = {}
_used, _filled = [0] * 8, [0] * 8
_next = {0: 0, 4: 0}


def _turn(*key, full=True):
    ring = 0 if key[0] == "sc" or key[1] in ("ffn1", "ffn2", "mem") or key[1:3] in (("mix", 1), ("mix", 2)) else 4
    b = ring + _next[ring] % 4
    _next[ring] += 1
    TURN[key] = (b, _used[b], _filled[b])
    _used[b] += 1
    _filled[b] += full


def _spread_turns(kind, n):
    for g in range(NORMS[kind, n].groups):
        _turn("rb", kind, n, g)


def _norm_turns(kind, n):
    _turn("st", kind, n, full=False)
    _spread_turns(kind, n)


def _gla_a(n, t):
    _turn("kdt", n, t)
    _turn("at", n, t, 0)
    _turn("at", n, t, 1)
    if NPROMPT[n] > t * P:
        for c in range(P // CH):
            _turn("kv", n, t, c)


def _gla_b(n, t):
    _turn("o", n, t, 0)
    _turn("o", n, t, 1)
    if NPROMPT[n] <= t * P:
        for b in range(NSEQ):
            _turn("kvs", b)


for _n in range(3):
    _norm_turns("ffn1", _n)
_norm_turns("mix", 0)
for _n in range(3):
    _turn("low", _n)
    _turn("z", _n, 0)
    _turn("z", _n, 1)
    for _j in range(8):
        _turn("gate", _n, _j)
    if _n < 2:
        _norm_turns("mix", _n + 1)
    _gla_a(_n, 0)
    _gla_a(_n, 1)
    _gla_b(_n, 0)
    if _n == 2:
        _turn("st", "mem", 0, full=False)
    _gla_a(_n, 2)
    _gla_b(_n, 1)
    if _n == 2:
        _spread_turns("mem", 0)
    _gla_b(_n, 2)
    _norm_turns("rgo", _n)
    _norm_turns("glo", _n)


def _pt(n, t):
    _turn("pt", n, t, 0)
    _turn("pt", n, t, 1)


def _pv(n, t):
    _turn("pv", n, t, 0)
    if NPROMPT[n] > t * P:
        _turn("pv", n, t, 1)


_norm_turns("xan", 0)
for _n in range(3):
    for _tt in range(TT):
        _turn("sc", _n, _tt, 0)
        _turn("sc", _n, _tt, 1)
    _pt(_n, 0)
    if _n < 2:
        _turn("st", "xan", _n + 1, full=False)
    _pt(_n, 1)
    _pv(_n, 0)
    _pt(_n, 2)
    _pv(_n, 1)
    _pv(_n, 2)
    if _n < 2:
        _spread_turns("xan", _n + 1)
for _k in ("ffn2", "fin"):
    for _n in range(3):
        _norm_turns(_k, _n)


def program(nc, a, out):
    base = (nc.sbuf_base + 63) // 64 * 64
    end = nc.sbuf_usable_end
    ctx = ExitStack()
    with ctx:
        def at(name, shape, offset, dtype=F32):
            offset = (offset + 31) // 32 * 32
            size = 4
            for s in shape[1:]:
                size *= s
            assert offset + size <= end, (name, offset + size - end)
            return nc.alloc_sbuf_tensor_at(name, shape, dtype, offset=offset), offset + size

        x, o = at("x", [P, KT, TOK], base)
        sq, o_ = at("sq", [P, 4, NMAX], o)
        o = o_
        diag, o = at("diag", [P, 2, TT, P], o)
        cst, o = at("cst", [P, NC_A], o)
        vec, o = at("vec", [P, NV + 1], o)
        rgc, o = at("rgc", [P, 8, 4], o)
        st, o = at("st", [P, 3, 12], o)
        o = (o + 63) // 64 * 64
        w_hi_sb, o = at("w_hi_sb", [P, 6, 1024], o, F32R)
        ffn_lo = o
        w_lo_sb, o = at("w_lo_sb", [P, 6, 1024], o, F32R)
        raw, o = at("raw", [P, 6, 1024], o)
        a_hi, o = at("a_hi", [P, KT, TOK], o, F32R)
        a_lo, o = at("a_lo", [P, KT, TOK], o, F32R)
        yb, _ = at("yb", [P, KT, TOK], ffn_lo + 12 * 4096)
        h_hi, h_lo = [None] * 2, [None] * 2
        for i in range(2):
            if i == 1:
                frow, _ = at("frow", [P, 4, NMAX], o)
            h_hi[i], o = at(f"h_hi{i}", [P, TOK], o, F32R)
            h_lo[i], o = at(f"h_lo{i}", [P, TOK], o, F32R)
        sil, o = at("sil", [P, 2, NMAX], o)
        hf, o = at("hf", [P, 2, NMAX], o)
        slot = 4096
        hole_hi = ffn_lo - 2 * slot
        hole_lo = ffn_lo + 4 * slot
        hole_raw = ffn_lo + 6 * slot + 4 * slot
        S, _ = at("S", [P, 8, 2, P], hole_hi)
        qm, q = at("qm", [P, 2, KT, SAMPLE], hole_hi)
        pt0, _ = at("pt0", [P, 2 * HEADS, P], q)
        cmix, q = at("cmix", [P, NCONST - NC_A], hole_lo)
        pt1, _ = at("pt1", [P, 2 * HEADS, P], q)
        pt = [pt0, pt1]
        bd, q = at("bd", [P, 8, P], q)
        assert q <= hole_lo + 2 * slot, q - hole_lo - 2 * slot
        o = hole_raw
        xn_hi, o = at("xn_hi", [P, KT, NMAX], o, F32R)
        xn_lo, o2 = at("xn_lo", [P, KT, NMAX], o, F32R)
        s0, q = at("s0", [P, NSEQ, 2, P], o - 4 * KT * NMAX)
        kdm, q = at("kdm", [P, NSEQ, 2 * P], o)
        o = o2
        mo_hi, o2 = at("mo_hi", [P, KT, NMAX], o, F32R)
        B, _ = at("B", [P, 2, NMAX], o)
        I, _ = at("I", [P, 4, NMAX], o + 4 * 4 * NMAX)
        o = o2
        mo_lo, o2 = at("mo_lo", [P, KT, NMAX], o, F32R)
        Z, q = at("Z", [P, 2, NMAX], o)
        E_, _ = at("E_", [P, 2, NMAX], q)
        T_, _ = at("T_", [P, 4, NMAX], o + 4 * 4 * NMAX)
        osb, _ = at("osb", [P, 4, NMAX], o + 4 * 4 * NMAX)
        qa, _ = at("qa", [P, KT, NMAX], o)
        o = o2
        region = o
        xbuf, o = at("xbuf", [P, 4, 3 + NMAX], o)
        xs, o = at("xs", [P, 4, NSEQ, 3 + TS], o)
        ybuf, o = at("ybuf", [P, 4, NMAX], o)
        kmem, o2 = at("kmem", [P, KT, MEM], region)
        memx, _ = at("memx", [P, KT, MEM], o2)
        vmem, o2 = at("vmem", [P, 2, D], o2)
        o = max(o, o2)
        union = o
        qk, o = at("qk", [P, 4, NMAX], o)
        gg, o = at("gg", [P, 4, NMAX], o)
        vt, o = at("vt", [P, TT, 4 * P], o)
        w_al_hi, o = at("w_al_hi", [P, KT, RANK], o, F32R)
        w_al_lo, o = at("w_al_lo", [P, KT, RANK], o, F32R)
        w_a2, o = at("w_a2", [RANK, 2 * P], o)
        hcar, o = at("hcar", [P, 4, 1], o)
        h0, o = at("h0", [P, 4, NSEQ], o)
        h0a, o = at("h0a", [P, 4, NSEQ], o)
        hlast, o = at("hlast", [P, 4, 1 + NSEQ], o)
        al, o = at("al", [RANK, NMAX], o)
        temps = o
        xc, o = at("xc", [P, 4, NMAX], o)
        R, o = at("R", [P, 4, NMAX], o)
        o2 = temps
        kd, o2 = at("kd", [P, 2, NMAX], o2)
        kdt, o2 = at("kdt", [P, TT, 2 * P], o2)
        AT, o2 = at("AT", [P, 2, 4, P], o2)
        o = union
        pr, o = at("pr", [P, 2, HEADS, MEM], o)
        kc, o = at("kc", [P, 3, 2 * D], o)
        mx, o = at("mx", [P, 2, 4, HEADS], o)

        ps = ctx.enter_context(nc.psum_tensor("ps", [P, 8, 512], F32))
        ones, ident = cst[:, C_ONES:C_ONES + P], cst[:, C_ID:C_ID + P]

        def mixc(c0, n):
            return cmix[:, c0 - NC_A:c0 - NC_A + n]

        def sem(name):
            return ctx.enter_context(nc.semaphore(name))

        raw_in = [sem(f"raw_in{k}") for k in range(6)]
        w_hi, w_lo = sem("w_hi"), sem("w_lo")
        const_in, mix_in, mem_in, state_in, s0_in = [sem(k) for k in ("const_in", "mix_in", "mem_in", "state_in", "s0_in")]
        x_in = [sem(f"x_in{n}") for n in range(3)]
        gu_done, silu_done, h_done, hhi_done, hid_done, down_done, x_added = [
            sem(k) for k in ("gu_done", "silu_done", "h_done", "hhi_done", "hid_done", "down_done", "x_added")]
        tile_done, evicted = sem("tile_done"), sem("evicted")
        squared, sq_used, root_done, diag_done, normed = [
            sem(k) for k in ("squared", "sq_used", "root_done", "diag_done", "normed")]
        bank_full = [sem(f"bank_full{b}") for b in range(8)]
        bank_free = [sem(f"bank_free{b}") for b in range(8)]
        dve_chain, act_chain = sem("dve_chain"), sem("act_chain")
        lam_done, wal_done = sem("lam_done"), sem("wal_done")
        conv_done, gates_done, u_ready, decay_done, mult_ready, root_mult, y_done, rg_out, rg_free = [
            sem(k) for k in ("conv_done", "gates_done", "u_ready", "decay_done", "mult_ready", "root_mult", "y_done", "rg_out", "rg_free")]
        soft_done, b_out, eneg_done, db_out, edb_done, qk_out, silug_done = [
            sem(k) for k in ("soft_done", "b_out", "eneg_done", "db_out", "edb_done", "qk_out", "silug_done")]
        kdm_done, max_done, pr_done, ohi_done, qm_done, ss_done, sv_done = [
            sem(k) for k in ("kdm_done", "max_done", "pr_done", "ohi_done", "qm_done", "ss_done", "sv_done")]
        kc_in = [sem(f"kc_in{k}") for k in range(3)]
        stored, y_stored = sem("stored"), sem("y_stored")

        block = ctx.enter_context(nc.Block())

        def bank(*key):
            return ps[:, TURN[key][0], :]

        def fill_wait(eng, *key):
            b, used, _ = TURN[key]
            if used:
                eng.wait_ge(bank_free[b], used)

        def full_wait(eng, *key):
            b, _, filled = TURN[key]
            eng.wait_ge(bank_full[b], filled + 1)

        def filled(ins, *key):
            ins.then_inc(bank_full[TURN[key][0]], 1)

        def release(ins, *key):
            ins.then_inc(bank_free[TURN[key][0]], 1)

        def read_wait(eng, *key):
            b, used, _ = TURN[key]
            eng.wait_ge(bank_free[b], used + 1)

        def tokens(n):
            return slice(OFFS[n], OFFS[n] + NS[n])

        def norm_source(kind, n, g, k):
            N = NORMS[kind, n].N
            if kind == "rgo":
                return I[:, k, 0:N]
            if kind == "glo":
                return osb[:, g, 0:N]
            if kind == "mem":
                return memx[:, k, :]
            return x[:, k, tokens(n)]

        GATE_UP_STEPS = 6 * ITS
        DOWNS = 3 * KT * ITS

        def wait_source(eng, kind, n):
            if kind == "ffn1":
                eng.wait_ge(x_in[n], 16)
            elif kind == "mix":
                eng.wait_ge(x_added, DOWNS - 3 * KT + KT * (n + 1))
            elif kind == "rgo":
                eng.wait_ge(rg_out, n + 1)
            elif kind == "glo":
                for t in range(TT):
                    for e in range(2):
                        read_wait(eng, "o", n, t, e)
            elif kind == "mem":
                eng.wait_ge(mem_in, 16)
            elif kind == "xan":
                eng.wait_ge(evicted, FIRST["out", n] + 8)
            elif kind == "ffn2":
                eng.wait_ge(evicted, FIRST["co", n] + 8)
            elif kind == "fin":
                eng.wait_ge(x_added, 2 * DOWNS - 3 * KT + KT * (n + 1))

        @block.sync
        def _(sp):
            def load_x(n):
                sp.dma_start(x[:, :, tokens(n)], a["x"].rearrange("(k p) t -> p k t", p=P)[:, :, tokens(n)]).then_inc(x_in[n], 16)

            load_x(0)
            sp.dma_start(cst[:, :], a["consts"][:, 0:NC_A]).then_inc(const_in, 16)
            sp.dma_start(vec[:, 0:NV], a["vectors"]).then_inc(const_in, 16)

            def ffn_loads(f, it, first):
                src = [a[f"ffn{f + 1}_{w}"] for w in ("gate", "up", "gate", "up", "down", "down")]
                for k in range(6):
                    if not first:
                        sp.wait_ge(w_lo, f * (FFN_TILES + MIX_TILES) + 6 * it + k - 5)
                    elif f and k < RING:
                        sp.wait_ge(w_lo, FFN_TILES + MIX_TILES - RING + k + 1)
                    elif f and k == RING:
                        sp.wait_ge(evicted, MIX_TILES)
                        sp.wait_ge(stored, 16 * 10)
                    elif k in (2, 4):
                        load_x(k // 2)
                    half = (0, 0, 1, 1, 0, 1)[k]
                    sp.dma_start(raw[:, k, :], src[k][bass.ds(2 * it + half, 1), :, :].rearrange("a p n -> p (a n)"))\
                      .then_inc(raw_in[k], 16)

            def cache_loads():
                for i in range(3, 2 * NSEQ):
                    if i - 3 < NSEQ - 1:
                        sp.wait_ge(ss_done, i - 2)
                    elif i - 3 == NSEQ - 1:
                        full_wait(sp, "sc", 2, 2, 1)
                    else:
                        sp.wait_ge(sv_done, i - 2 - NSEQ)
                    src = a["cache_k"][i, :, :] if i < NSEQ else a["cache_v"][i - NSEQ, :, :]
                    sp.dma_start(kc[:, i % 3, :], src).then_inc(kc_in[i % 3], 16)

            ffn_loads(0, 0, True)
            with sp.Fori(1, ITS) as it:
                ffn_loads(0, it, False)
            for t in range(MIX_TILES):
                if t == 4:
                    sp.wait_ge(down_done, DOWNS)
                    sp.dma_start(cmix[:, :], a["consts"][:, NC_A:NCONST]).then_inc(mix_in, 16)
                    sp.dma_start(bd[:, :, :], a["gates"]).then_inc(mix_in, 16)
                    sp.dma_start(w_a2[:, :], a["w_a2"]).then_inc(mix_in, 16)
                    sp.dma_start(h0[:, :, :], a["h0"]).then_inc(mix_in, 16)
                    sp.dma_start(R[:, 0, 0:KT * RANK], a["w_alow"]).then_inc(mix_in, 16)
                    for j in range(4):
                        sp.dma_start(xs[:, j, :, 0:3], a["conv0"][:, j, :, :]).then_inc(state_in, 16)
                if t == FIRST["memk", 0] + 2:
                    sp.wait_ge(rg_out, 3)
                    sp.dma_start(memx[:, :, :], a["mem"].rearrange("(k p) t -> p k t", p=P)).then_inc(mem_in, 16)
                    sp.dma_start(out["conv_p"], xbuf[:, :, NPROMPT[2]:NPROMPT[2] + 3]).then_inc(stored, 16)
                    for j in range(4):
                        sp.dma_start(out["conv_s"][:, j, :, :], xs[:, j, :, TS:TS + 3]).then_inc(stored, 16)
                    sp.dma_start(out["h"], hlast[:, :, :]).then_inc(stored, 16)
                if t == FIRST["co", 2] + 6:
                    cache_loads()
                stage = max((s for s in STAGES if FIRST[s] <= t), key=lambda s: FIRST[s])
                row = STAGE_TILES[stage[0]][0] + t - FIRST[stage]
                sp.wait_ge(w_lo, FFN_TILES + t - RING + 1 if t >= RING else FFN_TILES - 6 + t + 1)
                sp.dma_start(raw[:, t % RING, :], a["mix_tiles"][row, :, :]).then_inc(raw_in[t % RING], 16)
                if t == FIRST["out", 2]:
                    sp.wait_ge(tile_done, FIRST["memv", 0] + 8)
                    sp.dma_start(s0[:, :, :, :], a["s0"]).then_inc(s0_in, 16)
                    sp.wait_ge(evicted, FIRST["memv", 0] + 8)
                    sp.dma_start(out["mem_k"], kmem[:, :, :]).then_inc(stored, 16)
                    sp.dma_start(out["mem_v"], vmem[:, :, :]).then_inc(stored, 16)
                if t == FIRST["out", 2] + 5:
                    for b in range(NSEQ):
                        read_wait(sp, "kvs", b)
                    read_wait(sp, "kv", 2, 1, 3)
                    sp.dma_start(out["s_s"], s0[:, :, :, :]).then_inc(stored, 16)
                    sp.dma_start(out["s_p"], S[:, (SEQ // CH) % 8, :, :]).then_inc(stored, 16)
                if t == FIRST["cq", 2]:
                    for i in range(3):
                        sp.dma_start(kc[:, i, :], a["cache_k"][i, :, :]).then_inc(kc_in[i], 16)
            ffn_loads(1, 0, True)
            with sp.Fori(1, ITS) as it:
                ffn_loads(1, it, False)
            for n in range(3):
                p = NORMS["fin", n]
                for h in range(2):
                    if h == 0:
                        sp.wait_ge(normed, p.out0 + 1)
                    else:
                        read_wait(sp, "rb", "fin", n, 0)
                    sp.dma_start(out["y"].rearrange("(k p) t -> p k t", p=P)[:, 4 * h:4 * h + 4, tokens(n)], yb[:, 4 * h:4 * h + 4, tokens(n)])\
                      .then_inc(y_stored, 16)
            sp.wait_ge(y_stored, 16 * 6)

        @block.gpsimd
        def _(pool):
            def low(slot_, count):
                pool.wait_ge(w_hi, count)
                nc.gpsimd.tensor_tensor(w_lo_sb[:, slot_, :], raw[:, slot_, :], w_hi_sb[:, slot_, :].bitcast(F32), ALU.subtract)\
                  .then_inc(w_lo, 1)

            with pool.Fori(0, ITS) as it:
                for k in range(6):
                    low(k, 6 * it + k + 1)
            with pool.Fori(0, MIX_TILES // RING) as i:
                for k in range(RING):
                    low(k, FFN_TILES + RING * i + k + 1)
            with pool.Fori(0, ITS) as it:
                for k in range(6):
                    low(k, FFN_TILES + MIX_TILES + 6 * it + k + 1)

        @block.scalar
        def _(act):
            chain = [0]

            def link(ins):
                chain[0] += 1
                ins.then_inc(act_chain, 1)
                act.wait_ge(act_chain, chain[0])

            def prep(slot_, uses):
                act.wait_ge(raw_in[slot_], 16 * uses)
                nc.scalar.activation(w_hi_sb[:, slot_, :], raw[:, slot_, :], ACT.Copy).then_inc(w_hi, 1)

            mix_uses = MIX_TILES // RING

            def ffn_prep(f, it, k):
                before = f * (ITS + (mix_uses if k < RING else 0))
                prep(k, before + it + 1)

            def mix_prep(t):
                if t < MIX_TILES:
                    if t >= RING:
                        act.wait_ge(tile_done, t - RING + 1)
                    prep(t % RING, ITS + t // RING + 1)

            def norm_squares(kind, n, lo=0, hi=99):
                p = NORMS[kind, n]
                for i in range(max(lo, 0), min(hi, p.groups * p.rows)):
                    g, k = i // p.rows, i % p.rows
                    if i == 0:
                        wait_source(act, kind, n)
                        before = [k for k, v in NORMS.items() if v.index == p.index - 1]
                        if before and before[0][0] not in ("ffn1", "ffn2", "fin"):
                            act.wait_ge(normed, p.out0)
                    if p.sq0 + i >= 4:
                        act.wait_ge(sq_used, p.sq0 + i - 3)
                    nc.scalar.activation(sq[:, (p.sq0 + i) % 4, 0:p.N], norm_source(kind, n, g, k), ACT.Square).then_inc(squared, 1)

            def norm_root(kind, n):
                p = NORMS[kind, n]
                read_wait(act, "st", kind, n)
                m = p.groups * p.T
                nc.scalar.activation(st[:, 1, 0:m], st[:, 0, 0:m], ACT.Sqrt).then_inc(root_done, 1)

            def norm(kind, n):
                norm_squares(kind, n)
                norm_root(kind, n)

            def ffn(f):
                kinds = (("ffn1", "mix"), ("ffn2", "fin"))[f]

                def step(q0, s, first):
                    act.wait_ge(gu_done, f * GATE_UP_STEPS + q0 + s + 1)
                    if f or not first or s >= 2:
                        act.wait_ge(h_done, f * GATE_UP_STEPS + q0 + s - 1)
                    N = NS[s % 3]
                    nc.scalar.activation(sil[:, s % 2, 0:N], ps[:, 4 + 2 * (s % 2), 0:N], ACT.Silu).then_inc(silu_done, 1)

                def body(it, first, last):
                    q0 = 6 * it
                    if first:
                        norm(kinds[0], 0)
                        norm(kinds[0], 1)
                        for k in range(4):
                            if k == 0 and f:
                                act.wait_ge(tile_done, MIX_TILES)
                            ffn_prep(f, 0, k)
                    step(q0, 0, first)
                    if first:
                        norm(kinds[0], 2)
                    for k in (4, 5):
                        if not first:
                            act.wait_ge(down_done, f * DOWNS + 3 * KT * it)
                        ffn_prep(f, it, k)
                        step(q0, k - 3, first)
                    for k in (0, 1):
                        step(q0, 3 + k, first)
                        if not last:
                            act.wait_ge(gu_done, f * GATE_UP_STEPS + q0 + 3)
                            ffn_prep(f, it + 1, k)
                    step(q0, 5, first)
                    if not last:
                        for k in (2, 3):
                            act.wait_ge(gu_done, f * GATE_UP_STEPS + q0 + 6)
                            ffn_prep(f, it + 1, k)
                    else:
                        if f == 0:
                            for t in range(3):
                                mix_prep(t)
                        norm(kinds[1], 0)

                body(0, True, False)
                with act.Fori(1, ITS - 1) as it:
                    body(it, False, False)
                body(ITS - 1, False, True)

            act.wait_ge(const_in, 32)
            lam = vec[:, V_LAM:V_LAM + 4]
            link(nc.scalar.activation(rgc[:, 0, :], lam, ACT.Abs))
            nc.scalar.activation(rgc[:, 1, :], rgc[:, 0, :], ACT.Exp, scale=-1.0).then_inc(lam_done, 1)
            act.wait_ge(lam_done, 2)
            nc.scalar.activation(rgc[:, 3, :], rgc[:, 2, :], ACT.Ln).then_inc(lam_done, 1)

            ffn(0)

            for t in range(8):
                mix_prep(FIRST["rg", 0] + t + 3)
                if t == 4:
                    act.wait_ge(mix_in, 16 * 5)
                    nc.scalar.activation(w_al_hi[:, :, :], R[:, 0, 0:KT * RANK].rearrange("p (k r) -> p k r", k=KT), ACT.Copy)\
                      .then_inc(wal_done, 1)

            def rg_act(n, j):
                N = NS[n]
                if j in (4, 5):
                    if j == 4:
                        act.wait_ge(wal_done, 2)
                    for i in range(4):
                        full_wait(act, "gate", n, 4 * (j - 4) + i)
                        dst, bias = ((R, V_BA), (I, V_BX))[j - 4]
                        ins = nc.scalar.activation(dst[:, i, 0:N], bank("gate", n, 4 * (j - 4) + i)[:, 0:N], ACT.Sigmoid,
                                                   bias=vec[:, bias + i:bias + i + 1])
                        release(ins, "gate", n, 4 * (j - 4) + i)
                if j == 6:
                    act.wait_ge(lam_done, 4)
                    for i in range(8):
                        read_wait(act, "gate", n, i)
                    for i in range(4):
                        nc.scalar.activation(T_[:, i, 0:N], R[:, i, 0:N], ACT.Tanh, scale=rgc[:, 5, i:i + 1])
                if j == 7:
                    for i in range(4):
                        ins = nc.scalar.activation(R[:, i, 0:N], R[:, i, 0:N], ACT.Exp, scale=rgc[:, 6, i:i + 1])
                    ins.then_inc(decay_done, 1)
                if j == 9:
                    act.wait_ge(mult_ready, n + 1)
                    nc.scalar.activation(T_[:, :, 0:N], T_[:, :, 0:N], ACT.Sqrt).then_inc(root_mult, 1)
                if j == 10:
                    nc.scalar.activation(ybuf[:, :, 0:N], ybuf[:, :, 0:N], ACT.Gelu_apprx_tanh).then_inc(y_done, 1)

            def gla_act(n):
                N = NS[n]
                read_wait(act, "z", n, 0)
                read_wait(act, "z", n, 1)
                link(nc.scalar.activation(E_[:, :, 0:N], Z[:, :, 0:N], ACT.Abs))
                link(nc.scalar.activation(E_[:, :, 0:N], E_[:, :, 0:N], ACT.Exp, scale=-1.0))
                nc.scalar.activation(E_[:, :, 0:N], E_[:, :, 0:N], ACT.Ln, bias=1.0).then_inc(soft_done, 1)

            def gla_exp(n):
                N = NS[n]
                act.wait_ge(b_out, n + 1)
                nc.scalar.activation(E_[:, :, 0:N], B[:, :, 0:N], ACT.Exp, scale=-1.0 / 16).then_inc(eneg_done, 1)
                act.wait_ge(db_out, n + 1)
                nc.scalar.activation(Z[:, :, 0:N], Z[:, :, 0:N], ACT.Exp, scale=1.0 / 16)
                nc.scalar.activation(B[:, :, 0:N], B[:, :, 0:N], ACT.Exp, scale=1.0 / 16).then_inc(edb_done, 1)

            def gla_gate(n):
                N = NS[n]
                act.wait_ge(evicted, FIRST["gla", n] + 12)
                nc.scalar.activation(gg[:, :, 0:N], gg[:, :, 0:N], ACT.Silu).then_inc(silug_done, 1)

            def gla_keys(n, t):
                w = min(P, NS[n] - t * P)
                full_wait(act, "kdt", n, t)
                ins = nc.scalar.activation(kdt[0:w, t, :], bank("kdt", n, t)[0:w, 0:2 * P], ACT.Copy)
                release(ins, "kdt", n, t)

            def gla_outs(n, t):
                w = min(P, NS[n] - t * P)
                for e in range(2):
                    full_wait(act, "o", n, t, e)
                    ins = nc.scalar.activation(osb[:, e:4:2, t * P:t * P + w],
                                               bank("o", n, t, e)[:, 0:2 * P].rearrange("p (a i) -> p a i", a=2)[:, :, 0:w], ACT.Copy)
                    release(ins, "o", n, t, e)

            for n in range(3):
                for j in range(12):
                    mix_prep(FIRST["gla", n] + j + 3)
                    if j == 4:
                        gla_act(n)
                    rg_act(n, j)
                    if j == 6:
                        gla_exp(n)
                if n < 2:
                    norm("mix", n + 1)
                gla_gate(n)
                gla_keys(n, 0)
                gla_keys(n, 1)
                gla_outs(n, 0)
                if n == 2:
                    norm("mem", 0)
                gla_keys(n, 2)
                gla_outs(n, 1)
                if n == 2:
                    for j in range(16):
                        mix_prep(FIRST["memk", 0] + j + 3)
                gla_outs(n, 2)
                norm("rgo", n)
                if n < 2:
                    for j in range(4):
                        mix_prep(FIRST["rg", n + 1] + j + 3)
                norm("glo", n)
                if n < 2:
                    for j in range(4, 8):
                        mix_prep(FIRST["rg", n + 1] + j + 3)
                for j in range(8 if n < 2 else 4):
                    mix_prep(FIRST["out", n] + j + 3)

            def softmax(n, t):
                w = P if NPROMPT[n] > t * P else SAMPLE
                i = TT * n + t
                act.wait_ge(max_done, i + 1)
                if i >= 2:
                    full_wait(act, "pt", (i - 2) // TT, (i - 2) % TT, 1)
                for h in range(HEADS):
                    ins = nc.scalar.activation(pr[0:w, i % 2, h, :], bank("sc", n, t, h // 2)[0:w, (h % 2) * MEM:(h % 2 + 1) * MEM], ACT.Exp,
                                               bias=mx[0:w, i % 2, 1, h:h + 1], scale=1.0 / 16, accum_out=mx[0:w, i % 2, 2, h:h + 1])
                    if h % 2:
                        release(ins, "sc", n, t, h // 2)

            def probs_copy(n, t):
                w = P if NPROMPT[n] > t * P else SAMPLE
                for q in range(2):
                    full_wait(act, "pt", n, t, q)
                    ins = nc.scalar.activation(pt[(TT * n + t) % 2][:, 4 * q:4 * q + 4, 0:w],
                                               bank("pt", n, t, q)[:, 0:4 * w].rearrange("p (a i) -> p a i", a=4), ACT.Copy)
                    release(ins, "pt", n, t, q)

            def out_hi(n, t):
                w = P if NPROMPT[n] > t * P else SAMPLE
                for q in range(2 if w == P else 1):
                    full_wait(act, "pv", n, t, q)
                    m = 4 if w == P else 8
                    nc.scalar.activation(mo_hi[:, 4 * q:4 * q + m, t * P:t * P + w],
                                         bank("pv", n, t, q)[:, 0:m * w].rearrange("p (a i) -> p a i", a=m), ACT.Copy).then_inc(ohi_done, 1)

            norm("xan", 0)
            for j in range(4, 8):
                mix_prep(FIRST["out", 2] + j + 3)
            for n in range(3):
                for j in range(8):
                    mix_prep(FIRST["cq", n] + j + 3)
                softmax(n, 0)
                softmax(n, 1)
                probs_copy(n, 0)
                if n < 2:
                    norm_squares("xan", n + 1)
                softmax(n, 2)
                if n < 2:
                    norm_root("xan", n + 1)
                probs_copy(n, 1)
                out_hi(n, 0)
                probs_copy(n, 2)
                out_hi(n, 1)
                out_hi(n, 2)
                for j in range(8):
                    mix_prep(FIRST["co", n] + j + 3)

            ffn(1)
            for n in (1, 2):
                norm("fin", n)

        @block.vector
        def _(dve):
            chain = [0]

            def link(ins):
                chain[0] += 1
                ins.then_inc(dve_chain, 1)
                dve.wait_ge(dve_chain, chain[0])

            def norm_scale(kind, n):
                p = NORMS[kind, n]
                m = p.groups * p.T
                dve.wait_ge(sq_used, p.sq0 + p.groups * p.rows)
                width = P * p.rows
                ins = nc.vector.tensor_scalar(st[:, 0, 0:m], bank("st", kind, n)[:, 0:m], 1.0 / width, EPS, ALU.mult, ALU.add)
                release(ins, "st", kind, n)
                dve.wait_ge(root_done, p.index + 1)
                link(nc.vector.reciprocal(st[:, 2, 0:m], st[:, 1, 0:m]))

            def norm_diag(kind, n, g):
                p = NORMS[kind, n]
                d = p.diag0 + g
                if g >= 2:
                    full_wait(dve, "rb", kind, n, g - 2)
                nc.vector.tensor_tensor(diag[:, d % 2, 0:p.T, :], ident.rearrange("p (a i) -> p a i", a=1).to_broadcast([P, p.T, P]),
                                        st[:, 2, g * p.T:(g + 1) * p.T].rearrange("p (a i) -> p a i", i=1).to_broadcast([P, p.T, P]),
                                        ALU.mult).then_inc(diag_done, 1)

            def norm_head(kind, n):
                norm_scale(kind, n)
                norm_diag(kind, n, 0)

            def norm_rows(kind, n, between=None):
                p = NORMS[kind, n]
                N = p.N
                gain = {"rgo": V_RGO, "glo": V_GLO}.get(kind) or GAINS[kind]
                for half in range(p.groups * p.rows // 4):
                    for r in range(4):
                        row = 4 * half + r
                        g = row // p.rows
                        if row % p.rows == 0:
                            if g + 1 < p.groups:
                                norm_diag(kind, n, g + 1)
                            full_wait(dve, "rb", kind, n, g)
                        c = gain + (0 if kind == "glo" else row)
                        dst = {"ffn1": frow, "ffn2": frow}.get(kind, sq)[:, r, 0:N] if kind != "fin" else yb[:, row, tokens(n)]
                        ins = nc.vector.scalar_tensor_tensor(out=dst, in0=norm_source(kind, n, g, row % p.rows),
                                                             scalar=vec[:, c:c + 1], in1=bank("rb", kind, n, g)[:, 0:N],
                                                             op0=ALU.mult, op1=ALU.mult)
                        if row % p.rows == p.rows - 1:
                            release(ins, "rb", kind, n, g)
                            read_wait(dve, "rb", kind, n, g)
                        elif r == 3 and kind != "fin":
                            link(ins)
                        elif r == 3:
                            ins.then_inc(normed, 1)
                    if kind == "fin":
                        if between and half == 0:
                            between()
                        continue
                    src = (frow if kind in ("ffn1", "ffn2") else sq)[:, :, 0:N]
                    if kind == "glo":
                        dve.wait_ge(silug_done, n + 1)
                        link(nc.vector.tensor_tensor(src, src, gg[:, :, 0:N], ALU.mult))
                    rows = slice(4 * half, 4 * half + 4)
                    if kind == "rgo":
                        hi, lo = mo_hi[:, 0:4, 0:N], mo_lo[:, 0:4, 0:N]
                    elif kind == "glo":
                        hi, lo = mo_hi[:, 4:8, 0:N], mo_lo[:, 4:8, 0:N]
                    elif kind in ("ffn1", "ffn2"):
                        hi, lo = a_hi[:, rows, tokens(n)], a_lo[:, rows, tokens(n)]
                    else:
                        hi, lo = xn_hi[:, rows, 0:N], xn_lo[:, rows, 0:N]
                    link(nc.vector.tensor_copy(hi, src))
                    nc.vector.tensor_tensor(lo, src, hi.bitcast(F32), ALU.subtract).then_inc(normed, 1)
                    dve.wait_ge(normed, p.out0 + half + 1)
                    if between and half == 0:
                        between()

            def norm_wait_free(kind, n):
                if kind == "mix" and n == 0:
                    dve.wait_ge(gu_done, GATE_UP_STEPS)
                    dve.wait_ge(w_lo, FFN_TILES)
                if kind == "mix" and n:
                    dve.wait_ge(tile_done, FIRST["gla", n - 1] + 12)
                if kind == "mem":
                    dve.wait_ge(tile_done, FIRST["gla", 2] + 12)
                if kind == "xan":
                    if n == 0:
                        dve.wait_ge(stored, 16 * 10)
                    else:
                        dve.wait_ge(tile_done, FIRST["cq", n - 1] + 8)

            def norm(kind, n):
                norm_head(kind, n)
                norm_wait_free(kind, n)
                norm_rows(kind, n)

            def ffn(f):
                G, X, Q = f * GATE_UP_STEPS, f * DOWNS, 3 * KT
                kinds = (("ffn1", "mix"), ("ffn2", "fin"))[f]

                def body(it, first, last=False):
                    q0 = 6 * it
                    for s in range(6):
                        ft, n = s // 3, s % 3
                        N = NS[n]
                        if first and s == 0:
                            norm_head(kinds[0], 0)
                            norm_rows(kinds[0], 0, lambda: norm_head(kinds[0], 1))
                            norm_rows(kinds[0], 1)
                        if first and s == 1:
                            norm_head(kinds[0], 2)
                            norm_rows(kinds[0], 2)
                        b = 4 + 2 * (s % 2)
                        dve.wait_ge(silu_done, G + q0 + s + 1)
                        if f or not first or s >= 2:
                            dve.wait_ge(hid_done, G + q0 + s - 1)
                        nc.vector.tensor_tensor(hf[:, s % 2, 0:N], sil[:, s % 2, 0:N], ps[:, b + 1, 0:N], ALU.mult).then_inc(h_done, 1)
                        if f or not first:
                            dve.wait_ge(down_done, X + Q * it - Q + KT * (n + 1))
                        dve.wait_ge(h_done, G + q0 + s + 1)
                        nc.vector.tensor_copy(h_hi[ft][:, tokens(n)], hf[:, s % 2, 0:N]).then_inc(hhi_done, 1)
                        dve.wait_ge(hhi_done, G + q0 + s + 1)
                        nc.vector.tensor_tensor(h_lo[ft][:, tokens(n)], hf[:, s % 2, 0:N], h_hi[ft][:, tokens(n)].bitcast(F32), ALU.subtract)\
                          .then_inc(hid_done, 1)
                    for n in range(3):
                        if last and n == 2:
                            norm_head(kinds[1], 0)
                        for m in range(KT):
                            d = X + Q * it + KT * n + m
                            dve.wait_ge(down_done, d + 1)
                            if f or not first:
                                dve.wait_ge(x_added, d - Q + 1)
                            nc.vector.scalar_tensor_tensor(out=x[:, m, tokens(n)], in0=ps[:, m % 4, 0:NS[n]], scalar=0.5,
                                                           in1=x[:, m, tokens(n)], op0=ALU.mult, op1=ALU.add).then_inc(x_added, 1)

                body(0, True)
                with dve.Fori(1, ITS - 1) as it:
                    body(it, False)
                body(ITS - 1, False, True)

            dve.wait_ge(lam_done, 1)
            nc.vector.tensor_scalar(rgc[:, 2, :], rgc[:, 1, :], 1.0, None, ALU.add).then_inc(lam_done, 1)
            dve.wait_ge(lam_done, 3)
            link(nc.vector.tensor_scalar(rgc[:, 4, :], rgc[:, 2, :], -1.0, None, ALU.add))
            link(nc.vector.tensor_scalar(rgc[:, 5, :], rgc[:, 4, :], 0.0, None, ALU.is_equal))
            link(nc.vector.tensor_tensor(rgc[:, 4, :], rgc[:, 4, :], rgc[:, 5, :], ALU.add))
            link(nc.vector.tensor_tensor(rgc[:, 3, :], rgc[:, 3, :], rgc[:, 5, :], ALU.add))
            link(nc.vector.reciprocal(rgc[:, 6, :], rgc[:, 4, :]))
            link(nc.vector.tensor_tensor(rgc[:, 3, :], rgc[:, 3, :], rgc[:, 6, :], ALU.mult))
            link(nc.vector.tensor_tensor(rgc[:, 3, :], rgc[:, 3, :], rgc[:, 1, :], ALU.mult))
            link(nc.vector.tensor_scalar(rgc[:, 4, :], vec[:, V_LAM:V_LAM + 4], -1.0, 0.0, ALU.mult, ALU.max))
            link(nc.vector.tensor_tensor(rgc[:, 3, :], rgc[:, 3, :], rgc[:, 4, :], ALU.add))
            link(nc.vector.tensor_scalar(rgc[:, 5, :], rgc[:, 3, :], 8.0, None, ALU.mult))
            nc.vector.tensor_scalar(rgc[:, 6, :], rgc[:, 3, :], -8.0, None, ALU.mult).then_inc(lam_done, 1)

            ffn(0)

            def evict(kind, n, j):
                t = FIRST[kind, n] + j
                N = NS[n]
                dve.wait_ge(tile_done, t + 1)
                src = ps[:, t % RING, 0:N]
                if kind == "rg":
                    if j < 4:
                        np_ = NPROMPT[n]
                        if n == 2:
                            nc.vector.tensor_copy(xs[:, j, :, 3:3 + TS], ps[:, t % RING, np_:N].rearrange("p (b t) -> p b t", t=TS))
                        ins = nc.vector.tensor_copy(xbuf[:, j, 3:3 + np_], ps[:, t % RING, 0:np_])
                    else:
                        ins = nc.vector.tensor_copy(ybuf[:, j - 4, 0:N], src)
                elif kind == "gla":
                    dst = qk[:, j - 4, 0:N] if j < 8 else gg[:, j - 8, 0:N]
                    ins = nc.vector.tensor_copy(dst, src)
                elif kind == "memk":
                    ins = nc.vector.tensor_copy(kmem[:, j, :], ps[:, t % RING, 0:MEM])
                elif kind == "cq":
                    ins = nc.vector.tensor_copy(qa[:, j, 0:N], src)
                else:
                    ins = nc.vector.tensor_tensor(x[:, j, tokens(n)], x[:, j, tokens(n)], src, ALU.add)
                ins.then_inc(evicted, 1)

            def evict_values(n):
                t = FIRST["gla", n]
                dve.wait_ge(tile_done, t + 4)
                for i in range(TT):
                    w = min(P, NS[n] - i * P)
                    if w < P:
                        nc.vector.memset(vt[w:P, i, :], 0.0)
                    ins = nc.vector.tensor_copy(vt[0:w, i, :], ps[0:w, i, :])
                ins.then_inc(evicted, 4)

            def rg_conv(n):
                np_, N = NPROMPT[n], NS[n]
                dve.wait_ge(evicted, FIRST["rg", n] + 4)
                if n == 2:
                    dve.wait_ge(state_in, 16 * 4)
                for tap in range(4):
                    for j in range(4):
                        w = vec[:, V_CW + 4 * tap + j:V_CW + 4 * tap + j + 1]
                        parts = [(xc[:, j, 0:np_], xbuf[:, j, tap:tap + np_])]
                        if n == 2:
                            parts.append((xc[:, j, np_:N].rearrange("p (b t) -> p b t", t=TS), xs[:, j, :, tap:tap + TS]))
                        for dst, src in parts:
                            if tap == 0:
                                ins = nc.vector.tensor_scalar(dst, src, w, vec[:, V_CB + j:V_CB + j + 1], ALU.mult, ALU.add)
                            else:
                                ins = nc.vector.scalar_tensor_tensor(out=dst, in0=src, scalar=w, in1=dst, op0=ALU.mult, op1=ALU.add)
                    if tap < 3:
                        link(ins)
                ins.then_inc(conv_done, 1)
                if n < 2:
                    dve.wait_ge(conv_done, n + 1)
                    link(nc.vector.tensor_copy(xbuf[:, :, 0:3], xbuf[:, :, np_:np_ + 3]))

            def rg_vec(n, j):
                N, np_ = NS[n], NPROMPT[n]
                if j == 7:
                    dve.wait_ge(decay_done, n + 1)
                    link(nc.vector.tensor_tensor(I[:, :, 0:N], I[:, :, 0:N], xc[:, :, 0:N], ALU.mult))
                    link(nc.vector.tensor_tensor(xc[:, :, 0:N], R[:, :, 0:N], R[:, :, 0:N], ALU.mult))
                    nc.vector.scalar_tensor_tensor(out=T_[:, :, 0:N], in0=xc[:, :, 0:N], scalar=1.0, in1=T_[:, :, 0:N],
                                                   op0=ALU.add, op1=ALU.mult).then_inc(mult_ready, 1)
                if j == 9:
                    dve.wait_ge(root_mult, n + 1)
                    link(nc.vector.tensor_tensor(I[:, :, 0:N], I[:, :, 0:N], T_[:, :, 0:N], ALU.mult))
                    if n == 2:
                        starts_a = R[:, :, np_:N].rearrange("p j (b t) -> p j b t", t=TS)[:, :, :, 0]
                        starts_u = I[:, :, np_:N].rearrange("p j (b t) -> p j b t", t=TS)[:, :, :, 0]
                        link(nc.vector.tensor_tensor(h0a[:, :, :], starts_a, h0[:, :, :], ALU.mult))
                        link(nc.vector.tensor_tensor(starts_u, starts_u, h0a[:, :, :], ALU.add))
                        link(nc.vector.memset(starts_a, 0.0))
                    for i in range(4):
                        init = 0.0 if n == 0 else hcar[:, i, :]
                        ins = nc.vector.tensor_tensor_scan(xc[:, i, 0:N], R[:, i, 0:N], I[:, i, 0:N], init, ALU.mult, ALU.add)
                    link(ins)
                    if n < 2:
                        nc.vector.tensor_copy(hcar[:, :, :], xc[:, :, N - 1:N])
                    else:
                        nc.vector.tensor_copy(hlast[:, :, 0:1], xc[:, :, np_ - 1:np_])
                        nc.vector.tensor_copy(hlast[:, :, 1:], xc[:, :, np_ + TS - 1:N:TS])
                if j == 10:
                    dve.wait_ge(y_done, n + 1)
                    nc.vector.tensor_tensor(I[:, :, 0:N], xc[:, :, 0:N], ybuf[:, :, 0:N], ALU.mult).then_inc(rg_out, 1)

            def low_rank(n):
                N = NS[n]
                full_wait(dve, "low", n)
                ins = nc.vector.tensor_copy(al[:, 0:N], bank("low", n)[0:RANK, 0:N])
                release(ins, "low", n)

            def z_vec(n):
                N = NS[n]
                for j in range(2):
                    full_wait(dve, "z", n, j)
                    ins = nc.vector.tensor_scalar(Z[:, j, 0:N], bank("z", n, j)[:, 0:N], vec[:, V_BA2 + j:V_BA2 + j + 1], None, ALU.add)
                    release(ins, "z", n, j)

            def blocks(ap, lo, hi, c):
                return ap[:, :, lo:hi].rearrange("p j (b t) -> p j b t", t=c)

            def gla_cumsum(n):
                N, np_ = NS[n], NPROMPT[n]
                dve.wait_ge(soft_done, n + 1)
                link(nc.vector.scalar_tensor_tensor(out=Z[:, :, 0:N], in0=Z[:, :, 0:N], scalar=0.0, in1=E_[:, :, 0:N],
                                                    op0=ALU.min, op1=ALU.subtract))
                mask = mixc(C_SCAN2, N) if n == 2 else mixc(C_SCAN, N)
                for j in range(2):
                    ins = nc.vector.tensor_tensor_scan(B[:, j, 0:N], mask, Z[:, j, 0:N], 0.0, ALU.mult, ALU.add)
                ins.then_inc(b_out, 1)
                dve.wait_ge(b_out, n + 1)
                for lo, hi, c in [(0, np_, CH)] + ([(np_, N, TS)] if n == 2 else []):
                    for j in range(2):
                        bb = B[:, j, lo:hi].rearrange("p (b t) -> p b t", t=c)
                        ins = nc.vector.tensor_tensor(Z[:, j, lo:hi].rearrange("p (b t) -> p b t", t=c),
                                                      bb[:, :, c - 1:c].to_broadcast([P, (hi - lo) // c, c]), bb, ALU.subtract)
                ins.then_inc(db_out, 1)

            def gla_scaled(n):
                N = NS[n]
                dve.wait_ge(edb_done, n + 1)
                dve.wait_ge(rg_out, n + 1)
                dve.wait_ge(evicted, FIRST["gla", n] + 8)
                link(nc.vector.tensor_tensor(kd[:, :, 0:N], qk[:, 2:4, 0:N], Z[:, :, 0:N], ALU.mult))
                nc.vector.tensor_tensor(qk[:, 2:4, 0:N], qk[:, 2:4, 0:N], E_[:, :, 0:N], ALU.mult)
                nc.vector.scalar_tensor_tensor(out=qk[:, 0:2, 0:N], in0=qk[:, 0:2, 0:N], scalar=0.125, in1=B[:, :, 0:N],
                                               op0=ALU.mult, op1=ALU.mult).then_inc(qk_out, 1)

            def gla_scores(n, t):
                i = TT * n + t
                prompt = NPROMPT[n] > t * P
                w = P if prompt else SAMPLE
                mask = (mixc(C_M32, P) if prompt else mixc(C_M8, SAMPLE))[0:w, :].rearrange("p (a i) -> p a i", a=1).to_broadcast([w, 2, w])
                for e in range(2):
                    full_wait(dve, "at", n, t, e)
                    if i >= 2:
                        full_wait(dve, "o", (i - 2) // TT, (i - 2) % TT, e)
                    if w < P:
                        nc.vector.memset(AT[w:P, i % 2, 2 * e:2 * e + 2, 0:w], 0.0)
                    ins = nc.vector.tensor_tensor(AT[0:w, i % 2, 2 * e:2 * e + 2, 0:w],
                                                  bank("at", n, t, e)[0:w, 0:2 * w].rearrange("p (a i) -> p a i", a=2), mask, ALU.mult)
                    release(ins, "at", n, t, e)

            def gla_states(n, t):
                tile = TT * n + t
                for c in range(P // CH):
                    g = 4 * tile + c
                    full_wait(dve, "kv", n, t, c)
                    if g + 1 >= 8:
                        old = (g + 1 - 8) // 4
                        full_wait(dve, "o", old // TT, old % TT, 1)
                    for p in range(2):
                        for e in range(2):
                            rows = slice(64 * e, 64 * e + 64)
                            col = t * P + (c + 1) * CH - 1
                            ins = nc.vector.scalar_tensor_tensor(
                                out=S[rows, (g + 1) % 8, p, :], in0=S[rows, g % 8, p, :], scalar=B[rows, p, col:col + 1],
                                in1=bank("kv", n, t, c)[rows, (2 * p + e) * P:(2 * p + e + 1) * P], op0=ALU.mult, op1=ALU.add)
                    release(ins, "kv", n, t, c)
                    read_wait(dve, "kv", n, t, c)

            def gla_sample_keys():
                read_wait(dve, "kdt", 2, 2)
                dve.wait_ge(tile_done, FIRST["memv", 0] + 8)
                for b in range(NSEQ):
                    ins = nc.vector.tensor_scalar(kdm[0:SAMPLE, b, :], kdt[0:SAMPLE, 2, :], mixc(C_ROW, 8)[0:SAMPLE, b:b + 1], None, ALU.mult)
                ins.then_inc(kdm_done, 1)

            def gla_sample_states():
                for b in range(NSEQ):
                    full_wait(dve, "kvs", b)
                    for p in range(2):
                        for e in range(2):
                            rows = slice(64 * e, 64 * e + 64)
                            col = NPROMPT[2] + TS * b + TS - 1
                            ins = nc.vector.scalar_tensor_tensor(
                                out=s0[rows, b, p, :], in0=s0[rows, b, p, :], scalar=B[rows, p, col:col + 1],
                                in1=bank("kvs", b)[rows, (2 * p + e) * P:(2 * p + e + 1) * P], op0=ALU.mult, op1=ALU.add)
                    release(ins, "kvs", b)

            def gla_tile(n, t):
                gla_scores(n, t)
                if NPROMPT[n] > t * P:
                    gla_states(n, t)

            norm_wait_free("mix", 0)
            norm_rows("mix", 0)
            dve.wait_ge(down_done, DOWNS)
            nc.vector.memset(S[:, 0, :, :], 0.0)
            link(nc.vector.memset(xbuf[:, :, 0:3], 0.0))
            for j in range(8):
                evict("rg", 0, j)
            dve.wait_ge(wal_done, 1)
            nc.vector.tensor_tensor(w_al_lo[:, :, :], R[:, 0, 0:KT * RANK].rearrange("p (k r) -> p k r", k=KT),
                                    w_al_hi[:, :, :].bitcast(F32), ALU.subtract).then_inc(wal_done, 1)
            rg_conv(0)
            for n in range(3):
                low_rank(n)
                evict_values(n)
                z_vec(n)
                for j in range(4, 12):
                    evict("gla", n, j)
                    if j == 5:
                        gla_cumsum(n)
                    rg_vec(n, j)
                if n < 2:
                    norm_head("mix", n + 1)
                gla_scaled(n)
                gla_tile(n, 0)
                if n < 2:
                    norm_wait_free("mix", n + 1)
                    norm_rows("mix", n + 1, lambda: gla_tile(n, 1))
                    gla_tile(n, 2)
                    norm("rgo", n)
                    for j in range(4):
                        evict("rg", n + 1, j)
                    norm("glo", n)
                    for j in range(4, 8):
                        evict("rg", n + 1, j)
                    rg_conv(n + 1)
                else:
                    gla_tile(n, 1)
                    norm_head("mem", 0)
                    gla_tile(n, 2)
                    norm_wait_free("mem", 0)
                    norm_rows("mem", 0)
                    for j in range(8):
                        if j == 0:
                            dve.wait_ge(stored, 16 * 6)
                        evict("memk", 0, j)
                    for half in range(2):
                        t = FIRST["memv", 0] + 4 * half
                        dve.wait_ge(tile_done, t + 4)
                        for i in range(2):
                            ins = nc.vector.tensor_copy(vmem[:, i, 512 * half:512 * half + 512], ps[:, i, :])
                        ins.then_inc(evicted, 4)
                    gla_sample_keys()
                    gla_sample_states()
                    norm("rgo", n)
                    norm("glo", n)
                for j in range(8 if n < 2 else 4):
                    evict("out", n, j)

            def row_max(n, t):
                w = P if NPROMPT[n] > t * P else SAMPLE
                i = TT * n + t
                for q in range(2):
                    full_wait(dve, "sc", n, t, q)
                    ins = nc.vector.tensor_reduce(mx[0:w, i % 2, 0, 2 * q:2 * q + 2],
                                                  bank("sc", n, t, q)[0:w, :].rearrange("p (a m) -> p a m", a=2), AX.X, ALU.max)
                link(ins)
                nc.vector.tensor_scalar(mx[0:w, i % 2, 1, :], mx[0:w, i % 2, 0, :], -1.0 / 16, None, ALU.mult).then_inc(max_done, 1)

            def normalise(n, t):
                w = P if NPROMPT[n] > t * P else SAMPLE
                i = TT * n + t
                for q in range(2):
                    read_wait(dve, "sc", n, t, q)
                link(nc.vector.reciprocal(mx[0:w, i % 2, 3, :], mx[0:w, i % 2, 2, :]))
                for h in range(HEADS):
                    ins = nc.vector.tensor_scalar(pr[0:w, i % 2, h, :], pr[0:w, i % 2, h, :], mx[0:w, i % 2, 3, h:h + 1], None, ALU.mult)
                ins.then_inc(pr_done, 1)

            def out_lo(n, t):
                w = P if NPROMPT[n] > t * P else SAMPLE
                m = 4 if w == P else 8
                for q in range(2 if w == P else 1):
                    dve.wait_ge(ohi_done, 2 * (TT * n + t) + q + 1)
                    ins = nc.vector.tensor_tensor(mo_lo[:, 4 * q:4 * q + m, t * P:t * P + w],
                                                  bank("pv", n, t, q)[:, 0:m * w].rearrange("p (a i) -> p a i", a=m),
                                                  mo_hi[:, 4 * q:4 * q + m, t * P:t * P + w].bitcast(F32), ALU.subtract)
                    release(ins, "pv", n, t, q)

            def sample_queries():
                dve.wait_ge(evicted, FIRST["cq", 2] + 8)
                link(nc.vector.memset(qm[:, :, :, :], 0.0))
                for b in range(NSEQ):
                    if b >= 2:
                        dve.wait_ge(ss_done, b - 1)
                        link(nc.vector.memset(qm[:, b % 2, :, TS * (b - 2):TS * (b - 1)], 0.0))
                    c = NPROMPT[2] + TS * b
                    nc.vector.tensor_copy(qm[:, b % 2, :, TS * b:TS * b + TS], qa[:, :, c:c + TS]).then_inc(qm_done, 1)

            norm_head("xan", 0)
            for j in range(4, 8):
                evict("out", 2, j)
            norm_wait_free("xan", 0)
            norm_rows("xan", 0)
            for n in range(3):
                for j in range(8):
                    evict("cq", n, j)
                for t in range(2):
                    row_max(n, t)
                    normalise(n, t)
                if n == 2:
                    sample_queries()
                row_max(n, 2)
                normalise(n, 2)
                if n < 2:
                    norm_head("xan", n + 1)
                for t in range(TT):
                    out_lo(n, t)
                if n < 2:
                    norm_wait_free("xan", n + 1)
                    norm_rows("xan", n + 1)
                for j in range(8):
                    evict("co", n, j)

            dve.wait_ge(evicted, MIX_TILES)
            ffn(1)
            norm_rows("fin", 0, lambda: norm_head("fin", 1))
            norm_rows("fin", 1, lambda: norm_head("fin", 2))
            norm_rows("fin", 2)

        @block.tensor
        def _(pe):
            def split_mm(dst, w_h, w_l, x_h, x_l, start, stop):
                nc.tensor.matmul(dst, w_h, x_h, start=start, stop=False)
                nc.tensor.matmul(dst, w_h, x_l, start=False, stop=False)
                return nc.tensor.matmul(dst, w_l, x_h, start=False, stop=stop)

            def norm_stats(kind, n):
                p = NORMS[kind, n]
                fill_wait(pe, "st", kind, n)
                dst = bank("st", kind, n)
                for i in range(p.groups * p.rows):
                    g = i // p.rows
                    pe.wait_ge(squared, p.sq0 + i + 1)
                    for t in range(p.T):
                        c = min(t * P, p.N - P)
                        ins = nc.tensor.matmul(dst[:, g * p.T + t:g * p.T + t + 1], sq[:, (p.sq0 + i) % 4, c:c + P], ones[:, 0:1],
                                               start=(i == 0 and t == 0), stop=(i % p.rows == p.rows - 1), skip_group_check=True)
                    ins.then_inc(sq_used, 1)

            def norm_spread(kind, n):
                p = NORMS[kind, n]
                for g in range(p.groups):
                    fill_wait(pe, "rb", kind, n, g)
                    pe.wait_ge(diag_done, p.diag0 + g + 1)
                    d = diag[:, (p.diag0 + g) % 2, :, :].rearrange("p a i -> p (a i)")
                    whole = p.N // P * P
                    ins = nc.tensor.matmul(bank("rb", kind, n, g)[:, 0:whole], ones, d[:, 0:whole], start=True, stop=True)
                    if whole < p.N:
                        ins = nc.tensor.matmul(bank("rb", kind, n, g)[:, whole:p.N], ones, d[:, whole + P - (p.N - whole):whole + P], start=True, stop=True)
                    filled(ins, "rb", kind, n, g)

            def norm(kind, n):
                norm_stats(kind, n)
                norm_spread(kind, n)

            def ffn(f):
                kinds = (("ffn1", "mix"), ("ffn2", "fin"))[f]
                T0 = f * (FFN_TILES + MIX_TILES)
                G, X, Q = f * GATE_UP_STEPS, f * DOWNS, 3 * KT

                def body(it, first, last=False):
                    for s in range(6):
                        ft, n = s // 3, s % 3
                        if first and s == 0:
                            norm(kinds[0], 0)
                            norm(kinds[0], 1)
                        if first and s == 1:
                            norm(kinds[0], 2)
                        if first and s < 3:
                            pe.wait_ge(normed, NORMS[kinds[0], n].out0 + 2)
                        if n == 0:
                            pe.wait_ge(w_lo, T0 + 6 * it + 2 * ft + 2)
                        if f or not first or s >= 2:
                            pe.wait_ge(h_done, G + 6 * it + s - 1)
                        for u in range(2):
                            w = 2 * ft + u
                            for k in range(KT):
                                c = slice(k * P, k * P + P)
                                ins = split_mm(ps[:, 4 + 2 * (s % 2) + u, 0:NS[n]], w_hi_sb[:, w, c], w_lo_sb[:, w, c],
                                               a_hi[:, k, tokens(n)], a_lo[:, k, tokens(n)], k == 0, k == KT - 1)
                        ins.then_inc(gu_done, 1)
                    pe.wait_ge(w_lo, T0 + 6 * it + 6)
                    for n in range(3):
                        pe.wait_ge(hid_done, G + 6 * it + 3 + n + 1)
                        for m in range(KT):
                            if f or not first or KT * n + m >= 4:
                                pe.wait_ge(x_added, X + Q * it + KT * n + m - 3)
                            c = slice(m * P, m * P + P)
                            for ft in range(2):
                                ins = split_mm(ps[:, m % 4, 0:NS[n]], w_hi_sb[:, 4 + ft, c], w_lo_sb[:, 4 + ft, c],
                                               h_hi[ft][:, tokens(n)], h_lo[ft][:, tokens(n)], ft == 0, ft == 1)
                            ins.then_inc(down_done, 1)
                        if last and n == 1:
                            pe.wait_ge(h_done, G + GATE_UP_STEPS)
                            norm_stats(kinds[1], 0)
                    if last:
                        norm_spread(kinds[1], 0)

                body(0, True)
                with pe.Fori(1, ITS - 1) as it:
                    body(it, False)
                body(ITS - 1, False, True)

            def tiles(first, groups, hi, lo, N):
                def group(t):
                    for k4 in range(RING):
                        pe.wait_ge(w_lo, t + FFN_TILES + k4 + 1)
                        if not (first < 4 and isinstance(t, int) and t < 4):
                            pe.wait_ge(evicted, t + k4 - 3)
                        for k in range(KT):
                            c = slice(k * P, k * P + P)
                            ins = split_mm(ps[:, k4, 0:N], w_hi_sb[:, k4, c], w_lo_sb[:, k4, c], hi[:, k, 0:N], lo[:, k, 0:N],
                                           k == 0, k == KT - 1)
                        ins.then_inc(tile_done, 1)
                if first < 4 or groups == 1:
                    for g in range(groups):
                        group(first + RING * g)
                else:
                    with pe.Fori(0, groups) as g:
                        group(first + RING * g)

            def token_tiles(first, hi, lo, N):
                pe.wait_ge(evicted, first)
                for k4 in range(4):
                    pe.wait_ge(w_lo, FFN_TILES + first + k4 + 1)
                    for kk in range(2):
                        k = 2 * k4 + kk
                        c = slice(kk * 512, kk * 512 + 512)
                        for i in range((N + P - 1) // P):
                            r = slice(i * P, min(N, i * P + P))
                            w = r.stop - r.start
                            nc.tensor.matmul(ps[0:w, i, :], hi[:, k, r], w_hi_sb[:, k4, c], start=(k == 0), stop=False)
                            nc.tensor.matmul(ps[0:w, i, :], lo[:, k, r], w_hi_sb[:, k4, c], start=False, stop=False)
                            ins = nc.tensor.matmul(ps[0:w, i, :], hi[:, k, r], w_lo_sb[:, k4, c], start=False, stop=(k == KT - 1))
                    ins.then_inc(tile_done, 1)

            def gates(n):
                N = NS[n]
                pe.wait_ge(conv_done, n + 1)
                for j in range(8):
                    fill_wait(pe, "gate", n, j)
                    filled(nc.tensor.matmul(bank("gate", n, j)[:, 0:N], bd[:, j, :], xc[:, j % 4, 0:N], start=True, stop=True), "gate", n, j)

            def low_rank(n):
                N = NS[n]
                if n == 0:
                    pe.wait_ge(wal_done, 2)
                fill_wait(pe, "low", n)
                for k in range(KT):
                    ins = split_mm(bank("low", n)[0:RANK, 0:N], w_al_hi[:, k, :], w_al_lo[:, k, :], xn_hi[:, k, 0:N], xn_lo[:, k, 0:N],
                                   k == 0, k == KT - 1)
                filled(ins, "low", n)

            def decay_logits(n):
                N = NS[n]
                read_wait(pe, "low", n)
                for j in range(2):
                    fill_wait(pe, "z", n, j)
                    filled(nc.tensor.matmul(bank("z", n, j)[:, 0:N], w_a2[:, j * P:j * P + P], al[:, 0:N], start=True, stop=True), "z", n, j)

            def gla_a(n, t):
                prompt = NPROMPT[n] > t * P
                w = P if prompt else SAMPLE
                cols = slice(t * P, t * P + w)
                if t == 0:
                    pe.wait_ge(qk_out, n + 1)
                fill_wait(pe, "kdt", n, t)
                for p in range(2):
                    ins = nc.tensor.transpose(bank("kdt", n, t)[0:w, p * P:p * P + P], kd[:, p, cols], ident)
                filled(ins, "kdt", n, t)
                for e in range(2):
                    rows = slice(64 * e, 64 * e + 64)
                    fill_wait(pe, "at", n, t, e)
                    for p in range(2):
                        ins = nc.tensor.matmul(bank("at", n, t, e)[0:w, p * w:p * w + w], qk[rows, 2 + p, cols], qk[rows, p, cols],
                                               start=True, stop=True)
                    filled(ins, "at", n, t, e)
                if prompt:
                    read_wait(pe, "kdt", n, t)
                    for c in range(P // CH):
                        rows = slice(c * CH, c * CH + CH)
                        fill_wait(pe, "kv", n, t, c)
                        for p in range(2):
                            ins = nc.tensor.matmul(bank("kv", n, t, c)[:, 2 * p * P:2 * (p + 1) * P], kdt[rows, t, p * P:p * P + P],
                                                   vt[rows, t, 2 * p * P:2 * (p + 1) * P], start=True, stop=True)
                        filled(ins, "kv", n, t, c)

            def gla_b(n, t):
                prompt = NPROMPT[n] > t * P
                w = P if prompt else SAMPLE
                tile = TT * n + t
                for e in range(2):
                    rows = slice(64 * e, 64 * e + 64)
                    fill_wait(pe, "o", n, t, e)
                    read_wait(pe, "at", n, t, e)
                    if prompt:
                        read_wait(pe, "kv", n, t, 2)
                    else:
                        pe.wait_ge(s0_in, 16)
                    dst = bank("o", n, t, e)
                    for p in range(2):
                        h = 2 * p + e
                        nc.tensor.matmul(dst[:, p * P:p * P + w], vt[:, t, h * P:h * P + P], AT[:, tile % 2, 2 * e + p, 0:w],
                                         start=True, stop=False)
                        if prompt:
                            for c in range(P // CH):
                                s = slice(t * P + c * CH, t * P + (c + 1) * CH)
                                ins = nc.tensor.matmul(dst[:, p * P + c * CH:p * P + (c + 1) * CH], S[rows, (4 * tile + c) % 8, p, :],
                                                       qk[rows, p, s], start=False, stop=(c == P // CH - 1))
                        else:
                            for b in range(NSEQ):
                                s = slice(t * P + TS * b, t * P + TS * b + TS)
                                ins = nc.tensor.matmul(dst[:, p * P + TS * b:p * P + TS * b + TS], s0[rows, b, p, :],
                                                       qk[rows, p, s], start=False, stop=(b == NSEQ - 1))
                    filled(ins, "o", n, t, e)
                if not prompt:
                    pe.wait_ge(kdm_done, 1)
                    for b in range(NSEQ):
                        fill_wait(pe, "kvs", b)
                        for p in range(2):
                            ins = nc.tensor.matmul(bank("kvs", b)[:, 2 * p * P:2 * (p + 1) * P], kdm[0:SAMPLE, b, p * P:p * P + P],
                                                   vt[0:SAMPLE, 2, 2 * p * P:2 * (p + 1) * P], start=True, stop=True)
                        filled(ins, "kvs", b)

            pe.wait_ge(const_in, 32)
            ffn(0)
            pe.wait_ge(normed, NORMS["mix", 0].out0 + 2)
            pe.wait_ge(x_added, DOWNS)
            tiles(FIRST["rg", 0], 2, xn_hi, xn_lo, NS[0])
            for n in range(3):
                low_rank(n)
                token_tiles(FIRST["gla", n], xn_hi, xn_lo, NS[n])
                decay_logits(n)
                gates(n)
                tiles(FIRST["gla", n] + 4, 2, xn_hi, xn_lo, NS[n])
                pe.wait_ge(evicted, FIRST["gla", n] + 12)
                if n < 2:
                    norm("mix", n + 1)
                gla_a(n, 0)
                gla_a(n, 1)
                gla_b(n, 0)
                if n == 2:
                    norm_stats("mem", 0)
                gla_a(n, 2)
                gla_b(n, 1)
                if n == 2:
                    norm_spread("mem", 0)
                    pe.wait_ge(normed, NORMS["mem", 0].out0 + 2)
                    tiles(FIRST["memk", 0], 2, xn_hi, xn_lo, MEM)
                    for half in range(2):
                        token_tiles(FIRST["memv", 0] + 4 * half, xn_hi, xn_lo, MEM)
                gla_b(n, 2)
                norm("rgo", n)
                if n < 2:
                    pe.wait_ge(normed, NORMS["mix", n + 1].out0 + 2)
                    tiles(FIRST["rg", n + 1], 1, xn_hi, xn_lo, NS[n + 1])
                norm("glo", n)
                if n < 2:
                    tiles(FIRST["rg", n + 1] + 4, 1, xn_hi, xn_lo, NS[n + 1])
                pe.wait_ge(normed, NORMS["glo", n].out0 + 1)
                if n < 2:
                    tiles(FIRST["out", n], 2, mo_hi, mo_lo, NS[n])
                else:
                    tiles(FIRST["out", n], 1, mo_hi, mo_lo, NS[n])
                    norm("xan", 0)
                    tiles(FIRST["out", n] + 4, 1, mo_hi, mo_lo, NS[n])

            def scores(n, t):
                i = TT * n + t
                if t == 0:
                    pe.wait_ge(evicted, FIRST["cq", n] + 8)
                for q in range(2):
                    fill_wait(pe, "sc", n, t, q)
                if NPROMPT[n] > t * P:
                    for q in range(2):
                        for hh in range(2):
                            for dc in range(2):
                                f = 2 * (2 * q + hh) + dc
                                ins = nc.tensor.matmul(bank("sc", n, t, q)[:, hh * MEM:(hh + 1) * MEM], qa[:, f, t * P:t * P + P], kmem[:, f, :],
                                                       start=(dc == 0), stop=(dc == 1))
                        filled(ins, "sc", n, t, q)
                    return
                for b in range(NSEQ):
                    pe.wait_ge(qm_done, b + 1)
                    pe.wait_ge(kc_in[b % 3], 16 * (b // 3 + 1))
                    for f in range(KT):
                        q, hh, dc = f // 4, f // 2 % 2, f % 2
                        ins = nc.tensor.matmul(bank("sc", n, t, q)[0:SAMPLE, hh * MEM:(hh + 1) * MEM], qm[:, b % 2, f, :],
                                               kc[:, b % 3, f * MEM:(f + 1) * MEM], start=(b == 0 and hh == 0 and dc == 0),
                                               stop=(b == NSEQ - 1 and dc == 1), skip_group_check=True)
                        if b == NSEQ - 1 and f == 3:
                            filled(ins, "sc", n, t, 0)
                    if b < NSEQ - 1:
                        ins.then_inc(ss_done, 1)
                    else:
                        filled(ins, "sc", n, t, 1)

            def probs_transpose(n, t):
                w = P if NPROMPT[n] > t * P else SAMPLE
                i = TT * n + t
                pe.wait_ge(pr_done, i + 1)
                for q in range(2):
                    fill_wait(pe, "pt", n, t, q)
                    for r in range(4):
                        h, mc = 2 * q + r // 2, r % 2
                        ins = nc.tensor.transpose(bank("pt", n, t, q)[:, r * w:r * w + w], pr[0:w, i % 2, h, mc * P:mc * P + P], ident[0:w, 0:w])
                    filled(ins, "pt", n, t, q)

            def attend(n, t):
                prompt = NPROMPT[n] > t * P
                i = TT * n + t
                for q in range(2):
                    read_wait(pe, "pt", n, t, q)
                if prompt:
                    for q in range(2):
                        fill_wait(pe, "pv", n, t, q)
                        for r in range(4):
                            h, dc = 2 * q + r // 2, r % 2
                            for mc in range(2):
                                c = h * 2 * P + dc * P
                                ins = nc.tensor.matmul(bank("pv", n, t, q)[:, r * P:r * P + P], vmem[:, mc, c:c + P], pt[i % 2][:, 2 * h + mc, :],
                                                       start=(mc == 0), stop=(mc == 1))
                        filled(ins, "pv", n, t, q)
                    return
                fill_wait(pe, "pv", n, t, 0)
                for b in range(NSEQ):
                    kb = NSEQ + b
                    pe.wait_ge(kc_in[kb % 3], 16 * (kb // 3 + 1))
                    for f in range(KT):
                        for mc in range(2):
                            ins = nc.tensor.matmul(bank("pv", n, t, 0)[:, f * SAMPLE + TS * b:f * SAMPLE + TS * b + TS],
                                                   kc[:, kb % 3, mc * D + f * P:mc * D + f * P + P],
                                                   pt[i % 2][:, 2 * (f // 2) + mc, TS * b:TS * b + TS],
                                                   start=(b == 0 and f == 0 and mc == 0), stop=(mc == 1), skip_group_check=True)
                    if b < NSEQ - 1:
                        ins.then_inc(sv_done, 1)
                filled(ins, "pv", n, t, 0)

            for n in range(3):
                pe.wait_ge(normed, NORMS["xan", n].out0 + 2)
                tiles(FIRST["cq", n], 2, xn_hi, xn_lo, NS[n])
                scores(n, 0)
                scores(n, 1)
                probs_transpose(n, 0)
                scores(n, 2)
                if n < 2:
                    norm_stats("xan", n + 1)
                probs_transpose(n, 1)
                attend(n, 0)
                probs_transpose(n, 2)
                attend(n, 1)
                attend(n, 2)
                if n < 2:
                    norm_spread("xan", n + 1)
                for t in range(TT):
                    for q in range(2):
                        if t:
                            read_wait(pe, "sc", n, t, q)
                        if NPROMPT[n] > t * P or q == 0:
                            read_wait(pe, "pv", n, t, q)
                tiles(FIRST["co", n], 2, mo_hi, mo_lo, NS[n])

            pe.wait_ge(evicted, MIX_TILES)
            ffn(1)
            for n in (1, 2):
                norm("fin", n)


_OUTS = {"y": (D, TOK), "mem_k": (P, KT, MEM), "mem_v": (P, 2, D), "conv_p": (P, 4, 3), "h": (P, 4, 1 + NSEQ), "s_p": (P, 2, P),
         "conv_s": (P, 4, NSEQ, 3), "s_s": (P, NSEQ, 2, P)}


def kernel(**inputs):
    import numpy as np
    import concourse.bacc as bacc
    from concourse.bass_utils import run_bass_kernel_spmd

    i = {k: np.asarray(v) for k, v in inputs.items()}
    f32 = np.float32

    def tiles(w):
        return w.reshape(KT, P, -1, P).transpose(2, 1, 0, 3).reshape(-1, P, D)

    def wide(w):
        h = w.shape[1] // 512
        return w.reshape(4, 2, P, h, 512).transpose(3, 0, 2, 1, 4).reshape(4 * h, P, D)

    def cols(v):
        return v.reshape(-1, P).T

    w_in = i["w_in"]
    rg, q, k, v, g, low = np.split(w_in, [1024, 1280, 1536, 2048, 2560], axis=1)
    mix_tiles = np.concatenate([tiles(rg), wide(v), tiles(q), tiles(k), tiles(g), tiles(i["w_out"]), tiles(i["w_ck"]), wide(i["w_cv"]),
                                tiles(i["w_cq"]), tiles(i["w_co"])])
    vectors = np.concatenate([cols(i["ffn1_norm"]), cols(i["mix_norm"]), cols(i["mem_norm"]), cols(i["xattn_norm"]), cols(i["ffn2_norm"]),
                              cols(i["final_norm"]), cols(i["rg_out_norm"]), cols(i["gla_out_norm"]),
                              i["conv_w"].reshape(4, 4, P).transpose(2, 0, 1).reshape(P, 16), cols(i["conv_b"]),
                              cols(i["rg_b_a"].reshape(-1)), cols(i["rg_b_x"].reshape(-1)), cols(i["rg_lambda"]), cols(i["gla_b_a2"])], axis=1)

    gates = np.zeros((P, 8, P), f32)
    for j in range(4):
        for h in range(2):
            s = slice(64 * h, 64 * h + 64)
            gates[s, j, s] = i["rg_w_a"][2 * j + h]
            gates[s, 4 + j, s] = i["rg_w_x"][2 * j + h]

    consts = np.zeros((P, NCONST), f32)
    r, c = np.arange(P)[:, None], np.arange(P)[None, :]
    consts[:, C_ONES:C_ONES + P] = 1
    consts[:, C_ID:C_ID + P] = r == c
    consts[:, C_ROW:C_ROW + NSEQ] = r // TS == np.arange(NSEQ)
    consts[:, C_M32:C_M32 + P] = (r // CH == c // CH) & (r <= c)
    consts[:, C_M8:C_M8 + SAMPLE] = ((r // TS == c // TS) & (r <= c))[:, 0:SAMPLE]
    consts[:, C_SCAN:C_SCAN + NMAX] = np.arange(NMAX) % CH != 0
    t = np.arange(NS[2])
    consts[:, C_SCAN2:C_SCAN2 + NS[2]] = np.where(t < NPROMPT[2], t % CH != 0, t % TS != 0)

    def heads(s):
        return s.reshape(-1, 2, 2, 64, P).transpose(2, 3, 0, 1, 4).reshape(P, -1, 2, P)

    given = {
        "x": np.concatenate([i["x_prompt"].reshape(SEQ, D), i["x_sample"].reshape(SAMPLE, D)]).T,
        "consts": consts, "vectors": vectors, "gates": gates, "mix_tiles": mix_tiles,
        "w_alow": low.reshape(KT, P, RANK).transpose(1, 0, 2).reshape(P, KT * RANK), "w_a2": i["gla_w_a2"],
        "mem": i["mem_prompt"].reshape(MEM, D).T,
        "conv0": i["state_conv"].reshape(NSEQ, 3, 4, P).transpose(3, 2, 0, 1),
        "h0": i["state_rglru"].reshape(NSEQ, 4, P).transpose(2, 1, 0),
        "s0": heads(i["state_gla"]),
        "cache_k": i["cache_mem_k"].reshape(NSEQ, MEM, KT, P).transpose(0, 3, 2, 1).reshape(NSEQ, P, 2 * D),
        "cache_v": i["cache_mem_v"].reshape(NSEQ, 2, P, D).transpose(0, 2, 1, 3).reshape(NSEQ, P, 2 * D),
    }
    for f in (1, 2):
        given[f"ffn{f}_gate"] = tiles(i[f"ffn{f}_w_gate"])
        given[f"ffn{f}_up"] = tiles(i[f"ffn{f}_w_up"])
        given[f"ffn{f}_down"] = i[f"ffn{f}_w_down"].reshape(FT, P, D)

    nc = bacc.Bacc("TRN2", target_bir_lowering=False, num_devices=1)
    arrays, a, out = {}, {}, {}
    for name, v in given.items():
        arrays[f"in_{name}"] = np.ascontiguousarray(v)
        a[name] = nc.dram_tensor(f"in_{name}", v.shape, mybir.dt.from_np(v.dtype), kind="ExternalInput").ap()
    for name, shape in _OUTS.items():
        out[name] = nc.dram_tensor(f"out_{name}", shape, F32, kind="ExternalOutput").ap()
    program(nc, a, out)
    r = run_bass_kernel_spmd(nc, [arrays], core_ids=[0])
    o = {name: r.results[0][f"out_{name}"] for name in _OUTS}

    y = o["y"].T
    s_p, s_s = o["s_p"].reshape(P, 1, 2, P), o["s_s"]

    def unheads(s):
        return s.reshape(2, 64, -1, 2, P).transpose(2, 3, 0, 1, 4).reshape(-1, HEADS, 64, P)

    return (y[:SEQ].reshape(1, SEQ, D), y[SEQ:].reshape(NSEQ, TS, D),
            o["mem_k"].transpose(2, 1, 0).reshape(1, MEM, HEADS, MEM), o["mem_v"].transpose(1, 0, 2).reshape(1, MEM, HEADS, MEM),
            o["conv_p"].transpose(2, 1, 0).reshape(1, 3, 512), o["h"][:, :, 0].T.reshape(1, 512), unheads(s_p),
            o["conv_s"].transpose(2, 3, 1, 0).reshape(NSEQ, 3, 512), o["h"][:, :, 1:].transpose(2, 1, 0).reshape(NSEQ, 512), unheads(s_s))
```

```python
from contextlib import ExitStack

import concourse.bass as bass
from concourse import mybir

P = 128
D = 1024
KT = D // P
FF = 2816
FT = FF // P
SEQ, NSEQ, TS = 1024, 8, 8
SAMPLE = NSEQ * TS
TOK = SEQ + SAMPLE
MEM = 256
HEADS = 4
RANK = 16
CH = 32
EPS = 1e-6
OFFS = [0, 384, 768]
NS = [384, 384, 320]
NMAX = 384
NPROMPT = [384, 384, 256]
TT = NMAX // P

F32 = mybir.dt.float32
F32R = mybir.dt.float32r
ALU = mybir.AluOpType
ACT = mybir.ActivationFunctionType
AX = mybir.AxisListType

GAINS = {"ffn1": 0, "mix": 8, "mem": 16, "xan": 24, "ffn2": 32, "fin": 40}
V_RGO, V_GLO = 48, 52
V_CW, V_CB = 53, 69
V_BA, V_BX, V_LAM, V_BA2 = 73, 77, 81, 85
V_EPS = 87
NV = 88
C_ONES, C_ID, C_ROW, C_M32, C_M8, C_SCAN, C_SCAN2 = 0, 128, 256, 264, 392, 456, 840
NC_A = 256
NCONST = 1160

ITS = FT // 2
FFN_TILES = 6 * ITS
STAGE_TILES = {"rg": (0, 8), "gla": (8, 12), "out": (20, 8), "memk": (28, 8), "memv": (36, 8), "cq": (44, 8), "co": (52, 8)}
STAGES = [("rg", 0), ("gla", 0), ("rg", 1), ("out", 0), ("gla", 1), ("rg", 2), ("out", 1), ("gla", 2),
          ("memk", 0), ("memv", 0), ("out", 2), ("cq", 0), ("co", 0), ("cq", 1), ("co", 1), ("cq", 2), ("co", 2)]
FIRST = {}
_t = 0
for _s in STAGES:
    FIRST[_s] = _t
    _t += STAGE_TILES[_s[0]][1]
MIX_TILES = _t
RING = 4


def ffn_step(first, s):
    return (s % 2, s // 2) if first else (s // 3, s % 3)


class Norm:

    def __init__(self, kind, n, groups, rows, N, outs):
        self.kind, self.n, self.groups, self.rows, self.N, self.outs = kind, n, groups, rows, N, outs
        self.T = (N + P - 1) // P


NORMS = {}
AFTER_XA = [("xan", 1), ("xan", 2), ("ffn2", 0)]


def _norm(kind, n):
    if kind == "rgo":
        a = Norm(kind, n, 1, 4, NS[n], 1)
    elif kind == "glo":
        a = Norm(kind, n, 4, 1, NS[n], 1)
    elif kind == "mem":
        a = Norm(kind, n, 1, 8, MEM, 2)
    elif kind == "fin":
        a = Norm(kind, n, 1, 8, NS[n], 1)
    else:
        a = Norm(kind, n, 1, 8, NS[n], 2)
    a.index = len(NORMS)
    before = list(NORMS.values())
    a.quads = a.groups * a.rows // 4
    a.sq0 = sum(b.quads for b in before)
    a.sum0 = sum(b.quads for b in before if b.rows > 1)
    a.out0 = sum(b.outs for b in before)
    a.diag0 = sum(b.groups for b in before)
    NORMS[kind, n] = a


for _k in [("ffn1", 0), ("ffn1", 1), ("ffn1", 2), ("mix", 0), ("mix", 1), ("rgo", 0), ("glo", 0), ("mix", 2), ("rgo", 1),
           ("glo", 1), ("mem", 0), ("rgo", 2), ("glo", 2), ("xan", 0), ("xan", 1), ("xan", 2),
           ("ffn2", 0), ("ffn2", 1), ("ffn2", 2), ("fin", 0), ("fin", 1), ("fin", 2)]:
    _norm(*_k)

TURN = {}
_used, _filled = [0] * 8, [0] * 8
_next = {0: 0, 4: 0}


def _turn(*key, full=True):
    ring = 0 if key[0] == "sc" or key[1] in ("ffn1", "ffn2", "mem") or key[1:3] in (("mix", 1), ("mix", 2)) else 4
    if key[:3] in (("st", "ffn2", 0), ("rb", "ffn2", 0)):
        ring = 4
    if key[:2] == ("st", "mix"):
        ring = 4
    b = ring + _next[ring] % 4
    _next[ring] += 1
    TURN[key] = (b, _used[b], _filled[b])
    _used[b] += 1
    _filled[b] += full


def _spread_turns(kind, n):
    for g in range(NORMS[kind, n].groups):
        _turn("rb", kind, n, g)


def _norm_turns(kind, n):
    _turn("st", kind, n, full=False)
    _spread_turns(kind, n)


def _gla_a(n, t):
    _turn("kdt", n, t)
    _turn("at", n, t, 0)
    _turn("at", n, t, 1)
    if NPROMPT[n] > t * P:
        for c in range(P // CH):
            _turn("kv", n, t, c)


def _gla_b(n, t):
    _turn("o", n, t, 0)
    _turn("o", n, t, 1)
    if NPROMPT[n] <= t * P:
        for b in range(NSEQ):
            _turn("kvs", b)


for _n in range(3):
    _norm_turns("ffn1", _n)
_norm_turns("mix", 0)
for _n in range(3):
    _turn("low", _n)
    _turn("z", _n, 0)
    _turn("z", _n, 1)
    for _j in range(8):
        _turn("gate", _n, _j)
    if _n < 2:
        _norm_turns("mix", _n + 1)
    _gla_a(_n, 0)
    _gla_a(_n, 1)
    _gla_b(_n, 0)
    if _n == 2:
        _turn("st", "mem", 0, full=False)
    _gla_a(_n, 2)
    if _n < 2:
        _turn("st", "rgo", _n, full=False)
    else:
        _spread_turns("mem", 0)
    _gla_b(_n, 1)
    if _n < 2:
        _spread_turns("rgo", _n)
    _gla_b(_n, 2)
    if _n == 2:
        _norm_turns("rgo", _n)
    _norm_turns("glo", _n)


def _pt(n, t):
    _turn("pt", n, t, 0)
    _turn("pt", n, t, 1)


def _pv(n, t):
    _turn("pv", n, t, 0)
    _turn("pv", n, t, 1)


_norm_turns("xan", 0)
for _n in range(3):
    _turn("st", *AFTER_XA[_n], full=False)
    for _tt in range(TT):
        _turn("sc", _n, _tt, 0)
        _turn("sc", _n, _tt, 1)
    _pt(_n, 0)
    _pt(_n, 1)
    _pv(_n, 0)
    _pt(_n, 2)
    _pv(_n, 1)
    _pv(_n, 2)
    _spread_turns(*AFTER_XA[_n])
_turn("ot", 2)
_norm_turns("ffn2", 1)
_norm_turns("ffn2", 2)
for _n in range(3):
    _norm_turns("fin", _n)


def program(nc, a, out):
    base = (nc.sbuf_base + 63) // 64 * 64
    end = nc.sbuf_usable_end
    ctx = ExitStack()
    with ctx:
        def at(name, shape, offset, dtype=F32):
            offset = (offset + 31) // 32 * 32
            size = 4
            for s in shape[1:]:
                size *= s
            assert offset + size <= end, (name, offset + size - end)
            return nc.alloc_sbuf_tensor_at(name, shape, dtype, offset=offset), offset + size

        x, o = at("x", [P, KT, TOK], base)
        sq, o = at("sq", [P, 4, NMAX], o)
        diag, o = at("diag", [P, 2, TT, P], o)
        cst, o = at("cst", [P, NC_A], o)
        vec, o = at("vec", [P, NV], o)
        rgc, o = at("rgc", [P, 8, 4], o)
        st, o = at("st", [P, 2, 12], o)
        o = (o + 63) // 64 * 64
        w_hi_sb, o = at("w_hi_sb", [P, 6, 1024], o, F32R)
        ffn_lo = o
        w_lo_sb, o = at("w_lo_sb", [P, 6, 1024], o, F32R)
        raw, o = at("raw", [P, 6, 1024], o)
        operands = o
        yb, _ = at("yb", [P, KT, TOK], operands)
        a_hi, a_lo = [None] * 3, [None] * 3
        for n in range(3):
            a_hi[n], o = at(f"a_hi{n}", [P, KT, NS[n]], o, F32R)
            a_lo[n], o = at(f"a_lo{n}", [P, KT, NS[n]], o, F32R)
        h_hi, h_lo = [None] * 2, [None] * 2
        frow, _ = at("frow", [P, 4, TOK], o)
        for i in range(2):
            h_hi[i], o = at(f"h_hi{i}", [P, TOK], o, F32R)
            h_lo[i], o = at(f"h_lo{i}", [P, TOK], o, F32R)
        sil, o = at("sil", [P, 2, NMAX], o)
        sq_b, _ = at("sq_b", [P, 4, NMAX], o - 4 * 2 * NMAX)
        hf, o = at("hf", [P, 2, NMAX], o)
        slot = 4096
        hole_hi = ffn_lo - 2 * slot
        hole_lo = ffn_lo + 4 * slot
        hole_raw = ffn_lo + 6 * slot + 4 * slot
        S, _ = at("S", [P, 8, 2, P], hole_hi)
        qm, q = at("qm", [P, 2, KT, SAMPLE], hole_hi)
        pt0, _ = at("pt0", [P, 2 * HEADS, P], q)
        cmix, q = at("cmix", [P, NCONST - NC_A], hole_lo)
        pt1, _ = at("pt1", [P, 2 * HEADS, P], q)
        pt = [pt0, pt1]
        bd, q = at("bd", [P, 8, P], q)
        assert q <= hole_lo + 2 * slot, q - hole_lo - 2 * slot
        qk, q = at("qk", [P, 4, NMAX], hole_raw)
        al, q = at("al", [RANK, NMAX], q)
        pr, _ = at("pr", [P, 2, HEADS, MEM], hole_raw)
        assert q <= operands
        o = operands
        xn_hi, o = at("xn_hi", [P, KT, NMAX], o, F32R)
        xn_lo, o2 = at("xn_lo", [P, KT, NMAX], o, F32R)
        o = o2
        mo_hi, o2 = at("mo_hi", [P, KT, NMAX], o, F32R)
        B, q = at("B", [P, 2, NMAX], o)
        s0_b, _ = at("s0_b", [P, 2, 2, P], q)
        I, _ = at("I", [P, 4, NMAX], o + 4 * 4 * NMAX)
        o = o2
        mo_lo, o2 = at("mo_lo", [P, KT, NMAX], o, F32R)
        s0_a, _ = at("s0_a", [P, NSEQ - 2, 2, P], o)
        Z, q = at("Z", [P, 2, NMAX], o)
        E_, _ = at("E_", [P, 2, NMAX], q)
        T_, _ = at("T_", [P, 4, NMAX], o + 4 * 4 * NMAX)
        osb, _ = at("osb", [P, 4, NMAX], o + 4 * 4 * NMAX)
        qa, _ = at("qa", [P, KT, NMAX], o)
        o = o2
        conv_rows = o
        xbuf, o = at("xbuf", [P, 4, 3 + NMAX], o)
        xs, o = at("xs", [P, 4, NSEQ, 3 + TS], o)
        ybuf, o = at("ybuf", [P, 4, NMAX], o)
        kmem, o2 = at("kmem", [P, KT, MEM], conv_rows)
        memx, _ = at("memx", [P, KT, MEM], o2)
        vmem, o2 = at("vmem", [P, 2, D], o2)
        o = max(o, o2)
        behind_memory = o
        gg, o = at("gg", [P, 4, NMAX], o)
        vt, o = at("vt", [P, TT, 4 * P], o)
        w_al_hi, o = at("w_al_hi", [P, KT, RANK], o, F32R)
        w_al_lo, o = at("w_al_lo", [P, KT, RANK], o, F32R)
        w_a2, o = at("w_a2", [RANK, 2 * P], o)
        hcar, o = at("hcar", [P, 4, 1], o)
        h0, o = at("h0", [P, 4, NSEQ], o)
        h0a, o = at("h0a", [P, 4, NSEQ], o)
        hlast, o = at("hlast", [P, 4, 1 + NSEQ], o)
        temps = o
        xc, o = at("xc", [P, 4, NMAX], o)
        R, o = at("R", [P, 4, NMAX], o)
        o2 = temps
        kdt, o2 = at("kdt", [P, 4, 2 * P], o2)
        AT, o2 = at("AT", [P, 2, 4, P], o2)
        kd, o2 = at("kd", [P, 2, NMAX], o2)
        o = behind_memory
        kc, o = at("kc", [P, 3, 2 * D], o)
        mx, o = at("mx", [P, 2, 4, HEADS], o)

        ps = ctx.enter_context(nc.psum_tensor("ps", [P, 8, 512], F32))
        ones, ident = cst[:, C_ONES:C_ONES + P], cst[:, C_ID:C_ID + P]

        def mixc(c0, n):
            return cmix[:, c0 - NC_A:c0 - NC_A + n]

        def sem(name):
            return ctx.enter_context(nc.semaphore(name))

        raw_in = [sem(f"raw_in{k}") for k in range(6)]
        x_in = [sem(f"x_in{n}") for n in range(3)]
        const_in, mix_in, mem_in, state_in, s0_in = [sem(k) for k in ("const_in", "mix_in", "mem_in", "state_in", "s0_in")]
        kc_in = [sem(f"kc_in{k}") for k in range(3)]
        stored, states_stored, y_stored = sem("stored"), sem("states_stored"), sem("y_stored")
        w_hi, w_lo = sem("w_hi"), sem("w_lo")
        gu_done, silu_done, h_done, hhi_done, hid_done = [sem(k) for k in ("gu_done", "silu_done", "h_done", "hhi_done", "hid_done")]
        down_done, x_added = sem("down_done"), sem("x_added")
        tile_done, evicted = sem("tile_done"), sem("evicted")
        squared, summed, sq_used = sem("squared"), sem("summed"), sem("sq_used")
        diag_done, normed = sem("diag_done"), sem("normed")
        bank_full = [sem(f"bank_full{b}") for b in range(8)]
        bank_free = [sem(f"bank_free{b}") for b in range(8)]
        dve_chain, act_chain = sem("dve_chain"), sem("act_chain")
        lam_done, wal_done = sem("lam_done"), sem("wal_done")
        conv_done, mult_ready, rg_out = sem("conv_done"), sem("mult_ready"), sem("rg_out")
        decay_done, root_mult, y_done = sem("decay_done"), sem("root_mult"), sem("y_done")
        soft_done, eneg_done, edb_done, silug_done = [sem(k) for k in ("soft_done", "eneg_done", "edb_done", "silug_done")]
        b_out, db_out, qk_out = sem("b_out"), sem("db_out"), sem("qk_out")
        max_done, pr_done, ohi_done = sem("max_done"), sem("pr_done"), sem("ohi_done")
        qm_done, ss_done, sv_done = sem("qm_done"), sem("ss_done"), sem("sv_done")

        block = ctx.enter_context(nc.Block())

        def bank(*key):
            return ps[:, TURN[key][0], :]

        def fill_wait(eng, *key):
            b, used, _ = TURN[key]
            if used:
                eng.wait_ge(bank_free[b], used)

        def full_wait(eng, *key):
            b, _, filled = TURN[key]
            eng.wait_ge(bank_full[b], filled + 1)

        def filled(ins, *key):
            ins.then_inc(bank_full[TURN[key][0]], 1)

        def release(ins, *key):
            ins.then_inc(bank_free[TURN[key][0]], 1)

        def read_wait(eng, *key):
            b, used, _ = TURN[key]
            eng.wait_ge(bank_free[b], used + 1)

        def tokens(n):
            return slice(OFFS[n], OFFS[n] + NS[n])

        def s0(b):
            return s0_a[:, b] if b < NSEQ - 2 else s0_b[:, b - NSEQ + 2]

        def norm_source(kind, n, q):
            N = NORMS[kind, n].N
            if kind == "rgo":
                return I[:, :, 0:N]
            if kind == "glo":
                return osb[:, :, 0:N]
            return (memx if kind == "mem" else x)[:, 4 * q:4 * q + 4, slice(0, N) if kind == "mem" else tokens(n)]

        GATE_UP_STEPS = 6 * ITS
        DOWNS = 3 * KT * ITS

        def wait_source(eng, kind, n):
            if kind == "ffn1":
                eng.wait_ge(x_in[n], 16)
            elif kind == "mix":
                eng.wait_ge(x_added, DOWNS - 3 * KT + KT * (n + 1))
            elif kind == "rgo":
                eng.wait_ge(rg_out, n + 1)
            elif kind == "glo":
                for t in range(TT):
                    for e in range(2):
                        read_wait(eng, "o", n, t, e)
            elif kind == "mem":
                eng.wait_ge(mem_in, 16)
            elif kind == "xan":
                eng.wait_ge(evicted, FIRST["out", n] + 8)
            elif kind == "ffn2":
                eng.wait_ge(evicted, FIRST["co", n] + 8)
            elif kind == "fin":
                eng.wait_ge(x_added, 2 * DOWNS - 3 * KT + KT * (n + 1))

        def squares(kind, q):
            return sq_b if kind == "fin" and q else sq

        def rows_apart(kind, n):
            return kind in ("ffn1", "fin") or kind == "ffn2" and n > 0

        @block.sync
        def _(sp):
            def load_x(n):
                sp.dma_start(x[:, :, tokens(n)], a["x"].rearrange("(k p) t -> p k t", p=P)[:, :, tokens(n)]).then_inc(x_in[n], 16)

            load_x(0)
            sp.dma_start(cst[:, :], a["consts"][:, 0:NC_A]).then_inc(const_in, 16)
            sp.dma_start(vec[:, 0:NV], a["vectors"]).then_inc(const_in, 16)

            def ffn_loads(f, it, first):
                src = [a[f"ffn{f + 1}_{w}"] for w in ("gate", "up", "gate", "up", "down", "down")]
                for k in range(6):
                    if not first:
                        sp.wait_ge(w_lo, f * (FFN_TILES + MIX_TILES) + 6 * it + k - 5)
                    elif f and k < RING:
                        sp.wait_ge(w_lo, FFN_TILES + MIX_TILES - RING + k + 1)
                    elif f and k == RING:
                        sp.wait_ge(evicted, MIX_TILES)
                        sp.wait_ge(stored, 16 * 8)
                    elif k in (2, 4):
                        load_x(k // 2)
                    half = (0, 0, 1, 1, 0, 1)[k]
                    sp.dma_start(raw[:, k, :], src[k][bass.ds(2 * it + half, 1), :, :].rearrange("a p n -> p (a n)"))\
                      .then_inc(raw_in[k], 16)

            def cache_loads():
                for i in range(3, 2 * NSEQ):
                    if i - 3 < NSEQ - 1:
                        sp.wait_ge(ss_done, i - 2)
                    elif i - 3 == NSEQ - 1:
                        full_wait(sp, "sc", 2, 2, 1)
                    else:
                        sp.wait_ge(sv_done, i - 2 - NSEQ)
                    src = a["cache_k"][i, :, :] if i < NSEQ else a["cache_v"][i - NSEQ, :, :]
                    sp.dma_start(kc[:, i % 3, :], src).then_inc(kc_in[i % 3], 16)

            ffn_loads(0, 0, True)
            with sp.Fori(1, ITS) as it:
                ffn_loads(0, it, False)
            for t in range(MIX_TILES):
                if t == 4:
                    sp.wait_ge(down_done, DOWNS)
                    sp.dma_start(cmix[:, :], a["consts"][:, NC_A:NCONST]).then_inc(mix_in, 16)
                    sp.dma_start(bd[:, :, :], a["gates"]).then_inc(mix_in, 16)
                    sp.dma_start(w_a2[:, :], a["w_a2"]).then_inc(mix_in, 16)
                    sp.dma_start(h0[:, :, :], a["h0"]).then_inc(mix_in, 16)
                    sp.dma_start(R[:, 0, 0:KT * RANK], a["w_alow"]).then_inc(mix_in, 16)
                    for j in range(4):
                        sp.dma_start(xs[:, j, :, 0:3], a["conv0"][:, j, :, :]).then_inc(state_in, 16)
                if t == FIRST["memk", 0] + 3:
                    sp.wait_ge(rg_out, 3)
                    sp.dma_start(memx[:, :, :], a["mem"].rearrange("(k p) t -> p k t", p=P)).then_inc(mem_in, 16)
                    sp.dma_start(out["conv_p"], xbuf[:, :, NPROMPT[2]:NPROMPT[2] + 3]).then_inc(stored, 16)
                    for j in range(4):
                        sp.dma_start(out["conv_s"][:, j, :, :], xs[:, j, :, TS:TS + 3]).then_inc(stored, 16)
                    sp.dma_start(out["h"], hlast[:, :, :]).then_inc(stored, 16)
                    sp.wait_ge(qk_out, 3)
                    sp.dma_start(s0_a[:, :, :, :], a["s0"][:, 0:NSEQ - 2]).then_inc(s0_in, 16)
                    sp.dma_start(s0_b[:, :, :, :], a["s0"][:, NSEQ - 2:NSEQ]).then_inc(s0_in, 16)
                if t == FIRST["co", 2] + 6:
                    cache_loads()
                stage = max((s for s in STAGES if FIRST[s] <= t), key=lambda s: FIRST[s])
                row = STAGE_TILES[stage[0]][0] + t - FIRST[stage]
                sp.wait_ge(w_lo, FFN_TILES + t - RING + 1 if t >= RING else FFN_TILES - 6 + t + 1)
                sp.dma_start(raw[:, t % RING, :], a["mix_tiles"][row, :, :]).then_inc(raw_in[t % RING], 16)
                if t == FIRST["memk", 0] + 7:
                    for b in range(NSEQ):
                        read_wait(sp, "kvs", b)
                    read_wait(sp, "kv", 2, 1, 3)
                    sp.dma_start(out["s_s"][:, 0:NSEQ - 2], s0_a[:, :, :, :]).then_inc(states_stored, 16)
                    sp.dma_start(out["s_s"][:, NSEQ - 2:NSEQ], s0_b[:, :, :, :]).then_inc(states_stored, 16)
                    sp.dma_start(out["s_p"], S[:, (SEQ // CH) % 8, :, :]).then_inc(states_stored, 16)
                if t == FIRST["out", 2] + 3:
                    sp.wait_ge(evicted, FIRST["memv", 0] + 8)
                    sp.dma_start(out["mem_k"], kmem[:, :, :]).then_inc(stored, 16)
                    sp.dma_start(out["mem_v"], vmem[:, :, :]).then_inc(stored, 16)
                if t == FIRST["cq", 2]:
                    for i in range(3):
                        sp.dma_start(kc[:, i, :], a["cache_k"][i, :, :]).then_inc(kc_in[i], 16)
            ffn_loads(1, 0, True)
            with sp.Fori(1, ITS) as it:
                ffn_loads(1, it, False)
            for n in range(3):
                p = NORMS["fin", n]
                for h in range(2):
                    if h == 0:
                        sp.wait_ge(normed, p.out0 + 1)
                    else:
                        read_wait(sp, "rb", "fin", n, 0)
                    sp.dma_start(out["y"].rearrange("(k p) t -> p k t", p=P)[:, 4 * h:4 * h + 4, tokens(n)], yb[:, 4 * h:4 * h + 4, tokens(n)])\
                      .then_inc(y_stored, 16)
            sp.wait_ge(y_stored, 16 * 6)

        @block.gpsimd
        def _(pool):
            def low(slot_, count):
                pool.wait_ge(w_hi, count)
                nc.gpsimd.tensor_tensor(w_lo_sb[:, slot_, :], raw[:, slot_, :], w_hi_sb[:, slot_, :].bitcast(F32), ALU.subtract)\
                  .then_inc(w_lo, 1)

            with pool.Fori(0, ITS) as it:
                for k in range(6):
                    low(k, 6 * it + k + 1)
            with pool.Fori(0, MIX_TILES // RING) as i:
                for k in range(RING):
                    low(k, FFN_TILES + RING * i + k + 1)
            with pool.Fori(0, ITS) as it:
                for k in range(6):
                    low(k, FFN_TILES + MIX_TILES + 6 * it + k + 1)

        @block.scalar
        def _(act):
            chain = [0]

            def link(ins):
                chain[0] += 1
                ins.then_inc(act_chain, 1)
                act.wait_ge(act_chain, chain[0])

            def prep(slot_, uses):
                act.wait_ge(raw_in[slot_], 16 * uses)
                nc.scalar.activation(w_hi_sb[:, slot_, :], raw[:, slot_, :], ACT.Copy).then_inc(w_hi, 1)

            mix_uses = MIX_TILES // RING

            def ffn_prep(f, it, k):
                before = f * (ITS + (mix_uses if k < RING else 0))
                prep(k, before + it + 1)

            def mix_prep(t):
                if t < MIX_TILES:
                    if t >= RING:
                        act.wait_ge(tile_done, t - RING + 1)
                    prep(t % RING, ITS + t // RING + 1)

            def norm_squares(kind, n, quads=(0, 1)):
                p = NORMS[kind, n]
                for q in quads[:p.quads]:
                    if q == 0:
                        wait_source(act, kind, n)
                        before = [k for k, v in NORMS.items() if v.index == p.index - 1]
                        if before and not rows_apart(*before[0]):
                            act.wait_ge(normed, p.out0)
                    if kind == "fin":
                        act.wait_ge(sq_used, p.sq0 + q - 1)
                        act.wait_ge(hid_done, 2 * GATE_UP_STEPS)
                    elif p.sq0 + q:
                        act.wait_ge(sq_used, p.sq0 + q)
                    nc.scalar.activation(squares(kind, q)[:, :, 0:p.N], norm_source(kind, n, q), ACT.Square).then_inc(squared, 1)

            def norm_root(kind, n):
                p = NORMS[kind, n]
                act.wait_ge(sq_used, p.sq0 + p.quads)
                m = p.groups * p.T
                ins = nc.scalar.activation(st[:, 0, 0:m], bank("st", kind, n)[:, 0:m], ACT.Sqrt, bias=vec[:, V_EPS:V_EPS + 1],
                                           scale=1.0 / (P * p.rows))
                release(ins, "st", kind, n)

            def norm(kind, n):
                norm_squares(kind, n)
                norm_root(kind, n)

            def ffn(f):
                kinds = (("ffn1", "mix"), ("ffn2", "fin"))[f]

                def step(q0, s, first):
                    _, n = ffn_step(first, s)
                    act.wait_ge(gu_done, f * GATE_UP_STEPS + q0 + s + 1)
                    if f or not first or s >= 2:
                        act.wait_ge(h_done, f * GATE_UP_STEPS + q0 + s - 1)
                    N = NS[n]
                    nc.scalar.activation(sil[:, s % 2, 0:N], ps[:, 4 + 2 * (s % 2), 0:N], ACT.Silu).then_inc(silu_done, 1)

                def body(it, first, last):
                    q0 = 6 * it
                    if first:
                        if f == 0:
                            norm("ffn1", 0)
                            norm_squares("ffn1", 1, (0,))
                        for k in range(4):
                            if f:
                                act.wait_ge(tile_done, MIX_TILES - RING + k + 1)
                            ffn_prep(f, 0, k)
                            if k == (3 if f else 1):
                                norm_squares(kinds[0], 1, (1,))
                        norm_root(kinds[0], 1)
                    step(q0, 0, first)
                    if first:
                        norm_squares(kinds[0], 2, (0,))
                    for k in (4, 5):
                        if not first:
                            act.wait_ge(down_done, f * DOWNS + 3 * KT * it)
                        ffn_prep(f, it, k)
                        if first and k == 5:
                            norm_squares(kinds[0], 2, (1,))
                            norm_root(kinds[0], 2)
                        step(q0, k - 3, first)
                    step(q0, 3, first)
                    if not (first or last):
                        act.wait_ge(gu_done, f * GATE_UP_STEPS + q0 + 3)
                        ffn_prep(f, it + 1, 0)
                    step(q0, 4, first)
                    if not last:
                        if first:
                            act.wait_ge(gu_done, f * GATE_UP_STEPS + q0 + 5)
                            ffn_prep(f, it + 1, 0)
                        ffn_prep(f, it + 1, 1)
                    step(q0, 5, first)
                    if not last:
                        act.wait_ge(gu_done, f * GATE_UP_STEPS + q0 + 6)
                        ffn_prep(f, it + 1, 2)
                        ffn_prep(f, it + 1, 3)
                    else:
                        if f == 0:
                            for t in range(3):
                                mix_prep(t)
                        norm(kinds[1], 0)

                body(0, True, False)
                with act.Fori(1, ITS - 1) as it:
                    body(it, False, False)
                body(ITS - 1, False, True)

            act.wait_ge(const_in, 32)
            ffn(0)

            lam = vec[:, V_LAM:V_LAM + 4]
            link(nc.scalar.activation(rgc[:, 0, :], lam, ACT.Abs))
            nc.scalar.activation(rgc[:, 1, :], rgc[:, 0, :], ACT.Exp, scale=-1.0).then_inc(lam_done, 1)
            for t in range(8):
                mix_prep(FIRST["rg", 0] + t + 3)
                if t == 4:
                    act.wait_ge(mix_in, 16 * 5)
                    nc.scalar.activation(w_al_hi[:, :, :], R[:, 0, 0:KT * RANK].rearrange("p (k r) -> p k r", k=KT), ACT.Copy)\
                      .then_inc(wal_done, 1)

            act.wait_ge(lam_done, 2)
            nc.scalar.activation(rgc[:, 3, :], rgc[:, 2, :], ACT.Ln).then_inc(lam_done, 1)

            def rg_act(n, j):
                N = NS[n]
                if j in (4, 5):
                    if j == 4:
                        act.wait_ge(wal_done, 2)
                    for i in range(4):
                        full_wait(act, "gate", n, 4 * (j - 4) + i)
                        dst, bias = ((R, V_BA), (I, V_BX))[j - 4]
                        ins = nc.scalar.activation(dst[:, i, 0:N], bank("gate", n, 4 * (j - 4) + i)[:, 0:N], ACT.Sigmoid,
                                                   bias=vec[:, bias + i:bias + i + 1])
                        release(ins, "gate", n, 4 * (j - 4) + i)
                if j == 6:
                    act.wait_ge(lam_done, 4)
                    for i in range(8):
                        read_wait(act, "gate", n, i)
                    for i in range(4):
                        nc.scalar.activation(T_[:, i, 0:N], R[:, i, 0:N], ACT.Tanh, scale=rgc[:, 5, i:i + 1])
                if j == 7:
                    for i in range(4):
                        ins = nc.scalar.activation(R[:, i, 0:N], R[:, i, 0:N], ACT.Exp, scale=rgc[:, 6, i:i + 1])
                    ins.then_inc(decay_done, 1)
                if j == 9:
                    act.wait_ge(mult_ready, n + 1)
                    nc.scalar.activation(T_[:, :, 0:N], T_[:, :, 0:N], ACT.Sqrt).then_inc(root_mult, 1)
                if j == 10:
                    nc.scalar.activation(ybuf[:, :, 0:N], ybuf[:, :, 0:N], ACT.Gelu_apprx_tanh).then_inc(y_done, 1)

            def gla_act(n):
                N = NS[n]
                read_wait(act, "z", n, 0)
                read_wait(act, "z", n, 1)
                link(nc.scalar.activation(E_[:, :, 0:N], Z[:, :, 0:N], ACT.Abs))
                link(nc.scalar.activation(E_[:, :, 0:N], E_[:, :, 0:N], ACT.Exp, scale=-1.0))
                nc.scalar.activation(E_[:, :, 0:N], E_[:, :, 0:N], ACT.Ln, bias=1.0).then_inc(soft_done, 1)

            def gla_exp(n):
                N = NS[n]
                act.wait_ge(b_out, n + 1)
                nc.scalar.activation(E_[:, :, 0:N], B[:, :, 0:N], ACT.Exp, scale=-1.0 / 16).then_inc(eneg_done, 1)
                act.wait_ge(db_out, n + 1)
                nc.scalar.activation(Z[:, :, 0:N], Z[:, :, 0:N], ACT.Exp, scale=1.0 / 16)
                nc.scalar.activation(B[:, :, 0:N], B[:, :, 0:N], ACT.Exp, scale=1.0 / 16).then_inc(edb_done, 1)

            def gla_gate(n):
                N = NS[n]
                act.wait_ge(evicted, FIRST["gla", n] + 12)
                nc.scalar.activation(gg[:, :, 0:N], gg[:, :, 0:N], ACT.Silu).then_inc(silug_done, 1)

            def gla_keys(n, t):
                w = min(P, NS[n] - t * P)
                full_wait(act, "kdt", n, t)
                mask = mixc(C_ROW + (0 if w == P else 4), 4)
                for c in range(4):
                    ins = nc.scalar.activation(kdt[0:w, c, :], bank("kdt", n, t)[0:w, 0:2 * P], ACT.Copy, scale=mask[0:w, c:c + 1])
                release(ins, "kdt", n, t)

            def gla_outs(n, t):
                w = min(P, NS[n] - t * P)
                for e in range(2):
                    full_wait(act, "o", n, t, e)
                    ins = nc.scalar.activation(osb[:, e:4:2, t * P:t * P + w],
                                               bank("o", n, t, e)[:, 0:2 * P].rearrange("p (a i) -> p a i", a=2)[:, :, 0:w], ACT.Copy)
                    release(ins, "o", n, t, e)

            for n in range(3):
                for j in range(12):
                    mix_prep(FIRST["gla", n] + j + 3)
                    if j == 3 and n < 2:
                        norm_squares("mix", n + 1, (0,))
                    if j != 5:
                        rg_act(n, j)
                    if j == 4:
                        rg_act(n, 5)
                        gla_act(n)
                    if j == 7:
                        gla_exp(n)
                    if j == 8 and n < 2:
                        norm_squares("mix", n + 1, (1,))
                if n < 2:
                    norm_root("mix", n + 1)
                gla_keys(n, 0)
                gla_keys(n, 1)
                gla_gate(n)
                if n < 2:
                    tile = FIRST["rg", n + 1] + 3
                    mix_prep(tile)
                    gla_outs(n, 0)
                    norm_squares("rgo", n)
                    mix_prep(tile + 1)
                    gla_keys(n, 2)
                    mix_prep(tile + 2)
                    gla_outs(n, 1)
                    norm_root("rgo", n)
                    mix_prep(tile + 3)
                    gla_outs(n, 2)
                    mix_prep(tile + 4)
                    norm_squares("glo", n)
                    mix_prep(tile + 5)
                    norm_root("glo", n)
                    mix_prep(tile + 6)
                    mix_prep(tile + 7)
                else:
                    tile = FIRST["memk", 0] + 3
                    mix_prep(tile)
                    norm_squares("mem", 0, (0,))
                    gla_outs(n, 0)
                    norm_squares("mem", 0, (1,))
                    gla_keys(n, 2)
                    norm_root("mem", 0)
                    gla_outs(n, 1)
                    mix_prep(tile + 1)
                    gla_outs(n, 2)
                    mix_prep(tile + 2)
                    mix_prep(tile + 3)
                    norm_squares("rgo", n)
                    mix_prep(tile + 4)
                    norm_root("rgo", n)
                    mix_prep(tile + 5)
                    mix_prep(tile + 6)
                    norm_squares("glo", n)
                    mix_prep(tile + 7)
                    norm_root("glo", n)
                    for j in range(8, 16):
                        mix_prep(tile + j)
                    norm_squares("xan", 0, (0,))
                for j in range(8):
                    mix_prep(FIRST["out", n] + j + 3)
                    if n == 2 and j == 1:
                        norm_squares("xan", 0, (1,))
                    if n == 2 and j == 4:
                        norm_root("xan", 0)

            def softmax(n, t):
                w = P if NPROMPT[n] > t * P else SAMPLE
                i = TT * n + t
                act.wait_ge(max_done, i + 1)
                if i >= 2:
                    full_wait(act, "pt", (i - 2) // TT, (i - 2) % TT, 1)
                for h in range(HEADS):
                    ins = nc.scalar.activation(pr[0:w, i % 2, h, :], bank("sc", n, t, h // 2)[0:w, (h % 2) * MEM:(h % 2 + 1) * MEM], ACT.Exp,
                                               bias=mx[0:w, i % 2, 1, h:h + 1], scale=1.0 / 16, accum_out=mx[0:w, i % 2, 2, h:h + 1])
                    if h % 2:
                        release(ins, "sc", n, t, h // 2)

            def probs_copy(n, t):
                w = P if NPROMPT[n] > t * P else SAMPLE
                for q in range(2):
                    full_wait(act, "pt", n, t, q)
                    ins = nc.scalar.activation(pt[(TT * n + t) % 2][:, 4 * q:4 * q + 4, 0:w],
                                               bank("pt", n, t, q)[:, 0:4 * w].rearrange("p (a i) -> p a i", a=4), ACT.Copy)
                    release(ins, "pt", n, t, q)

            def out_hi(n, t):
                w = P if NPROMPT[n] > t * P else SAMPLE
                if w == P:
                    for q in range(2):
                        full_wait(act, "pv", n, t, q)
                        nc.scalar.activation(mo_hi[:, 4 * q:4 * q + 4, t * P:t * P + P],
                                             bank("pv", n, t, q)[:, :].rearrange("p (a i) -> p a i", a=4), ACT.Copy).then_inc(ohi_done, 1)
                    return
                for q in range(2):
                    full_wait(act, "pv", n, t, q)
                    ins = nc.scalar.activation(pr[0:SAMPLE, (TT * n + t) % 2, 2 * q:2 * q + 2, :],
                                               bank("pv", n, t, q)[0:SAMPLE, :].rearrange("p (a i) -> p a i", a=2), ACT.Copy)
                    release(ins, "pv", n, t, q)
                full_wait(act, "ot", 2)
                nc.scalar.activation(mo_hi[:, :, t * P:t * P + w], bank("ot", 2)[:, 0:8 * w].rearrange("p (a i) -> p a i", a=8), ACT.Copy)\
                  .then_inc(ohi_done, 1)

            for n in range(3):
                beside = AFTER_XA[n]
                for j in range(8):
                    mix_prep(FIRST["cq", n] + j + 3)
                    if j == 1:
                        norm_squares(*beside, (0,))
                    if j == 5:
                        norm_squares(*beside, (1,))
                norm_root(*beside)
                softmax(n, 0)
                softmax(n, 1)
                probs_copy(n, 0)
                softmax(n, 2)
                probs_copy(n, 1)
                out_hi(n, 0)
                probs_copy(n, 2)
                out_hi(n, 1)
                out_hi(n, 2)
                for j in range(8):
                    mix_prep(FIRST["co", n] + j + 3)
                    if n == 2 and j == 3:
                        norm_squares("ffn2", 1, (0,))

            ffn(1)
            norm("fin", 1)
            norm("fin", 2)

        @block.vector
        def _(dve):
            chain = [0]

            def link(ins):
                chain[0] += 1
                ins.then_inc(dve_chain, 1)
                dve.wait_ge(dve_chain, chain[0])

            def norm_scale(kind, n):
                p = NORMS[kind, n]
                m = p.groups * p.T
                read_wait(dve, "st", kind, n)
                link(nc.vector.reciprocal(st[:, 1, 0:m], st[:, 0, 0:m]))

            def norm_diag(kind, n, g):
                p = NORMS[kind, n]
                d = p.diag0 + g
                if g >= 2:
                    full_wait(dve, "rb", kind, n, g - 2)
                nc.vector.tensor_tensor(diag[:, d % 2, 0:p.T, :], ident.rearrange("p (a i) -> p a i", a=1).to_broadcast([P, p.T, P]),
                                        st[:, 1, g * p.T:(g + 1) * p.T].rearrange("p (a i) -> p a i", i=1).to_broadcast([P, p.T, P]),
                                        ALU.mult).then_inc(diag_done, 1)

            def norm_sum(kind, n, q):
                p = NORMS[kind, n]
                dve.wait_ge(squared, p.sq0 + q + 1)
                buf = squares(kind, q)
                link(nc.vector.tensor_tensor(buf[:, 0:2, 0:p.N], buf[:, 0:2, 0:p.N], buf[:, 2:4, 0:p.N], ALU.add))
                nc.vector.tensor_tensor(buf[:, 0, 0:p.N], buf[:, 0, 0:p.N], buf[:, 1, 0:p.N], ALU.add).then_inc(summed, 1)

            def norm_head(kind, n, sums=(0, 1)):
                p = NORMS[kind, n]
                if p.rows > 1:
                    for q in sums[:p.quads]:
                        norm_sum(kind, n, q)
                norm_scale(kind, n)
                norm_diag(kind, n, 0)

            def norm_rows(kind, n, between=None):
                p = NORMS[kind, n]
                N = p.N
                rowbuf = frow[:, :, TOK - N:TOK] if rows_apart(kind, n) else sq[:, :, 0:N]
                gain = {"rgo": V_RGO, "glo": V_GLO}.get(kind) or GAINS[kind]
                for half in range(p.groups * p.rows // 4):
                    for r in range(4):
                        row = 4 * half + r
                        g = row // p.rows
                        if row % p.rows == 0:
                            if g + 1 < p.groups:
                                norm_diag(kind, n, g + 1)
                            full_wait(dve, "rb", kind, n, g)
                        c = gain + (0 if kind == "glo" else row)
                        dst = yb[:, row, tokens(n)] if kind == "fin" else rowbuf[:, r, :]
                        ins = nc.vector.scalar_tensor_tensor(out=dst, in0=norm_source(kind, n, half)[:, r, :],
                                                             scalar=vec[:, c:c + 1], in1=bank("rb", kind, n, g)[:, 0:N],
                                                             op0=ALU.mult, op1=ALU.mult)
                        if row % p.rows == p.rows - 1:
                            release(ins, "rb", kind, n, g)
                            read_wait(dve, "rb", kind, n, g)
                        elif r == 3 and kind != "fin":
                            link(ins)
                        elif r == 3:
                            ins.then_inc(normed, 1)
                    if kind == "fin":
                        if between and half == 0:
                            between()
                        continue
                    src = rowbuf
                    if kind == "glo":
                        dve.wait_ge(silug_done, n + 1)
                        link(nc.vector.tensor_tensor(src, src, gg[:, :, 0:N], ALU.mult))
                    rows = slice(4 * half, 4 * half + 4)
                    if kind == "rgo":
                        hi, lo = mo_hi[:, 0:4, 0:N], mo_lo[:, 0:4, 0:N]
                    elif kind == "glo":
                        hi, lo = mo_hi[:, 4:8, 0:N], mo_lo[:, 4:8, 0:N]
                    elif kind in ("ffn1", "ffn2"):
                        hi, lo = a_hi[n][:, rows, :], a_lo[n][:, rows, :]
                    else:
                        hi, lo = xn_hi[:, rows, 0:N], xn_lo[:, rows, 0:N]
                    link(nc.vector.tensor_copy(hi, src))
                    nc.vector.tensor_tensor(lo, src, hi.bitcast(F32), ALU.subtract).then_inc(normed, 1)
                    dve.wait_ge(normed, p.out0 + half + 1)
                    if between and half == 0:
                        between()

            def norm_wait_free(kind, n):
                if kind == "mix" and n == 0:
                    dve.wait_ge(gu_done, GATE_UP_STEPS)
                if kind == "mix" and n:
                    dve.wait_ge(tile_done, FIRST["gla", n - 1] + 12)
                if kind == "mem":
                    dve.wait_ge(tile_done, FIRST["gla", 2] + 12)
                if kind == "rgo" and n == 2:
                    dve.wait_ge(states_stored, 16 * 3)
                if kind == "xan":
                    if n == 0:
                        dve.wait_ge(tile_done, FIRST["memv", 0] + 8)
                    else:
                        dve.wait_ge(tile_done, FIRST["cq", n - 1] + 8)
                if kind == "ffn2" and n == 0:
                    dve.wait_ge(tile_done, FIRST["cq", 2] + 8)

            def norm(kind, n):
                norm_head(kind, n)
                norm_wait_free(kind, n)
                norm_rows(kind, n)

            def ffn(f):
                G, X, Q = f * GATE_UP_STEPS, f * DOWNS, 3 * KT
                kinds = (("ffn1", "mix"), ("ffn2", "fin"))[f]

                def body(it, first, last=False):
                    q0 = 6 * it
                    for s in range(6):
                        ft, n = ffn_step(first, s)
                        N = NS[n]
                        if first and s == 0 and f == 0:
                            norm_head("ffn1", 0)
                            norm_sum("ffn1", 1, 0)
                            norm_rows("ffn1", 0, lambda: norm_sum("ffn1", 1, 1))
                            norm_head("ffn1", 1, ())
                        elif first and s in (0, 2):
                            norm_head(kinds[0], n + 1, (1,))
                        if first and s == 1:
                            norm_rows(kinds[0], 1, lambda: norm_sum(kinds[0], 2, 0))
                        if first and s == 3:
                            norm_rows(kinds[0], 2)
                        b = 4 + 2 * (s % 2)
                        dve.wait_ge(silu_done, G + q0 + s + 1)
                        if f or not first or s >= 2:
                            dve.wait_ge(hid_done, G + q0 + s - 1)
                        nc.vector.tensor_tensor(hf[:, s % 2, 0:N], sil[:, s % 2, 0:N], ps[:, b + 1, 0:N], ALU.mult).then_inc(h_done, 1)
                        if f or not first:
                            dve.wait_ge(down_done, X + Q * it - Q + KT * (n + 1))
                        dve.wait_ge(h_done, G + q0 + s + 1)
                        nc.vector.tensor_copy(h_hi[ft][:, tokens(n)], hf[:, s % 2, 0:N]).then_inc(hhi_done, 1)
                        dve.wait_ge(hhi_done, G + q0 + s + 1)
                        nc.vector.tensor_tensor(h_lo[ft][:, tokens(n)], hf[:, s % 2, 0:N], h_hi[ft][:, tokens(n)].bitcast(F32), ALU.subtract)\
                          .then_inc(hid_done, 1)
                    for n in range(3):
                        def add(m):
                            d = X + Q * it + KT * n + m
                            dve.wait_ge(down_done, d + 1)
                            if f or not first:
                                dve.wait_ge(x_added, d - Q + 1)
                            nc.vector.scalar_tensor_tensor(out=x[:, m, tokens(n)], in0=ps[:, m % 4, 0:NS[n]], scalar=0.5,
                                                           in1=x[:, m, tokens(n)], op0=ALU.mult, op1=ALU.add).then_inc(x_added, 1)

                        if last and n == 1:
                            norm_sum(kinds[1], 0, 0)
                        if last and n == 2:
                            norm_head(kinds[1], 0, (1,))
                            for m in range(4):
                                add(m)
                            norm_wait_free(kinds[1], 0)
                            norm_rows(kinds[1], 0, lambda: [add(m) for m in range(4, KT)] + ([norm_sum("fin", 1, 0), norm_sum("fin", 1, 1)] if f else []))
                        else:
                            for m in range(KT):
                                add(m)

                body(0, True)
                with dve.Fori(1, ITS - 1) as it:
                    body(it, False)
                body(ITS - 1, False, True)

            ffn(0)

            def evict(kind, n, j):
                t = FIRST[kind, n] + j
                N = NS[n]
                dve.wait_ge(tile_done, t + 1)
                src = ps[:, t % RING, 0:N]
                if kind == "rg":
                    if j < 4:
                        np_ = NPROMPT[n]
                        if n == 2:
                            nc.vector.tensor_copy(xs[:, j, :, 3:3 + TS], ps[:, t % RING, np_:N].rearrange("p (b t) -> p b t", t=TS))
                        ins = nc.vector.tensor_copy(xbuf[:, j, 3:3 + np_], ps[:, t % RING, 0:np_])
                    else:
                        ins = nc.vector.tensor_copy(ybuf[:, j - 4, 0:N], src)
                elif kind == "gla":
                    dst = qk[:, j - 4, 0:N] if j < 8 else gg[:, j - 8, 0:N]
                    ins = nc.vector.tensor_copy(dst, src)
                elif kind == "memk":
                    ins = nc.vector.tensor_copy(kmem[:, j, :], ps[:, t % RING, 0:MEM])
                elif kind == "cq":
                    ins = nc.vector.tensor_copy(qa[:, j, 0:N], src)
                else:
                    ins = nc.vector.tensor_tensor(x[:, j, tokens(n)], x[:, j, tokens(n)], src, ALU.add)
                ins.then_inc(evicted, 1)

            def evict_values(n):
                t = FIRST["gla", n]
                dve.wait_ge(tile_done, t + 4)
                for i in range(TT):
                    w = min(P, NS[n] - i * P)
                    if w < P:
                        nc.vector.memset(vt[w:P, i, :], 0.0)
                    ins = nc.vector.tensor_copy(vt[0:w, i, :], ps[0:w, i, :])
                ins.then_inc(evicted, 4)

            def rg_conv(n):
                np_, N = NPROMPT[n], NS[n]
                dve.wait_ge(evicted, FIRST["rg", n] + 4)
                if n == 2:
                    dve.wait_ge(state_in, 16 * 4)
                for tap in range(4):
                    for j in range(4):
                        w = vec[:, V_CW + 4 * tap + j:V_CW + 4 * tap + j + 1]
                        parts = [(xc[:, j, 0:np_], xbuf[:, j, tap:tap + np_])]
                        if n == 2:
                            parts.append((xc[:, j, np_:N].rearrange("p (b t) -> p b t", t=TS), xs[:, j, :, tap:tap + TS]))
                        for dst, src in parts:
                            if tap == 0:
                                ins = nc.vector.tensor_scalar(dst, src, w, vec[:, V_CB + j:V_CB + j + 1], ALU.mult, ALU.add)
                            else:
                                ins = nc.vector.scalar_tensor_tensor(out=dst, in0=src, scalar=w, in1=dst, op0=ALU.mult, op1=ALU.add)
                    if tap < 3:
                        link(ins)
                ins.then_inc(conv_done, 1)
                if n < 2:
                    dve.wait_ge(conv_done, n + 1)
                    link(nc.vector.tensor_copy(xbuf[:, :, 0:3], xbuf[:, :, np_:np_ + 3]))

            def rg_vec(n, j):
                N, np_ = NS[n], NPROMPT[n]
                if j == 7:
                    dve.wait_ge(decay_done, n + 1)
                    link(nc.vector.tensor_tensor(I[:, :, 0:N], I[:, :, 0:N], xc[:, :, 0:N], ALU.mult))
                    link(nc.vector.tensor_tensor(xc[:, :, 0:N], R[:, :, 0:N], R[:, :, 0:N], ALU.mult))
                    nc.vector.scalar_tensor_tensor(out=T_[:, :, 0:N], in0=xc[:, :, 0:N], scalar=1.0, in1=T_[:, :, 0:N],
                                                   op0=ALU.add, op1=ALU.mult).then_inc(mult_ready, 1)
                if j == 9:
                    dve.wait_ge(root_mult, n + 1)
                    link(nc.vector.tensor_tensor(I[:, :, 0:N], I[:, :, 0:N], T_[:, :, 0:N], ALU.mult))
                    if n == 2:
                        starts_a = R[:, :, np_:N].rearrange("p j (b t) -> p j b t", t=TS)[:, :, :, 0]
                        starts_u = I[:, :, np_:N].rearrange("p j (b t) -> p j b t", t=TS)[:, :, :, 0]
                        link(nc.vector.tensor_tensor(h0a[:, :, :], starts_a, h0[:, :, :], ALU.mult))
                        link(nc.vector.tensor_tensor(starts_u, starts_u, h0a[:, :, :], ALU.add))
                        link(nc.vector.memset(starts_a, 0.0))
                    for i in range(4):
                        init = 0.0 if n == 0 else hcar[:, i, :]
                        ins = nc.vector.tensor_tensor_scan(xc[:, i, 0:N], R[:, i, 0:N], I[:, i, 0:N], init, ALU.mult, ALU.add)
                    link(ins)
                    if n < 2:
                        nc.vector.tensor_copy(hcar[:, :, :], xc[:, :, N - 1:N])
                    else:
                        nc.vector.tensor_copy(hlast[:, :, 0:1], xc[:, :, np_ - 1:np_])
                        nc.vector.tensor_copy(hlast[:, :, 1:], xc[:, :, np_ + TS - 1:N:TS])
                if j == 10:
                    dve.wait_ge(y_done, n + 1)
                    nc.vector.tensor_tensor(I[:, :, 0:N], xc[:, :, 0:N], ybuf[:, :, 0:N], ALU.mult).then_inc(rg_out, 1)

            def low_rank(n):
                N = NS[n]
                full_wait(dve, "low", n)
                ins = nc.vector.tensor_copy(al[:, 0:N], bank("low", n)[0:RANK, 0:N])
                release(ins, "low", n)

            def z_vec(n):
                N = NS[n]
                for j in range(2):
                    full_wait(dve, "z", n, j)
                    ins = nc.vector.tensor_scalar(Z[:, j, 0:N], bank("z", n, j)[:, 0:N], vec[:, V_BA2 + j:V_BA2 + j + 1], None, ALU.add)
                    release(ins, "z", n, j)

            def gla_cumsum(n):
                N, np_ = NS[n], NPROMPT[n]
                dve.wait_ge(soft_done, n + 1)
                link(nc.vector.scalar_tensor_tensor(out=Z[:, :, 0:N], in0=Z[:, :, 0:N], scalar=0.0, in1=E_[:, :, 0:N],
                                                    op0=ALU.min, op1=ALU.subtract))
                mask = mixc(C_SCAN2, N) if n == 2 else mixc(C_SCAN, N)
                for j in range(2):
                    ins = nc.vector.tensor_tensor_scan(B[:, j, 0:N], mask, Z[:, j, 0:N], 0.0, ALU.mult, ALU.add)
                ins.then_inc(b_out, 1)
                dve.wait_ge(b_out, n + 1)
                for lo, hi, c in [(0, np_, CH)] + ([(np_, N, TS)] if n == 2 else []):
                    for j in range(2):
                        bb = B[:, j, lo:hi].rearrange("p (b t) -> p b t", t=c)
                        ins = nc.vector.tensor_tensor(Z[:, j, lo:hi].rearrange("p (b t) -> p b t", t=c),
                                                      bb[:, :, c - 1:c].to_broadcast([P, (hi - lo) // c, c]), bb, ALU.subtract)
                ins.then_inc(db_out, 1)

            def gla_scaled(n):
                N = NS[n]
                dve.wait_ge(edb_done, n + 1)
                dve.wait_ge(rg_out, n + 1)
                dve.wait_ge(evicted, FIRST["gla", n] + 8)
                link(nc.vector.tensor_tensor(kd[:, :, 0:N], qk[:, 2:4, 0:N], Z[:, :, 0:N], ALU.mult))
                nc.vector.tensor_tensor(qk[:, 2:4, 0:N], qk[:, 2:4, 0:N], E_[:, :, 0:N], ALU.mult)
                nc.vector.scalar_tensor_tensor(out=qk[:, 0:2, 0:N], in0=qk[:, 0:2, 0:N], scalar=0.125, in1=B[:, :, 0:N],
                                               op0=ALU.mult, op1=ALU.mult).then_inc(qk_out, 1)

            def gla_scores(n, t):
                i = TT * n + t
                prompt = NPROMPT[n] > t * P
                w = P if prompt else SAMPLE
                mask = (mixc(C_M32, P) if prompt else mixc(C_M8, SAMPLE))[0:w, :].rearrange("p (a i) -> p a i", a=1).to_broadcast([w, 2, w])
                for e in range(2):
                    full_wait(dve, "at", n, t, e)
                    if i >= 2:
                        full_wait(dve, "o", (i - 2) // TT, (i - 2) % TT, e)
                    if w < P:
                        nc.vector.memset(AT[w:P, i % 2, 2 * e:2 * e + 2, 0:w], 0.0)
                    ins = nc.vector.tensor_tensor(AT[0:w, i % 2, 2 * e:2 * e + 2, 0:w],
                                                  bank("at", n, t, e)[0:w, 0:2 * w].rearrange("p (a i) -> p a i", a=2), mask, ALU.mult)
                    release(ins, "at", n, t, e)

            def gla_states(n, t, lo=0, hi=P // CH):
                tile = TT * n + t
                for c in range(lo, hi):
                    g = 4 * tile + c
                    full_wait(dve, "kv", n, t, c)
                    if g + 1 >= 8:
                        old = (g + 1 - 8) // 4
                        full_wait(dve, "o", old // TT, old % TT, 1)
                    for p in range(2):
                        for e in range(2):
                            rows = slice(64 * e, 64 * e + 64)
                            col = t * P + (c + 1) * CH - 1
                            ins = nc.vector.scalar_tensor_tensor(
                                out=S[rows, (g + 1) % 8, p, :], in0=S[rows, g % 8, p, :], scalar=B[rows, p, col:col + 1],
                                in1=bank("kv", n, t, c)[rows, (2 * p + e) * P:(2 * p + e + 1) * P], op0=ALU.mult, op1=ALU.add)
                    release(ins, "kv", n, t, c)
                    read_wait(dve, "kv", n, t, c)

            def gla_sample_states(lo, hi):
                for b in range(lo, hi):
                    full_wait(dve, "kvs", b)
                    for p in range(2):
                        for e in range(2):
                            rows = slice(64 * e, 64 * e + 64)
                            col = NPROMPT[2] + TS * b + TS - 1
                            ins = nc.vector.scalar_tensor_tensor(
                                out=s0(b)[rows, p, :], in0=s0(b)[rows, p, :], scalar=B[rows, p, col:col + 1],
                                in1=bank("kvs", b)[rows, (2 * p + e) * P:(2 * p + e + 1) * P], op0=ALU.mult, op1=ALU.add)
                    release(ins, "kvs", b)

            def gla_tile(n, t):
                gla_scores(n, t)
                if NPROMPT[n] > t * P:
                    gla_states(n, t)

            dve.wait_ge(down_done, DOWNS)
            nc.vector.memset(S[:, 0, :, :], 0.0)
            link(nc.vector.memset(xbuf[:, :, 0:3], 0.0))
            dve.wait_ge(lam_done, 1)
            nc.vector.tensor_scalar(rgc[:, 2, :], rgc[:, 1, :], 1.0, None, ALU.add).then_inc(lam_done, 1)
            for j in range(8):
                evict("rg", 0, j)
            dve.wait_ge(wal_done, 1)
            nc.vector.tensor_tensor(w_al_lo[:, :, :], R[:, 0, 0:KT * RANK].rearrange("p (k r) -> p k r", k=KT),
                                    w_al_hi[:, :, :].bitcast(F32), ALU.subtract).then_inc(wal_done, 1)
            rg_conv(0)
            dve.wait_ge(lam_done, 3)
            link(nc.vector.tensor_scalar(rgc[:, 4, :], rgc[:, 2, :], -1.0, None, ALU.add))
            link(nc.vector.tensor_scalar(rgc[:, 5, :], rgc[:, 4, :], 0.0, None, ALU.is_equal))
            link(nc.vector.tensor_tensor(rgc[:, 4, :], rgc[:, 4, :], rgc[:, 5, :], ALU.add))
            link(nc.vector.tensor_tensor(rgc[:, 3, :], rgc[:, 3, :], rgc[:, 5, :], ALU.add))
            link(nc.vector.reciprocal(rgc[:, 6, :], rgc[:, 4, :]))
            link(nc.vector.tensor_tensor(rgc[:, 3, :], rgc[:, 3, :], rgc[:, 6, :], ALU.mult))
            link(nc.vector.tensor_tensor(rgc[:, 3, :], rgc[:, 3, :], rgc[:, 1, :], ALU.mult))
            link(nc.vector.tensor_scalar(rgc[:, 4, :], vec[:, V_LAM:V_LAM + 4], -1.0, 0.0, ALU.mult, ALU.max))
            link(nc.vector.tensor_tensor(rgc[:, 3, :], rgc[:, 3, :], rgc[:, 4, :], ALU.add))
            link(nc.vector.tensor_scalar(rgc[:, 5, :], rgc[:, 3, :], 8.0, None, ALU.mult))
            nc.vector.tensor_scalar(rgc[:, 6, :], rgc[:, 3, :], -8.0, None, ALU.mult).then_inc(lam_done, 1)
            for n in range(3):
                low_rank(n)
                evict_values(n)
                z_vec(n)
                for j in range(4, 12):
                    evict("gla", n, j)
                    if n < 2 and j in (5, 10):
                        norm_sum("mix", n + 1, j // 10)
                    if j == 6:
                        gla_cumsum(n)
                    rg_vec(n, j)
                if n < 2:
                    norm_head("mix", n + 1, ())
                gla_scaled(n)
                gla_tile(n, 0)
                if n < 2:
                    norm_wait_free("mix", n + 1)

                    def first_half_of_tile_1():
                        gla_scores(n, 1)
                        gla_states(n, 1, 0, 2)

                    norm_rows("mix", n + 1, first_half_of_tile_1)
                    gla_states(n, 1, 2)
                    evict("rg", n + 1, 0)
                    norm_sum("rgo", n, 0)
                    gla_tile(n, 2)
                    evict("rg", n + 1, 1)
                    norm_head("rgo", n, ())
                    evict("rg", n + 1, 2)
                    norm_rows("rgo", n)
                    evict("rg", n + 1, 3)
                    evict("rg", n + 1, 4)
                    norm_head("glo", n)
                    evict("rg", n + 1, 5)
                    norm_rows("glo", n)
                    evict("rg", n + 1, 6)
                    evict("rg", n + 1, 7)
                    rg_conv(n + 1)
                else:
                    norm_sum("mem", 0, 0)
                    gla_tile(n, 1)
                    norm_head("mem", 0, (1,))
                    gla_tile(n, 2)
                    norm_wait_free("mem", 0)
                    norm_rows("mem", 0)
                    dve.wait_ge(stored, 16 * 6)
                    evict("memk", 0, 0)
                    evict("memk", 0, 1)
                    gla_sample_states(0, 4)
                    evict("memk", 0, 2)
                    gla_sample_states(4, NSEQ)
                    evict("memk", 0, 3)
                    norm_sum("rgo", n, 0)
                    evict("memk", 0, 4)
                    norm_head("rgo", n, ())
                    norm_wait_free("rgo", n)
                    norm_rows("rgo", n)
                    for j in range(5, 8):
                        evict("memk", 0, j)
                    norm_head("glo", n)
                    norm_rows("glo", n)
                    for half in range(2):
                        t = FIRST["memv", 0] + 4 * half
                        dve.wait_ge(tile_done, t + 4)
                        for i in range(2):
                            ins = nc.vector.tensor_copy(vmem[:, i, 512 * half:512 * half + 512], ps[:, i, :])
                        ins.then_inc(evicted, 4)
                    norm_sum("xan", 0, 0)
                for j in range(8 if n < 2 else 4):
                    evict("out", n, j)

            def row_max(n, t):
                w = P if NPROMPT[n] > t * P else SAMPLE
                i = TT * n + t
                for q in range(2):
                    full_wait(dve, "sc", n, t, q)
                    ins = nc.vector.tensor_reduce(mx[0:w, i % 2, 0, 2 * q:2 * q + 2],
                                                  bank("sc", n, t, q)[0:w, :].rearrange("p (a m) -> p a m", a=2), AX.X, ALU.max)
                link(ins)
                nc.vector.tensor_scalar(mx[0:w, i % 2, 1, :], mx[0:w, i % 2, 0, :], -1.0 / 16, None, ALU.mult).then_inc(max_done, 1)

            def normalise(n, t):
                w = P if NPROMPT[n] > t * P else SAMPLE
                i = TT * n + t
                for q in range(2):
                    read_wait(dve, "sc", n, t, q)
                link(nc.vector.reciprocal(mx[0:w, i % 2, 3, :], mx[0:w, i % 2, 2, :]))
                for h in range(HEADS):
                    ins = nc.vector.tensor_scalar(pr[0:w, i % 2, h, :], pr[0:w, i % 2, h, :], mx[0:w, i % 2, 3, h:h + 1], None, ALU.mult)
                ins.then_inc(pr_done, 1)

            def out_lo(n, t):
                w = P if NPROMPT[n] > t * P else SAMPLE
                m = 4 if w == P else 8
                for q in range(2 if w == P else 1):
                    key = ("pv", n, t, q) if w == P else ("ot", 2)
                    dve.wait_ge(ohi_done, 2 * (TT * n + t) + q + 1)
                    ins = nc.vector.tensor_tensor(mo_lo[:, 4 * q:4 * q + m, t * P:t * P + w],
                                                  bank(*key)[:, 0:m * w].rearrange("p (a i) -> p a i", a=m),
                                                  mo_hi[:, 4 * q:4 * q + m, t * P:t * P + w].bitcast(F32), ALU.subtract)
                    release(ins, *key)

            def sample_probs():
                for q in range(2):
                    read_wait(dve, "pt", 2, 2, q)
                link(nc.vector.memset(qm[:, :, :, :], 0.0))
                for b in range(NSEQ):
                    if b >= 2:
                        dve.wait_ge(sv_done, b - 1)
                        link(nc.vector.memset(qm[:, b % 2, :, TS * (b - 2):TS * (b - 1)], 0.0))
                    c = slice(TS * b, TS * b + TS)
                    nc.vector.tensor_copy(qm[:, b % 2, :, c], pt[(3 * TT - 1) % 2][:, :, c]).then_inc(qm_done, 1)

            def sample_queries(lo, hi):
                if lo == 0:
                    dve.wait_ge(evicted, FIRST["cq", 2] + 8)
                    link(nc.vector.memset(qm[:, :, :, :], 0.0))
                for b in range(lo, hi):
                    if b >= 2:
                        dve.wait_ge(ss_done, b - 1)
                        link(nc.vector.memset(qm[:, b % 2, :, TS * (b - 2):TS * (b - 1)], 0.0))
                    c = NPROMPT[2] + TS * b
                    nc.vector.tensor_copy(qm[:, b % 2, :, TS * b:TS * b + TS], qa[:, :, c:c + TS]).then_inc(qm_done, 1)

            norm_head("xan", 0, (1,))
            norm_wait_free("xan", 0)
            norm_rows("xan", 0, lambda: evict("out", 2, 4))
            for j in range(5, 8):
                evict("out", 2, j)
            for n in range(3):
                beside = AFTER_XA[n]
                for j in range(8):
                    evict("cq", n, j)
                    if j in (2, 6):
                        norm_sum(*beside, j // 6)
                norm_head(*beside, ())
                if n == 2:
                    sample_queries(0, 2)
                for t in range(2):
                    row_max(n, t)
                    normalise(n, t)
                if n == 2:
                    sample_queries(2, NSEQ)
                row_max(n, 2)
                normalise(n, 2)
                for t in range(TT):
                    if n == 2 and t == 2:
                        sample_probs()
                    out_lo(n, t)
                norm_wait_free(*beside)
                norm_rows(*beside)
                for j in range(8):
                    evict("co", n, j)
                    if n == 2 and j == 4:
                        norm_sum("ffn2", 1, 0)

            dve.wait_ge(evicted, MIX_TILES)
            ffn(1)
            norm_head("fin", 1, ())
            norm_rows("fin", 1, lambda: [norm_sum("fin", 2, 0), norm_sum("fin", 2, 1)])
            norm_head("fin", 2, ())
            norm_rows("fin", 2)

        @block.tensor
        def _(pe):
            def split_mm(dst, w_h, w_l, x_h, x_l, start, stop):
                nc.tensor.matmul(dst, w_h, x_h, start=start, stop=False)
                nc.tensor.matmul(dst, w_h, x_l, start=False, stop=False)
                return nc.tensor.matmul(dst, w_l, x_h, start=False, stop=stop)

            def norm_stats(kind, n, quads=(0, 1)):
                p = NORMS[kind, n]
                dst = bank("st", kind, n)
                for q in quads[:p.quads]:
                    if q == 0:
                        fill_wait(pe, "st", kind, n)
                    if p.rows > 1:
                        pe.wait_ge(summed, p.sum0 + q + 1)
                    else:
                        pe.wait_ge(squared, p.sq0 + q + 1)
                    for g in range(p.groups):
                        for t in range(p.T):
                            c = min(t * P, p.N - P)
                            ins = nc.tensor.matmul(dst[:, g * p.T + t:g * p.T + t + 1], squares(kind, q)[:, g, c:c + P], ones[:, 0:1],
                                                   start=(q == 0 and g == 0 and t == 0), stop=(q == p.quads - 1), skip_group_check=True)
                    ins.then_inc(sq_used, 1)

            def norm_spread(kind, n):
                p = NORMS[kind, n]
                if kind == "mix" and n:
                    pe.wait_ge(evicted, FIRST["gla", n - 1] + 12)
                for g in range(p.groups):
                    fill_wait(pe, "rb", kind, n, g)
                    pe.wait_ge(diag_done, p.diag0 + g + 1)
                    d = diag[:, (p.diag0 + g) % 2, :, :].rearrange("p a i -> p (a i)")
                    whole = p.N // P * P
                    ins = nc.tensor.matmul(bank("rb", kind, n, g)[:, 0:whole], ones, d[:, 0:whole], start=True, stop=True)
                    if whole < p.N:
                        ins = nc.tensor.matmul(bank("rb", kind, n, g)[:, whole:p.N], ones, d[:, whole + P - (p.N - whole):whole + P], start=True, stop=True)
                    filled(ins, "rb", kind, n, g)

            def norm(kind, n):
                norm_stats(kind, n)
                norm_spread(kind, n)

            def ffn(f):
                kinds = (("ffn1", "mix"), ("ffn2", "fin"))[f]
                T0 = f * (FFN_TILES + MIX_TILES)
                G, X, Q = f * GATE_UP_STEPS, f * DOWNS, 3 * KT

                def body(it, first, last=False):
                    for s in range(6):
                        ft, n = ffn_step(first, s)
                        if first and s == 0 and f == 0:
                            norm("ffn1", 0)
                        if first and s in (0, 2):
                            norm_stats(kinds[0], n + 1, (0,))
                        if first and ft == 0:
                            pe.wait_ge(normed, NORMS[kinds[0], n].out0 + 1)
                        if n == 0:
                            pe.wait_ge(w_lo, T0 + 6 * it + 2 * ft + 2)
                        if f or not first or s >= 2:
                            pe.wait_ge(h_done, G + 6 * it + s - 1)
                        for u in range(2):
                            w = 2 * ft + u
                            for k in range(KT):
                                if first and ft == 0 and u == 0 and k == 4:
                                    pe.wait_ge(normed, NORMS[kinds[0], n].out0 + 2)
                                c = slice(k * P, k * P + P)
                                ins = split_mm(ps[:, 4 + 2 * (s % 2) + u, 0:NS[n]], w_hi_sb[:, w, c], w_lo_sb[:, w, c],
                                               a_hi[n][:, k, :], a_lo[n][:, k, :], k == 0, k == KT - 1)
                            if u:
                                ins.then_inc(gu_done, 1)
                            if first and s in (0, 2) and u == 0:
                                norm_stats(kinds[0], n + 1, (1,))
                            if first and s in (0, 2) and u:
                                norm_spread(kinds[0], n + 1)
                    pe.wait_ge(w_lo, T0 + 6 * it + 6)
                    for n in range(3):
                        pe.wait_ge(hid_done, G + 6 * it + (2 * n + 2 if first else 3 + n + 1))
                        for m in range(KT):
                            if last and n == 1 and m == 4:
                                pe.wait_ge(h_done, G + GATE_UP_STEPS)
                                norm_stats(kinds[1], 0, (0,))
                            if last and n == 2 and m == 4:
                                norm_spread(kinds[1], 0)
                            if f or not first or KT * n + m >= 4:
                                pe.wait_ge(x_added, X + Q * it + KT * n + m - 3)
                            c = slice(m * P, m * P + P)
                            for ft in range(2):
                                ins = split_mm(ps[:, m % 4, 0:NS[n]], w_hi_sb[:, 4 + ft, c], w_lo_sb[:, 4 + ft, c],
                                               h_hi[ft][:, tokens(n)], h_lo[ft][:, tokens(n)], ft == 0, ft == 1)
                            ins.then_inc(down_done, 1)
                        if last and n == 1:
                            norm_stats(kinds[1], 0, (1,))
                body(0, True)
                with pe.Fori(1, ITS - 1) as it:
                    body(it, False)
                body(ITS - 1, False, True)

            def tile(t, k4, hi, lo, N, norm_of=None):
                pe.wait_ge(w_lo, t + FFN_TILES + 1)
                if not (isinstance(t, int) and t < 4):
                    pe.wait_ge(evicted, t - 3)
                for k in range(KT):
                    if norm_of and k in (0, 4):
                        pe.wait_ge(normed, NORMS[norm_of].out0 + k // 4 + 1)
                    c = slice(k * P, k * P + P)
                    ins = split_mm(ps[:, k4, 0:N], w_hi_sb[:, k4, c], w_lo_sb[:, k4, c], hi[:, k, 0:N], lo[:, k, 0:N],
                                   k == 0, k == KT - 1)
                ins.then_inc(tile_done, 1)

            def tiles(first, groups, hi, lo, N, norm_of=None):
                if first < 4 or groups == 1:
                    for t in range(first, first + RING * groups):
                        tile(t, t % RING, hi, lo, N, norm_of if t == first else None)
                else:
                    with pe.Fori(0, groups) as g:
                        for k4 in range(RING):
                            tile(first + RING * g + k4, k4, hi, lo, N)

            def token_tiles(first, hi, lo, N):
                pe.wait_ge(evicted, first)
                for k4 in range(4):
                    pe.wait_ge(w_lo, FFN_TILES + first + k4 + 1)
                    for kk in range(2):
                        k = 2 * k4 + kk
                        c = slice(kk * 512, kk * 512 + 512)
                        for i in range((N + P - 1) // P):
                            r = slice(i * P, min(N, i * P + P))
                            w = r.stop - r.start
                            nc.tensor.matmul(ps[0:w, i, :], hi[:, k, r], w_hi_sb[:, k4, c], start=(k == 0), stop=False)
                            nc.tensor.matmul(ps[0:w, i, :], lo[:, k, r], w_hi_sb[:, k4, c], start=False, stop=False)
                            ins = nc.tensor.matmul(ps[0:w, i, :], hi[:, k, r], w_lo_sb[:, k4, c], start=False, stop=(k == KT - 1))
                    ins.then_inc(tile_done, 1)

            def gates(n):
                N = NS[n]
                pe.wait_ge(conv_done, n + 1)
                for j in range(8):
                    fill_wait(pe, "gate", n, j)
                    filled(nc.tensor.matmul(bank("gate", n, j)[:, 0:N], bd[:, j, :], xc[:, j % 4, 0:N], start=True, stop=True), "gate", n, j)

            def low_rank(n):
                N = NS[n]
                if n == 0:
                    pe.wait_ge(wal_done, 2)
                fill_wait(pe, "low", n)
                for k in range(KT):
                    ins = split_mm(bank("low", n)[0:RANK, 0:N], w_al_hi[:, k, :], w_al_lo[:, k, :], xn_hi[:, k, 0:N], xn_lo[:, k, 0:N],
                                   k == 0, k == KT - 1)
                filled(ins, "low", n)

            def decay_logits(n):
                N = NS[n]
                read_wait(pe, "low", n)
                for j in range(2):
                    fill_wait(pe, "z", n, j)
                    filled(nc.tensor.matmul(bank("z", n, j)[:, 0:N], w_a2[:, j * P:j * P + P], al[:, 0:N], start=True, stop=True), "z", n, j)

            def gla_a(n, t):
                prompt = NPROMPT[n] > t * P
                w = P if prompt else SAMPLE
                cols = slice(t * P, t * P + w)
                if t == 0:
                    pe.wait_ge(qk_out, n + 1)
                fill_wait(pe, "kdt", n, t)
                for p in range(2):
                    ins = nc.tensor.transpose(bank("kdt", n, t)[0:w, p * P:p * P + P], kd[:, p, cols], ident)
                filled(ins, "kdt", n, t)
                for e in range(2):
                    rows = slice(64 * e, 64 * e + 64)
                    fill_wait(pe, "at", n, t, e)
                    for p in range(2):
                        ins = nc.tensor.matmul(bank("at", n, t, e)[0:w, p * w:p * w + w], qk[rows, 2 + p, cols], qk[rows, p, cols],
                                               start=True, stop=True)
                    filled(ins, "at", n, t, e)
                if prompt:
                    read_wait(pe, "kdt", n, t)
                    for c in range(P // CH):
                        fill_wait(pe, "kv", n, t, c)
                        for p in range(2):
                            ins = nc.tensor.matmul(bank("kv", n, t, c)[:, 2 * p * P:2 * (p + 1) * P], kdt[:, c, p * P:p * P + P],
                                                   vt[:, t, 2 * p * P:2 * (p + 1) * P], start=True, stop=True)
                        filled(ins, "kv", n, t, c)

            def gla_b(n, t):
                prompt = NPROMPT[n] > t * P
                w = P if prompt else SAMPLE
                tile = TT * n + t
                for e in range(2):
                    rows = slice(64 * e, 64 * e + 64)
                    fill_wait(pe, "o", n, t, e)
                    read_wait(pe, "at", n, t, e)
                    if prompt:
                        read_wait(pe, "kv", n, t, 2)
                    else:
                        pe.wait_ge(s0_in, 32)
                    dst = bank("o", n, t, e)
                    for p in range(2):
                        h = 2 * p + e
                        nc.tensor.matmul(dst[:, p * P:p * P + w], vt[:, t, h * P:h * P + P], AT[:, tile % 2, 2 * e + p, 0:w],
                                         start=True, stop=False)
                        if prompt:
                            for c in range(P // CH):
                                s = slice(t * P + c * CH, t * P + (c + 1) * CH)
                                ins = nc.tensor.matmul(dst[:, p * P + c * CH:p * P + (c + 1) * CH], S[rows, (4 * tile + c) % 8, p, :],
                                                       qk[rows, p, s], start=False, stop=(c == P // CH - 1))
                        else:
                            for b in range(NSEQ):
                                s = slice(t * P + TS * b, t * P + TS * b + TS)
                                ins = nc.tensor.matmul(dst[:, p * P + TS * b:p * P + TS * b + TS], s0(b)[rows, p, :],
                                                       qk[rows, p, s], start=False, stop=(b == NSEQ - 1))
                    filled(ins, "o", n, t, e)

            def gla_sample_kv(lo, hi):
                read_wait(pe, "kdt", 2, 2)
                for b in range(lo, hi):
                    rows = slice(32 * (b // 4), 32 * (b // 4) + 32)
                    fill_wait(pe, "kvs", b)
                    for p in range(2):
                        ins = nc.tensor.matmul(bank("kvs", b)[:, 2 * p * P:2 * (p + 1) * P], kdt[rows, b % 4, p * P:p * P + P],
                                               vt[rows, 2, 2 * p * P:2 * (p + 1) * P], start=True, stop=True)
                    filled(ins, "kvs", b)

            pe.wait_ge(const_in, 32)
            ffn(0)
            pe.wait_ge(x_added, DOWNS)
            tiles(FIRST["rg", 0], 2, xn_hi, xn_lo, NS[0], ("mix", 0))
            for n in range(3):
                low_rank(n)
                token_tiles(FIRST["gla", n], xn_hi, xn_lo, NS[n])
                decay_logits(n)
                gates(n)
                tiles(FIRST["gla", n] + 4, 1, xn_hi, xn_lo, NS[n])
                if n < 2:
                    norm_stats("mix", n + 1, (0,))
                tiles(FIRST["gla", n] + 8, 1, xn_hi, xn_lo, NS[n])
                if n < 2:
                    norm_stats("mix", n + 1, (1,))
                    norm_spread("mix", n + 1)
                gla_a(n, 0)
                gla_a(n, 1)
                if n == 2:
                    pe.wait_ge(evicted, FIRST["gla", 2] + 12)
                    norm_stats("mem", 0, (0,))
                gla_b(n, 0)
                if n < 2:
                    def rg_tile(j):
                        tile(FIRST["rg", n + 1] + j, j % RING, xn_hi, xn_lo, NS[n + 1], None if j else ("mix", n + 1))

                    rg_tile(0)
                    gla_a(n, 2)
                    rg_tile(1)
                    norm_stats("rgo", n)
                    gla_b(n, 1)
                    rg_tile(2)
                    norm_spread("rgo", n)
                    gla_b(n, 2)
                    rg_tile(3)
                    rg_tile(4)
                    norm_stats("glo", n)
                    rg_tile(5)
                    norm_spread("glo", n)
                    rg_tile(6)
                    rg_tile(7)
                else:
                    norm_stats("mem", 0, (1,))
                    gla_a(n, 2)
                    norm_spread("mem", 0)
                    gla_b(n, 1)

                    def memk_tile(j):
                        tile(FIRST["memk", 0] + j, j % RING, xn_hi, xn_lo, MEM, None if j else ("mem", 0))

                    memk_tile(0)
                    gla_b(n, 2)
                    memk_tile(1)
                    gla_sample_kv(0, 4)
                    memk_tile(2)
                    gla_sample_kv(4, NSEQ)
                    memk_tile(3)
                    memk_tile(4)
                    norm_stats("rgo", n)
                    memk_tile(5)
                    norm_spread("rgo", n)
                    memk_tile(6)
                    memk_tile(7)
                    norm_stats("glo", n)
                    norm_spread("glo", n)
                    for half in range(2):
                        token_tiles(FIRST["memv", 0] + 4 * half, xn_hi, xn_lo, MEM)
                pe.wait_ge(normed, NORMS["glo", n].out0 + 1)
                if n < 2:
                    tiles(FIRST["out", n], 2, mo_hi, mo_lo, NS[n])
                else:
                    norm_stats("xan", 0, (0,))
                    tiles(FIRST["out", n], 1, mo_hi, mo_lo, NS[n])
                    norm_stats("xan", 0, (1,))
                    norm_spread("xan", 0)
                    tiles(FIRST["out", n] + 4, 1, mo_hi, mo_lo, NS[n])

            def scores(n, t):
                i = TT * n + t
                if t == 0:
                    pe.wait_ge(evicted, FIRST["cq", n] + 8)
                for q in range(2):
                    fill_wait(pe, "sc", n, t, q)
                if NPROMPT[n] > t * P:
                    for q in range(2):
                        for hh in range(2):
                            for dc in range(2):
                                f = 2 * (2 * q + hh) + dc
                                ins = nc.tensor.matmul(bank("sc", n, t, q)[:, hh * MEM:(hh + 1) * MEM], qa[:, f, t * P:t * P + P], kmem[:, f, :],
                                                       start=(dc == 0), stop=(dc == 1))
                        filled(ins, "sc", n, t, q)
                    return
                for b in range(NSEQ):
                    pe.wait_ge(qm_done, b + 1)
                    pe.wait_ge(kc_in[b % 3], 16 * (b // 3 + 1))
                    for f in range(KT):
                        q, hh, dc = f // 4, f // 2 % 2, f % 2
                        ins = nc.tensor.matmul(bank("sc", n, t, q)[0:SAMPLE, hh * MEM:(hh + 1) * MEM], qm[:, b % 2, f, :],
                                               kc[:, b % 3, f * MEM:(f + 1) * MEM], start=(b == 0 and hh == 0 and dc == 0),
                                               stop=(b == NSEQ - 1 and dc == 1), skip_group_check=True)
                        if b == NSEQ - 1 and f == 3:
                            filled(ins, "sc", n, t, 0)
                    if b < NSEQ - 1:
                        ins.then_inc(ss_done, 1)
                    else:
                        filled(ins, "sc", n, t, 1)

            def probs_transpose(n, t):
                w = P if NPROMPT[n] > t * P else SAMPLE
                i = TT * n + t
                pe.wait_ge(pr_done, i + 1)
                for q in range(2):
                    fill_wait(pe, "pt", n, t, q)
                    for r in range(4):
                        h, mc = 2 * q + r // 2, r % 2
                        ins = nc.tensor.transpose(bank("pt", n, t, q)[:, r * w:r * w + w], pr[0:w, i % 2, h, mc * P:mc * P + P], ident[0:w, 0:w])
                    filled(ins, "pt", n, t, q)

            def attend(n, t):
                prompt = NPROMPT[n] > t * P
                i = TT * n + t
                for q in range(2):
                    read_wait(pe, "pt", n, t, q)
                if prompt:
                    for q in range(2):
                        fill_wait(pe, "pv", n, t, q)
                        for r in range(4):
                            h, dc = 2 * q + r // 2, r % 2
                            for mc in range(2):
                                c = h * 2 * P + dc * P
                                ins = nc.tensor.matmul(bank("pv", n, t, q)[:, r * P:r * P + P], vmem[:, mc, c:c + P], pt[i % 2][:, 2 * h + mc, :],
                                                       start=(mc == 0), stop=(mc == 1))
                        filled(ins, "pv", n, t, q)
                    return
                for q in range(2):
                    fill_wait(pe, "pv", n, t, q)
                for b in range(NSEQ):
                    kb = NSEQ + b
                    pe.wait_ge(qm_done, kb + 1)
                    pe.wait_ge(kc_in[kb % 3], 16 * (kb // 3 + 1))
                    for h in range(HEADS):
                        for mc in range(2):
                            c = mc * D + h * MEM
                            ins = nc.tensor.matmul(bank("pv", n, t, h // 2)[0:SAMPLE, (h % 2) * MEM:(h % 2 + 1) * MEM], qm[:, b % 2, 2 * h + mc, :],
                                                   kc[:, kb % 3, c:c + MEM], start=(b == 0 and h % 2 == 0 and mc == 0),
                                                   stop=(b == NSEQ - 1 and mc == 1), skip_group_check=True)
                        if b == NSEQ - 1 and h == 1:
                            filled(ins, "pv", n, t, 0)
                    if b < NSEQ - 1:
                        ins.then_inc(sv_done, 1)
                    else:
                        filled(ins, "pv", n, t, 1)

            def sample_transpose():
                for q in range(2):
                    read_wait(pe, "pv", 2, 2, q)
                fill_wait(pe, "ot", 2)
                for f in range(KT):
                    ins = nc.tensor.transpose(bank("ot", 2)[:, f * SAMPLE:(f + 1) * SAMPLE],
                                              pr[0:SAMPLE, (3 * TT - 1) % 2, f // 2, (f % 2) * P:(f % 2 + 1) * P], ident[0:SAMPLE, 0:SAMPLE])
                filled(ins, "ot", 2)

            for n in range(3):
                beside = AFTER_XA[n]
                tiles(FIRST["cq", n], 1, xn_hi, xn_lo, NS[n], ("xan", n))
                norm_stats(*beside, (0,))
                tiles(FIRST["cq", n] + 4, 1, xn_hi, xn_lo, NS[n])
                norm_stats(*beside, (1,))
                scores(n, 0)
                scores(n, 1)
                probs_transpose(n, 0)
                scores(n, 2)
                probs_transpose(n, 1)
                attend(n, 0)
                probs_transpose(n, 2)
                attend(n, 1)
                attend(n, 2)
                norm_spread(*beside)
                if n == 2:
                    sample_transpose()
                for t in range(TT):
                    for q in range(2):
                        if t:
                            read_wait(pe, "sc", n, t, q)
                        if NPROMPT[n] > t * P:
                            read_wait(pe, "pv", n, t, q)
                        elif q == 0:
                            read_wait(pe, "ot", 2)
                if n < 2:
                    tiles(FIRST["co", n], 2, mo_hi, mo_lo, NS[n])
                else:
                    tiles(FIRST["co", n], 2, mo_hi, mo_lo, NS[n])

            pe.wait_ge(evicted, MIX_TILES)
            ffn(1)
            norm("fin", 1)
            norm("fin", 2)


_OUTS = {"y": (D, TOK), "mem_k": (P, KT, MEM), "mem_v": (P, 2, D), "conv_p": (P, 4, 3), "h": (P, 4, 1 + NSEQ), "s_p": (P, 2, P),
         "conv_s": (P, 4, NSEQ, 3), "s_s": (P, NSEQ, 2, P)}


def kernel(**inputs):
    import numpy as np
    import concourse.bacc as bacc
    from concourse.bass_utils import run_bass_kernel_spmd

    i = {k: np.asarray(v) for k, v in inputs.items()}
    f32 = np.float32

    def tiles(w):
        return w.reshape(KT, P, -1, P).transpose(2, 1, 0, 3).reshape(-1, P, D)

    def wide(w):
        h = w.shape[1] // 512
        return w.reshape(4, 2, P, h, 512).transpose(3, 0, 2, 1, 4).reshape(4 * h, P, D)

    def cols(v):
        return v.reshape(-1, P).T

    w_in = i["w_in"]
    rg, q, k, v, g, low = np.split(w_in, [1024, 1280, 1536, 2048, 2560], axis=1)
    mix_tiles = np.concatenate([tiles(rg), wide(v), tiles(q), tiles(k), tiles(g), tiles(i["w_out"]), tiles(i["w_ck"]), wide(i["w_cv"]),
                                tiles(i["w_cq"]), tiles(i["w_co"])])
    vectors = np.concatenate([cols(i["ffn1_norm"]), cols(i["mix_norm"]), cols(i["mem_norm"]), cols(i["xattn_norm"]), cols(i["ffn2_norm"]),
                              cols(i["final_norm"]), cols(i["rg_out_norm"]), cols(i["gla_out_norm"]),
                              i["conv_w"].reshape(4, 4, P).transpose(2, 0, 1).reshape(P, 16), cols(i["conv_b"]),
                              cols(i["rg_b_a"].reshape(-1)), cols(i["rg_b_x"].reshape(-1)), cols(i["rg_lambda"]), cols(i["gla_b_a2"]),
                              np.full((P, 1), EPS, f32)], axis=1)

    gates = np.zeros((P, 8, P), f32)
    for j in range(4):
        for h in range(2):
            s = slice(64 * h, 64 * h + 64)
            gates[s, j, s] = i["rg_w_a"][2 * j + h]
            gates[s, 4 + j, s] = i["rg_w_x"][2 * j + h]

    consts = np.zeros((P, NCONST), f32)
    r, c = np.arange(P)[:, None], np.arange(P)[None, :]
    consts[:, C_ONES:C_ONES + P] = 1
    consts[:, C_ID:C_ID + P] = r == c
    consts[:, C_ROW:C_ROW + 4] = r // CH == np.arange(4)
    consts[:, C_ROW + 4:C_ROW + 8] = r // TS % 4 == np.arange(4)
    consts[:, C_M32:C_M32 + P] = (r // CH == c // CH) & (r <= c)
    consts[:, C_M8:C_M8 + SAMPLE] = ((r // TS == c // TS) & (r <= c))[:, 0:SAMPLE]
    consts[:, C_SCAN:C_SCAN + NMAX] = np.arange(NMAX) % CH != 0
    t = np.arange(NS[2])
    consts[:, C_SCAN2:C_SCAN2 + NS[2]] = np.where(t < NPROMPT[2], t % CH != 0, t % TS != 0)

    def heads(s):
        return s.reshape(-1, 2, 2, 64, P).transpose(2, 3, 0, 1, 4).reshape(P, -1, 2, P)

    given = {
        "x": np.concatenate([i["x_prompt"].reshape(SEQ, D), i["x_sample"].reshape(SAMPLE, D)]).T,
        "consts": consts, "vectors": vectors, "gates": gates, "mix_tiles": mix_tiles,
        "w_alow": low.reshape(KT, P, RANK).transpose(1, 0, 2).reshape(P, KT * RANK), "w_a2": i["gla_w_a2"],
        "mem": i["mem_prompt"].reshape(MEM, D).T,
        "conv0": i["state_conv"].reshape(NSEQ, 3, 4, P).transpose(3, 2, 0, 1),
        "h0": i["state_rglru"].reshape(NSEQ, 4, P).transpose(2, 1, 0),
        "s0": heads(i["state_gla"]),
        "cache_k": i["cache_mem_k"].reshape(NSEQ, MEM, KT, P).transpose(0, 3, 2, 1).reshape(NSEQ, P, 2 * D),
        "cache_v": i["cache_mem_v"].reshape(NSEQ, 2, P, D).transpose(0, 2, 1, 3).reshape(NSEQ, P, 2 * D),
    }
    for f in (1, 2):
        given[f"ffn{f}_gate"] = tiles(i[f"ffn{f}_w_gate"])
        given[f"ffn{f}_up"] = tiles(i[f"ffn{f}_w_up"])
        given[f"ffn{f}_down"] = i[f"ffn{f}_w_down"].reshape(FT, P, D)

    nc = bacc.Bacc("TRN2", target_bir_lowering=False, num_devices=1)
    arrays, a, out = {}, {}, {}
    for name, v in given.items():
        arrays[f"in_{name}"] = np.ascontiguousarray(v)
        a[name] = nc.dram_tensor(f"in_{name}", v.shape, mybir.dt.from_np(v.dtype), kind="ExternalInput").ap()
    for name, shape in _OUTS.items():
        out[name] = nc.dram_tensor(f"out_{name}", shape, F32, kind="ExternalOutput").ap()
    program(nc, a, out)
    r = run_bass_kernel_spmd(nc, [arrays], core_ids=[0])
    o = {name: r.results[0][f"out_{name}"] for name in _OUTS}

    y = o["y"].T
    s_p, s_s = o["s_p"].reshape(P, 1, 2, P), o["s_s"]

    def unheads(s):
        return s.reshape(2, 64, -1, 2, P).transpose(2, 3, 0, 1, 4).reshape(-1, HEADS, 64, P)

    return (y[:SEQ].reshape(1, SEQ, D), y[SEQ:].reshape(NSEQ, TS, D),
            o["mem_k"].transpose(2, 1, 0).reshape(1, MEM, HEADS, MEM), o["mem_v"].transpose(1, 0, 2).reshape(1, MEM, HEADS, MEM),
            o["conv_p"].transpose(2, 1, 0).reshape(1, 3, 512), o["h"][:, :, 0].T.reshape(1, 512), unheads(s_p),
            o["conv_s"].transpose(2, 3, 1, 0).reshape(NSEQ, 3, 512), o["h"][:, :, 1:].transpose(2, 1, 0).reshape(NSEQ, 512), unheads(s_s))
```
